# Optimizing a Trainium2 kernel written in Bass

```python
import jax
import jax.numpy as jnp
from jax import lax
import numpy as np
import jax, jax.numpy as jnp

D_MODEL = 1024
BATCH = 1
SEQ = 256
DEPTH = 2

CHUNK = 64
EPS = 1e-6
CONV_CH = D_MODEL // 2
CONV_WIDTH = 31
GLA_HEADS = 4
GLA_DK = D_MODEL // 16
GLA_DV = D_MODEL // 8
GLA_GATE_RANK = 16
GLA_GATE_TAU = 16.0
FOX_HEADS = 16
FOX_HD = D_MODEL // FOX_HEADS
Q_BLOCK = 128
PEER_HEADS = 8
PEER_NKEYS = 128
PEER_N = PEER_NKEYS * PEER_NKEYS
PEER_QDIM = 256
PEER_TOPK = 16
PEER_TOKEN_BLOCK = 128

EVEN_IN = 2 * CONV_CH + 2 * GLA_HEADS * GLA_DK + 2 * GLA_HEADS * GLA_DV + GLA_GATE_RANK
ODD_IN = 3 * FOX_HEADS * FOX_HD + FOX_HEADS


def rms_norm(x, g):
    xf = x.astype(jnp.float32)
    y = xf * lax.rsqrt(jnp.mean(xf * xf, axis=-1, keepdims=True) + EPS)
    return (y * g.astype(jnp.float32)).astype(x.dtype)

def layer_norm(x, g, b):
    xf = x.astype(jnp.float32)
    mu = jnp.mean(xf, axis=-1, keepdims=True)
    xc = xf - mu
    y = xc * lax.rsqrt(jnp.mean(xc * xc, axis=-1, keepdims=True) + EPS)
    return (y * g.astype(jnp.float32) + b.astype(jnp.float32)).astype(x.dtype)

def conformer_conv(val, gate, conv_w, conv_b, ln_g, ln_b):
    u = val * jax.nn.sigmoid(gate)
    w = conv_w.astype(u.dtype)[:, None, :]
    y = lax.conv_general_dilated(u, w, window_strides=(1,), padding=[(CONV_WIDTH - 1, 0)],
                                 dimension_numbers=('NWC', 'WIO', 'NWC'),
                                 feature_group_count=u.shape[-1])
    y = y + conv_b.astype(y.dtype)
    return jax.nn.silu(layer_norm(y, ln_g, ln_b))

def gla_chunked(q, k, v, log_a):
    B, S, H, dk = q.shape
    dv = v.shape[-1]
    n = S // CHUNK

    def to_chunks(t):
        return t.reshape(B, n, CHUNK, H, t.shape[-1]).transpose(1, 0, 3, 2, 4)

    qc, kc, vc, gc = to_chunks(q * (dk ** -0.5)), to_chunks(k), to_chunks(v), to_chunks(log_a)
    causal = jnp.tril(jnp.ones((CHUNK, CHUNK), dtype=bool))

    def step(state, inp):
        qi, ki, vi, gi = inp
        b = jnp.cumsum(gi, axis=2)
        b_last = b[:, :, -1:, :]
        o_inter = jnp.einsum('bhtk,bhkv->bhtv', qi * jnp.exp(b), state)
        diff = b[:, :, :, None, :] - b[:, :, None, :, :]
        decay = jnp.exp(jnp.where(causal[:, :, None], diff, -jnp.inf))
        attn = jnp.einsum('bhtk,bhsk,bhtsk->bhts', qi, ki, decay)
        o = o_inter + jnp.einsum('bhts,bhsv->bhtv', attn, vi)
        k_dec = ki * jnp.exp(b_last - b)
        new_state = state * jnp.exp(b_last[:, :, 0, :, None]) + jnp.einsum('bhsk,bhsv->bhkv', k_dec, vi)
        return new_state, o

    s0 = jnp.zeros((B, H, dk, dv), jnp.float32)
    _, o = lax.scan(step, s0, (qc, kc, vc, gc))
    return o.transpose(1, 0, 3, 2, 4).reshape(B, S, H, dv)

def even_mix(h, w_in, conv_w, conv_b, ln_g, ln_b, gate_w2, gate_b, gla_norm_g, w_out):
    B, S, _ = h.shape
    hk = GLA_HEADS * GLA_DK
    hv = GLA_HEADS * GLA_DV
    p = h @ w_in
    cuts = [int(c) for c in np.cumsum([CONV_CH, CONV_CH, hk, hk, hv, hv])]
    a_val, a_gate, q, k, v, r, glr = jnp.split(p, cuts, axis=-1)
    y_a = conformer_conv(a_val, a_gate, conv_w, conv_b, ln_g, ln_b)
    f32 = jnp.float32
    log_a = jax.nn.log_sigmoid((glr @ gate_w2 + gate_b).astype(f32)) / GLA_GATE_TAU
    o = gla_chunked(q.reshape(B, S, GLA_HEADS, GLA_DK).astype(f32),
                    k.reshape(B, S, GLA_HEADS, GLA_DK).astype(f32),
                    v.reshape(B, S, GLA_HEADS, GLA_DV).astype(f32),
                    log_a.reshape(B, S, GLA_HEADS, GLA_DK))
    o = rms_norm(o, gla_norm_g).reshape(B, S, hv).astype(h.dtype)
    y_b = o * jax.nn.silu(r)
    return jnp.concatenate([y_a, y_b], axis=-1) @ w_out

def fox_mix(h, w_in, fgate_b, q_g, k_g, w_out):
    B, S, _ = h.shape
    hd = FOX_HEADS * FOX_HD
    p = h @ w_in
    q, k, v, fz = jnp.split(p, [hd, 2 * hd, 3 * hd], axis=-1)
    q = rms_norm(q.reshape(B, S, FOX_HEADS, FOX_HD), q_g).transpose(0, 2, 1, 3)
    k = rms_norm(k.reshape(B, S, FOX_HEADS, FOX_HD), k_g).transpose(0, 2, 1, 3)
    v = v.reshape(B, S, FOX_HEADS, FOX_HD).transpose(0, 2, 1, 3)
    f32 = jnp.float32
    log_f = jax.nn.log_sigmoid(fz.astype(f32) + fgate_b.astype(f32))
    c = jnp.cumsum(log_f, axis=1).transpose(0, 2, 1)
    scale = FOX_HD ** -0.5
    pos = jnp.arange(S)
    outs = []
    for i in range(S // Q_BLOCK):
        lo, hi = i * Q_BLOCK, (i + 1) * Q_BLOCK
        logits = jnp.einsum('bhqd,bhkd->bhqk', q[:, :, lo:hi], k[:, :, :hi]).astype(f32) * scale
        logits = logits + c[:, :, lo:hi, None] - c[:, :, None, :hi]
        mask = pos[lo:hi, None] >= pos[None, :hi]
        probs = jax.nn.softmax(jnp.where(mask, logits, -jnp.inf), axis=-1)
        outs.append(jnp.einsum('bhqk,bhkd->bhqd', probs.astype(v.dtype), v[:, :, :hi]))
    o = jnp.concatenate(outs, axis=2).transpose(0, 2, 1, 3).reshape(B, S, hd)
    return o @ w_out

def peer_ffn(h, wq, keys, u, v):
    B, S, D = h.shape
    f32 = jnp.float32
    half = PEER_QDIM // 2
    q = (h @ wq).reshape(B, S, PEER_HEADS, 2, half).astype(f32)
    s1 = jnp.einsum('bshd,hnd->bshn', q[..., 0, :], keys[:, 0].astype(f32))
    s2 = jnp.einsum('bshd,hnd->bshn', q[..., 1, :], keys[:, 1].astype(f32))
    v1, i1 = lax.top_k(s1, PEER_TOPK)
    v2, i2 = lax.top_k(s2, PEER_TOPK)
    cand = (v1[..., :, None] + v2[..., None, :]).reshape(B, S, PEER_HEADS, PEER_TOPK * PEER_TOPK)
    sc, j = lax.top_k(cand, PEER_TOPK)
    e1 = jnp.take_along_axis(i1, j // PEER_TOPK, axis=-1)
    e2 = jnp.take_along_axis(i2, j % PEER_TOPK, axis=-1)
    experts = e1 * PEER_NKEYS + e2
    gates = jax.nn.softmax(sc, axis=-1)
    nb = (B * S) // PEER_TOKEN_BLOCK
    ne = PEER_HEADS * PEER_TOPK
    hb = h.reshape(nb, PEER_TOKEN_BLOCK, D)
    eb = experts.reshape(nb, PEER_TOKEN_BLOCK, ne)
    gb = gates.reshape(nb, PEER_TOKEN_BLOCK, ne).astype(h.dtype)

    def block(args):
        ht, et, gt = args
        act = jax.nn.gelu(jnp.einsum('td,ted->te', ht, u[et]), approximate=False)
        return jnp.einsum('te,ted->td', gt * act, v[et])

    out = lax.map(block, (hb, eb, gb))
    return out.reshape(B, S, D)

def first_inputs(seed: int = 0) -> dict:
    key = jax.random.key(seed)
    ks = iter(jax.random.split(key, 32))
    n_even = (DEPTH + 1) // 2
    n_odd = DEPTH // 2
    f32 = jnp.float32
    D = D_MODEL

    def nrm(shape, scale):
        return jax.random.normal(next(ks), shape, f32) * scale

    def gain(shape):
        return 1.0 + 0.05 * jax.random.normal(next(ks), shape, f32)

    return {
        'x': nrm((BATCH, SEQ, D), 1.0),
        'ev_norm_mix': gain((n_even, D)),
        'ev_w_in': nrm((n_even, D, EVEN_IN), D ** -0.5),
        'ev_conv_w': nrm((n_even, CONV_WIDTH, CONV_CH), CONV_WIDTH ** -0.5),
        'ev_conv_b': nrm((n_even, CONV_CH), 0.02),
        'ev_conv_ln_g': gain((n_even, CONV_CH)),
        'ev_conv_ln_b': nrm((n_even, CONV_CH), 0.02),
        'ev_gate_w2': nrm((n_even, GLA_GATE_RANK, GLA_HEADS * GLA_DK), GLA_GATE_RANK ** -0.5),
        'ev_gate_b': nrm((n_even, GLA_HEADS * GLA_DK), 0.1),
        'ev_gla_norm_g': gain((n_even, GLA_DV)),
        'ev_w_out': nrm((n_even, CONV_CH + GLA_HEADS * GLA_DV, D), (CONV_CH + GLA_HEADS * GLA_DV) ** -0.5),
        'od_norm_mix': gain((n_odd, D)),
        'od_w_in': nrm((n_odd, D, ODD_IN), D ** -0.5),
        'od_fgate_b': jax.random.uniform(next(ks), (n_odd, FOX_HEADS), f32, minval=1.0, maxval=4.0),
        'od_q_norm_g': gain((n_odd, FOX_HD)),
        'od_k_norm_g': gain((n_odd, FOX_HD)),
        'od_w_out': nrm((n_odd, FOX_HEADS * FOX_HD, D), (FOX_HEADS * FOX_HD) ** -0.5),
        'ffn_norm': gain((DEPTH, D)),
        'peer_wq': nrm((DEPTH, D, PEER_HEADS * PEER_QDIM), D ** -0.5),
        'peer_keys': nrm((DEPTH, PEER_HEADS, 2, PEER_NKEYS, PEER_QDIM // 2), (PEER_QDIM // 2) ** -0.5),
        'peer_u': nrm((DEPTH, PEER_N, D), D ** -0.5),
        'peer_v': nrm((DEPTH, PEER_N, D), (PEER_HEADS * PEER_TOPK) ** -0.5),
    }

def first_block(x, ev_norm_mix, ev_w_in, ev_conv_w, ev_conv_b, ev_conv_ln_g, ev_conv_ln_b,
              ev_gate_w2, ev_gate_b, ev_gla_norm_g, ev_w_out,
              od_norm_mix, od_w_in, od_fgate_b, od_q_norm_g, od_k_norm_g, od_w_out,
              ffn_norm, peer_wq, peer_keys, peer_u, peer_v):
    for layer in range(DEPTH):
        j = layer // 2
        if layer % 2 == 0:
            h = rms_norm(x, ev_norm_mix[j])
            x = x + even_mix(h, ev_w_in[j], ev_conv_w[j], ev_conv_b[j], ev_conv_ln_g[j], ev_conv_ln_b[j],
                             ev_gate_w2[j], ev_gate_b[j], ev_gla_norm_g[j], ev_w_out[j])
        else:
            h = rms_norm(x, od_norm_mix[j])
            x = x + fox_mix(h, od_w_in[j], od_fgate_b[j], od_q_norm_g[j], od_k_norm_g[j], od_w_out[j])
        h = rms_norm(x, ffn_norm[layer])
        x = x + peer_ffn(h, peer_wq[layer], peer_keys[layer], peer_u[layer], peer_v[layer])
    return x


DEPTH_2 = 1

N_Q_HEADS = 8
N_KV_HEADS = 2
HEAD_DIM = 64
Q_GROUP = N_Q_HEADS // N_KV_HEADS
ATT_WIDTH = N_Q_HEADS * HEAD_DIM
KV_WIDTH = N_KV_HEADS * HEAD_DIM
WINDOW = 128
ATT_BLOCK = 128
SGU_WIDTH = D_MODEL // 2
SGU_GROUPS = 8
SGU_GROUP_DIM = SGU_WIDTH // SGU_GROUPS
SGU_CHUNK = 128
N_BRANCHES = 2
IN_WIDTH = ATT_WIDTH + 2 * KV_WIDTH + 2 * SGU_WIDTH + N_BRANCHES * D_MODEL
D_FF = 256 * ((8 * D_MODEL // 3 + 255) // 256)
CONV_WIDTH_2 = 3
NORM_EPS = 1e-6
NEG_INF = -1e30


def rmsnorm(x, gain):
    xf = x.astype(jnp.float32)
    y = xf * lax.rsqrt(jnp.mean(xf * xf, axis=-1, keepdims=True) + NORM_EPS)
    return (y * gain.astype(jnp.float32)).astype(x.dtype)

def alibi_slopes():
    return jnp.exp2(-8.0 * (jnp.arange(N_Q_HEADS, dtype=jnp.float32) + 1.0) / N_Q_HEADS)

def sliding_window_attention(q, k, v, q_gain, k_gain, sinks):
    B, S, _ = q.shape
    nb = S // ATT_BLOCK
    q = rmsnorm(q.reshape(B, S, N_Q_HEADS, HEAD_DIM), q_gain)
    k = rmsnorm(k.reshape(B, S, N_KV_HEADS, HEAD_DIM), k_gain)
    v = v.reshape(B, S, N_KV_HEADS, HEAD_DIM)
    qb = q.reshape(B, nb, ATT_BLOCK, N_KV_HEADS, Q_GROUP, HEAD_DIM)

    def band(t):
        tp = jnp.pad(t, ((0, 0), (ATT_BLOCK, 0), (0, 0), (0, 0)))
        tp = tp.reshape(B, nb + 1, ATT_BLOCK, N_KV_HEADS, HEAD_DIM)
        return jnp.concatenate([tp[:, :-1], tp[:, 1:]], axis=2)

    kb, vb = band(k), band(v)
    scores = jnp.einsum('bnqhgd,bnkhd->bnhgqk', qb, kb,
                        preferred_element_type=jnp.float32) * (HEAD_DIM ** -0.5)
    qi = jnp.arange(ATT_BLOCK)[:, None]
    kj = jnp.arange(2 * ATT_BLOCK)[None, :]
    dist = qi + ATT_BLOCK - kj
    key_pos = jnp.arange(nb)[:, None] * ATT_BLOCK - ATT_BLOCK + kj
    valid = ((dist >= 0) & (dist < WINDOW))[None] & (key_pos >= 0)[:, None, :]
    slopes = alibi_slopes().reshape(N_KV_HEADS, Q_GROUP)
    alibi = -slopes[:, :, None, None] * dist.astype(jnp.float32)[None, None]
    scores = jnp.where(valid[None, :, None, None], scores + alibi[None, None], NEG_INF)
    sink = jnp.broadcast_to(
        sinks.astype(jnp.float32).reshape(1, 1, N_KV_HEADS, Q_GROUP, 1, 1),
        scores.shape[:-1] + (1,))
    probs = jax.nn.softmax(jnp.concatenate([scores, sink], axis=-1), axis=-1)[..., :-1]
    out = jnp.einsum('bnhgqk,bnkhd->bnqhgd', probs.astype(v.dtype), vb)
    return out.reshape(B, S, ATT_WIDTH)

def chunked_spatial_gating(u, v, sgu_gain, w_s, b_s):
    B, S, _ = u.shape
    nc = S // SGU_CHUNK
    u = jax.nn.gelu(u)
    v = rmsnorm(jax.nn.gelu(v), sgu_gain)
    vc = v.reshape(B, nc, SGU_CHUNK, SGU_GROUPS, SGU_GROUP_DIM)
    causal = jnp.tril(jnp.ones((SGU_CHUNK, SGU_CHUNK), dtype=bool))
    w = jnp.where(causal[None], w_s, 0)
    mixed = jnp.einsum('gij,bcjgd->bcigd', w, vc) + b_s.T[:, :, None]
    return u * mixed.reshape(B, S, SGU_WIDTH)

def conv_gated_mlp(h, w_up, conv_w, conv_b, w_down):
    S = h.shape[1]
    z = h @ w_up
    zp = jnp.pad(z, ((0, 0), (CONV_WIDTH_2 - 1, 0), (0, 0)))
    zc = conv_b
    for tap in range(CONV_WIDTH_2):
        zc = zc + conv_w[tap] * zp[:, tap:tap + S]
    gate, val = jnp.split(zc, 2, axis=-1)
    return (jax.nn.silu(gate) * val) @ w_down

def second_inputs(seed: int = 0) -> dict:
    key = jax.random.key(seed)
    ks = jax.random.split(key, 20)
    f32 = jnp.float32

    def nrm(k, shape, scale):
        return jax.random.normal(k, shape, f32) * scale

    return {
        "x": nrm(ks[0], (BATCH, SEQ, D_MODEL), 1.0),
        "mix_norm": 1.0 + nrm(ks[1], (DEPTH_2, D_MODEL), 0.05),
        "w_in": nrm(ks[2], (DEPTH_2, D_MODEL, IN_WIDTH), D_MODEL ** -0.5),
        "q_norm": 1.0 + nrm(ks[3], (DEPTH_2, HEAD_DIM), 0.05),
        "k_norm": 1.0 + nrm(ks[4], (DEPTH_2, HEAD_DIM), 0.05),
        "sinks": nrm(ks[5], (DEPTH_2, N_Q_HEADS), 0.5),
        "sgu_norm": 1.0 + nrm(ks[6], (DEPTH_2, SGU_WIDTH), 0.05),
        "w_s": nrm(ks[7], (DEPTH_2, SGU_GROUPS, SGU_CHUNK, SGU_CHUNK), SGU_CHUNK ** -0.5),
        "b_s": 1.0 + nrm(ks[8], (DEPTH_2, SGU_GROUPS, SGU_CHUNK), 0.1),
        "w_oa": nrm(ks[9], (DEPTH_2, ATT_WIDTH, D_MODEL), ATT_WIDTH ** -0.5),
        "w_ob": nrm(ks[10], (DEPTH_2, SGU_WIDTH, D_MODEL), SGU_WIDTH ** -0.5),
        "w_out": nrm(ks[11], (DEPTH_2, D_MODEL, D_MODEL), D_MODEL ** -0.5),
        "ffn_norm": 1.0 + nrm(ks[12], (DEPTH_2, D_MODEL), 0.05),
        "w_up": nrm(ks[13], (DEPTH_2, D_MODEL, 2 * D_FF), D_MODEL ** -0.5),
        "conv_w": nrm(ks[14], (DEPTH_2, CONV_WIDTH_2, 2 * D_FF), CONV_WIDTH_2 ** -0.5),
        "conv_b": nrm(ks[15], (DEPTH_2, 2 * D_FF), 0.02),
        "w_down": nrm(ks[16], (DEPTH_2, D_FF, D_MODEL), D_FF ** -0.5),
    }

def second_block(x, mix_norm, w_in, q_norm, k_norm, sinks, sgu_norm, w_s, b_s,
              w_oa, w_ob, w_out, ffn_norm, w_up, conv_w, conv_b, w_down):
    splits = (ATT_WIDTH,
              ATT_WIDTH + KV_WIDTH,
              ATT_WIDTH + 2 * KV_WIDTH,
              ATT_WIDTH + 2 * KV_WIDTH + SGU_WIDTH,
              ATT_WIDTH + 2 * KV_WIDTH + 2 * SGU_WIDTH,
              ATT_WIDTH + 2 * KV_WIDTH + 2 * SGU_WIDTH + D_MODEL)
    for l in range(DEPTH_2):
        h = rmsnorm(x, mix_norm[l])
        proj = h @ w_in[l]
        q, k, v, su, sv, g_a, g_b = jnp.split(proj, splits, axis=-1)
        y_att = sliding_window_attention(q, k, v, q_norm[l], k_norm[l], sinks[l])
        y_sgu = chunked_spatial_gating(su, sv, sgu_norm[l], w_s[l], b_s[l])
        merged = (jax.nn.sigmoid(g_a) * (y_att @ w_oa[l])
                  + jax.nn.sigmoid(g_b) * (y_sgu @ w_ob[l]))
        x = x + merged @ w_out[l]
        x = x + conv_gated_mlp(rmsnorm(x, ffn_norm[l]), w_up[l], conv_w[l], conv_b[l], w_down[l])
    return x


def setup_inputs(seed=0):
    out = dict(first_inputs(seed))
    for name, value in second_inputs(seed + 1).items():
        if name != "x":
            out[name + "_2"] = value
    return out


def reference(
    x, ev_norm_mix, ev_w_in, ev_conv_w, ev_conv_b, ev_conv_ln_g, ev_conv_ln_b, ev_gate_w2,
    ev_gate_b, ev_gla_norm_g, ev_w_out, od_norm_mix, od_w_in, od_fgate_b, od_q_norm_g,
    od_k_norm_g, od_w_out, ffn_norm, peer_wq, peer_keys, peer_u, peer_v, mix_norm_2, w_in_2,
    q_norm_2, k_norm_2, sinks_2, sgu_norm_2, w_s_2, b_s_2, w_oa_2, w_ob_2, w_out_2, ffn_norm_2,
    w_up_2, conv_w_2, conv_b_2, w_down_2,
):
    x = first_block(
        x, ev_norm_mix, ev_w_in, ev_conv_w, ev_conv_b, ev_conv_ln_g, ev_conv_ln_b, ev_gate_w2,
        ev_gate_b, ev_gla_norm_g, ev_w_out, od_norm_mix, od_w_in, od_fgate_b, od_q_norm_g,
        od_k_norm_g, od_w_out, ffn_norm, peer_wq, peer_keys, peer_u, peer_v,
    )
    return second_block(
        x, mix_norm_2, w_in_2, q_norm_2, k_norm_2, sinks_2, sgu_norm_2, w_s_2, b_s_2, w_oa_2,
        w_ob_2, w_out_2, ffn_norm_2, w_up_2, conv_w_2, conv_b_2, w_down_2,
    )


_drawn_inputs = setup_inputs


def setup_inputs(seed=0):
    import zlib

    import numpy as np

    out = dict(_drawn_inputs(seed))
    spreads = {}
    factors = {'ev_conv_ln_b': 4.533,
     'ev_gate_b': 2.918,
     'od_q_norm_g': 4.445,
     'od_k_norm_g': 4.658,
     'ffn_norm': 3.79,
     'q_norm_2': 8.0,
     'k_norm_2': 8.0,
     'sinks_2': 115.264,
     'sgu_norm_2': 5.371,
     'conv_b_2': 4.786,
     'b_s_2': 3.157,
     'ffn_norm_2': 2.836}
    for name, (base, spread) in spreads.items():
        noise = np.random.default_rng([zlib.crc32(name.encode()), seed]).standard_normal(out[name].shape)
        drawn = base * np.exp(spread * noise) if base else spread * noise
        out[name] = jnp.asarray(drawn.astype(out[name].dtype))
    for name, factor in factors.items():
        out[name] = (out[name] * factor).astype(out[name].dtype)
    return out
```

```python
from contextlib import ExitStack

import numpy as np

import concourse.bass as bass
from concourse import mybir

F32 = mybir.dt.float32
BF16 = mybir.dt.bfloat16
I32 = mybir.dt.int32
U16 = mybir.dt.uint16
U32 = mybir.dt.uint32
ALU = mybir.AluOpType
ACT = mybir.ActivationFunctionType
AX = mybir.AxisListType

P = 128
T = 256
TB = T // P
D = 1024
KC = D // P
EPS = 1e-6
RING = 8
PIECE = 1024

CONV_CH, CONV_W = 512, 31
CC = CONV_CH // P
GH, DK, DV, CHUNK, RANK, TAU = 4, 64, 128, 64, 16, 16.0
NCH = T // CHUNK
LEVELS = [32, 16, 8, 4, 2, 1]

FH, HD = 16, 64

PH, NK, TOPK = 8, 128, 16
NEG_BIG = -3.0e38

QH, KVH, GROUP = 8, 2, 4
SG, SGD = 8, 64
D_FF = 2816
FC = D_FF // P
FAR = 1e33

G_EV, G_PEER0, G_OD, G_PEER1, G_MIX2, G_FFN2 = range(6)
NORMS = 6


def build(nc, a, out):
    ctx = ExitStack()
    with ctx:
        def sb(name, shape, dt=F32):
            return ctx.enter_context(nc.sbuf_tensor(name, shape, dt))

        def sem(name):
            return ctx.enter_context(nc.semaphore(name))

        bank = [ctx.enter_context(nc.psum_tensor(f"bank{i}", [P, 512], F32)) for i in range(8)]

        big = sb("big", [P, 128 * T])
        ring = sb("ring", [P, RING, PIECE])
        xT = sb("xT", [P, KC * T])
        hT = sb("hT", [P, KC * T])
        sco = sb("sco", [P, TB * 16 * NK])
        ones = sb("ones", [P, P])
        ident = sb("ident", [P, P])
        halves = sb("halves", [P, P])
        iota = sb("iota", [P, P])
        zeros = sb("zeros", [P, 512], BF16)
        gains = sb("gains", [P, NORMS * KC])
        qk_gain = sb("qk_gain", [P, 4])
        sinks = sb("sinks", [P, QH])
        neg_row = sb("neg_row", [P, 2])
        top_v = sb("top_v", [P, TB * 16 * 16])
        top_i = sb("top_i", [P, TB * 16 * 16], U16)
        top_if = sb("top_if", [P, TB * 16 * 16])
        cand_v = sb("cand_v", [P, P])
        cand_i = sb("cand_i", [P, P], U32)
        rank_u = sb("rank_u", [P, 2 * P], U32)
        rank_f = sb("rank_f", [P, 2 * P])
        gate_s = sb("gate_s", [P, 2 * PH])
        slot3 = sb("slot3", [P, 3 * TB * P])
        e1T, e2T, gT = top_v[:, 0:T], top_v[:, T:2 * T], sb("gT", [P, T])
        e2c = sb("e2c", [P, 12])

        cursor = [0]

        def carve(n, size=1):
            at = cursor[0]
            cursor[0] += n
            assert cursor[0] <= 27904, cursor
            return big[:, at:at + n]

        ms, rt, rr = (big[:, 27904 + i * T:27904 + (i + 1) * T] for i in range(3))
        sq = big[:, 28672:28672 + KC * T]
        keysb = big[:, 30720:30720 + 16 * NK]
        qT = big[:, 0:16 * T]

        def b3(ap, n):
            return ap.rearrange("p (a b) -> p a b", a=n)

        xv, hv, sqv = b3(xT[:, :], KC), b3(hT[:, :], KC), b3(sq, KC)

        cursor[0] = 0
        ev_small = carve(4 * CONV_W + 4 * 3 + 2 + 2)
        o = 4 * CONV_W
        cw, cb, lng, lnb = ev_small[:, 0:o], ev_small[:, o:o + 4], ev_small[:, o + 4:o + 8], ev_small[:, o + 8:o + 12]
        gb, glag = ev_small[:, o + 12:o + 14], ev_small[:, o + 14:o + 15]
        w_rank = carve(KC * RANK)
        w_gate2 = carve(GH * DK)
        e_val, e_sig = carve(CC * T), carve(CC * T)
        UW = T + CONV_W - 1
        e_u = carve(CC * UW)
        e_conv, e_xc = carve(CC * T), carve(CC * T)
        e_sq2, e_xn = e_sig, e_val
        e_q, e_k, e_r = carve(2 * T), carve(2 * T), carve(4 * T)
        e_v = carve(TB * GH * DV)
        e_glr = carve(T)
        at_zb = cursor[0]
        e_zb, e_az, e_mn, e_ln, e_la, e_b, e_eb, e_nd, e_kd, e_qb = (carve(2 * T) for _ in range(10))
        e_reset = carve(T)
        e_dif = [carve(2 * T) for _ in range(2)]
        e_exp = [carve(2 * T) for _ in range(2)]
        e_qe = [carve(2 * T) for _ in range(2)]
        e_ke = [carve(2 * T) for _ in range(2)]
        e_at = carve(2 * 2 * TB * P)
        e_kdt = carve(TB * 2 * P)
        e_state = carve(3 * 2 * DV)
        e_o, e_osq, e_orr = carve(4 * T), carve(4 * T), carve(4 * T)
        e_y = carve(KC * T)
        e_mask = carve(7 * P).bitcast(I32)
        e_si, e_ti, e_xr = carve(P).bitcast(I32), carve(P).bitcast(I32), carve(2 * P).bitcast(I32)
        e_mu = big[:, at_zb:at_zb + 3 * T]

        cursor[0] = 0
        o_fz = carve(KC * P)
        o_fb = carve(4)
        o_qk, o_sq = carve(16 * T), carve(16 * T)
        o_n = o_sq
        o_v = carve(TB * D)
        o_left, o_right = carve(FH * T), carve(FH * T)
        o_z = [carve(T) for _ in range(6)]
        causal = carve(3 * P)
        at_s = [carve(3 * P) for _ in range(2)]
        at_p = [carve(3 * P) for _ in range(2)]
        at_pt = [carve(3 * P) for _ in range(2)]
        at_small = carve(2 * 8)
        o_tmp = carve(3 * 512)
        o_y = carve(KC * T)

        cursor[0] = 0
        s_ws = carve(SG * P)
        s_bs = carve(4 * P)
        s_norm = carve(512)
        f_cw = carve(2 * FC * 3)
        f_cb = carve(2 * FC)
        s_qk, s_sq, s_n = carve(6 * T), carve(6 * T), carve(6 * T)
        s_v = carve(TB * P)
        s_u = carve(4 * T)
        s_gv, s_gv2, s_vn = carve(TB * 512), carve(TB * 512), carve(TB * 512)
        s_small = carve(8)
        s_gate = carve(16 * T)
        s_mix = carve(4 * T)
        s_ya, s_yb = carve(4 * T), carve(4 * T)
        s_prod = carve(2 * 2 * T)
        s_m = carve(KC * T)
        f_act = None
        assert cursor[0] <= 24000, cursor
        cursor[0] = max(cursor[0], 0)
        dist = carve(3 * P)
        s_at_s = [carve(3 * P) for _ in range(2)]
        s_at_p = [carve(3 * P) for _ in range(2)]
        s_at_pt = [carve(3 * P) for _ in range(2)]
        s_at_small = carve(2 * 8)
        s_tmp = carve(3 * 512)
        ZW = T + 2
        f_at = 2688
        f_z = [big[:, f_at + i * 2 * ZW:f_at + (i + 1) * 2 * ZW] for i in range(4)]
        f_at += 4 * 2 * ZW
        f_zc = [big[:, f_at + i * 2 * T:f_at + (i + 1) * 2 * T] for i in range(4)]
        f_at += 4 * 2 * T
        f_sil = [big[:, f_at + i * T:f_at + (i + 1) * T] for i in range(4)]
        f_at += 4 * T
        f_act = big[:, f_at:f_at + FC * T]
        assert f_at + FC * T <= 27904

        names = """x_loaded ev_tables_loaded tables_loaded keys_loaded od_tables_loaded sb_tables_loaded stored
            consts masks_built
            pieces_used units_out
            norm_squared norm_summed norm_mean norm_root h_ready x_ready
            key_scored scores_out ranked gate_shifted gate_exped slots_ready slots_turned turned
            first_hot second_hot gates_spread gated pool_waits pool_step dve_step act_step
            ev_rank_ready ev_rank_out ev_z_ready ev_z_in ev_z_log ev_decay_part ev_fade ev_fade_in
            ev_expb ev_expk ev_dif ev_difexp ev_qk_level ev_level ev_level_in ev_kdec ev_kdec_turned ev_kdt
            ev_chunk_sums ev_states ev_o ev_o_out ev_o_sq ev_o_sum ev_o_mean ev_o_root ev_y
            conv_step conv_done ln_sum ln_centred ln_sq ln_var ln_mean ln_root ln_normed ev_ya ev_u_in
            od_z_ready od_z_in od_z_log od_bias_ready od_sq od_sum od_mean od_root od_qk_ready od_sel
            at_score at_masked at_exped at_prob at_turned at_pt at_mixed at_y
            sb_sq sb_sum sb_mean sb_root sb_qk_ready sgu_sq sgu_mean sgu_root sgu_v_ready sgu_w_ready
            sgu_mixed sgu_y merge_ready merged_out merged ff_silu ff_z ff_gated ff_tap""".split()
        g = {n: sem(n) for n in names}
        slot_loaded = [sem(f"slot_loaded{i}") for i in range(RING)]


        def unit_bank(u):
            return bank[u % 4]

        def hot(ring_at, half):
            o = (half * 12 + ring_at) * P
            return sco[:, o:o + P]

        odd_att = dict(heads=FH, tag=0, s=at_s, p=at_p, pt=at_pt, small=at_small, y=b3(o_y, KC),
                       q=lambda h: (b3(o_n, 16), h // 2), k=lambda h: (b3(o_n, 16), 8 + h // 2),
                       v=lambda tb, h: o_v[:, tb * D + h * HD:tb * D + h * HD + HD],
                       table=causal, factor=lambda h: 1.0, base=0)
        swa_att = dict(heads=QH, tag=1, s=s_at_s, p=s_at_p, pt=s_at_pt, small=s_at_small, y=b3(s_ya, 4),
                       q=lambda h: (b3(s_n, 6), h // 2), k=lambda h: (b3(s_n, 6), 4 + h // GROUP),
                       v=lambda tb, h: s_v[:, tb * P + (h // GROUP) * HD:tb * P + (h // GROUP) * HD + HD],
                       table=dist, factor=lambda h: -(2.0 ** (-8.0 * (h + 1.0) / QH)), base=FH)

        block = ctx.enter_context(nc.Block())

        @block.sync
        def _(sp):
            n = [0]

            def load(src, at, i=0):
                k = n[0] + at
                sp.dma_start(ring[:, k % RING, :], src).then_inc(slot_loaded[k % RING], 16)

            def stream(name, count):
                done = 0
                while n[0] < RING and done < count:
                    load(a[name][done], 0)
                    n[0] += 1
                    done += 1
                loops = (count - done) // RING
                if loops:
                    with sp.Fori(0, loops) as i:
                        for j in range(RING):
                            sp.wait_ge(g["pieces_used"], i * RING + (n[0] + j - RING + 1))
                            load(a[name][bass.ds(i * RING + (done + j), 1)].rearrange("o p n -> (o p) n"), j)
                    n[0] += RING * loops
                    done += RING * loops
                for j in range(done, count):
                    sp.wait_ge(g["pieces_used"], n[0] - RING + 1)
                    load(a[name][j], 0)
                    n[0] += 1

            sp.dma_start(xT[:, :], a["x"]).then_inc(g["x_loaded"], 16)
            sp.dma_start(gains[:, :], a["gains"]).then_inc(g["tables_loaded"], 16)
            stream("ev_in", 20)
            stream("ev_out", 8)
            stream("wq0", 16)
            stream("u0", NK)
            stream("v0", NK)
            stream("od_in", 24)
            stream("od_out", 8)
            stream("wq1", 16)
            stream("u1", NK)
            stream("v1", NK)
            stream("sb_in", 31)
            stream("sb_ab", 8)
            stream("sb_out", 8)
            stream("up", 2 * FC)
            stream("down", FC)
            for j in range(4):
                sp.wait_ge(g["x_ready"], 4 * 5 + j + 1)
                sp.dma_start(out[:, j * 512:(j + 1) * 512], xT[:, j * 512:(j + 1) * 512]).then_inc(g["stored"], 16)
            sp.wait_ge(g["stored"], 64)

        @block.gpsimd
        def _(pool):
            steps = [0]

            def step(ins):
                steps[0] += 1
                ins.then_inc(g["pool_step"], 1)

            def settle():
                pool.wait_ge(g["pool_step"], steps[0])

            step(pool.memset(zeros[:, :], 0.0))
            step(pool.memset(ones[:, :], 1.0))
            step(pool.memset(ident[:, :], 0.0))
            step(pool.memset(halves[:, :], 0.0))
            step(pool.iota(iota[:, :], [[1, P]], base=0, channel_multiplier=0, allow_small_or_imprecise_dtypes=True))
            step(pool.iota(e_si, [[0, P]], base=0, channel_multiplier=1))
            step(pool.iota(e_ti, [[1, P]], base=0, channel_multiplier=0))
            step(pool.memset(e_reset, 1.0))
            step(pool.memset(e_u, 0.0))
            step(pool.memset(e_at, 0.0))
            settle()
            step(pool.affine_select(out=ident[:, :], in_=ident[:, :], compare_op=ALU.not_equal, fill=1.0,
                                    base=0, pattern=[[-1, P]], channel_multiplier=1))
            step(pool.memset(halves[0:64, 0:64], 1.0))
            settle()
            step(pool.memset(halves[64:128, 64:128], 1.0))
            settle()
            step(pool.memset(b3(e_reset, NCH)[:, :, 0:1], 0.0))
            settle()
            pool.memset(neg_row[:, :], 0.0).then_inc(g["consts"], 1)

            for layer in range(2):
                pool.wait_ge(g["turned"], 3 * (layer + 1))
                pool.tensor_copy(e2c[:, 0:12], e2T[:, 0:12]).then_inc(g["pool_step"], 1)
                steps[0] += 1
                settle()
                for q in range(3):
                    for j in range(4):
                        last = pool.tensor_scalar(hot(4 * q + j, 1), iota[:, :], e2c[:, 4 * q + j:4 * q + j + 1],
                                                  None, ALU.is_equal)
                    last.then_inc(g["second_hot"], 1)
                with pool.Fori(1, 21) as i:
                    pool.wait_ge(g["second_hot"], i * 3 + 64 * layer)
                    pool.tensor_copy(e2c[:, 0:12], e2T[:, bass.ds(i * 12, 12)]).then_inc(g["pool_step"], 1)
                    pool.wait_ge(g["pool_step"], i + steps[0])
                    for q in range(3):
                        pool.wait_ge(g["gates_spread"], i * 3 + (q - 2 + 64 * layer))
                        pool.sem_inc(g["pool_waits"], 1)
                        for j in range(4):
                            last = pool.tensor_scalar(hot(4 * q + j, 1), iota[:, :], e2c[:, 4 * q + j:4 * q + j + 1],
                                                      None, ALU.is_equal)
                        last.then_inc(g["second_hot"], 1)
                steps[0] += 20
                pool.wait_ge(g["second_hot"], 63 + 64 * layer)
                step(pool.tensor_copy(e2c[:, 0:4], e2T[:, T - 4:T]))
                settle()
                pool.wait_ge(g["gates_spread"], 61 + 64 * layer)
                for j in range(4):
                    last = pool.tensor_scalar(hot(j, 1), iota[:, :], e2c[:, j:j + 1], None, ALU.is_equal)
                last.then_inc(g["second_hot"], 1)

                if layer == 0:
                    pool.wait_ge(g["x_ready"], 4 * 2)
                    for tab in (o_left, o_right):
                        step(pool.memset(tab, 0.0))
                    step(pool.memset(causal, 0.0))
                    settle()
                    for tab, rows in ((o_left, 0), (o_left, 64), (o_right, 32), (o_right, 96)):
                        v = tab.rearrange("p (h t) -> p h t", h=FH)[rows:rows + 32]
                        step(pool.affine_select(out=v, in_=v, compare_op=ALU.not_equal, fill=1.0, base=0,
                                                pattern=[[-1, FH], [0, T]], channel_multiplier=1))
                        settle()
                    for c in (0, 2):
                        v = causal[:, c * P:(c + 1) * P]
                        step(pool.affine_select(out=v, in_=v, compare_op=ALU.is_ge, fill=-1e30, base=0,
                                                pattern=[[-1, P]], channel_multiplier=1))
                    settle()
                    pool.memset(neg_row[:, :], 0.0).then_inc(g["od_sel"], 1)
                else:
                    pool.wait_ge(g["x_ready"], 4 * 4)
                    for c, base in ((0, 0), (1, P), (2, 0)):
                        step(pool.iota(dist[:, c * P:(c + 1) * P], [[-1, P]], base=base, channel_multiplier=1,
                                       allow_small_or_imprecise_dtypes=True))
                    settle()
                    for c in (0, 2):
                        v = dist[:, c * P:(c + 1) * P]
                        step(pool.affine_select(out=v, in_=v, compare_op=ALU.is_ge, fill=FAR, base=0,
                                                pattern=[[-1, P]], channel_multiplier=1))
                    v = dist[:, P:2 * P]
                    step(pool.affine_select(out=v, in_=v, compare_op=ALU.is_gt, fill=FAR, base=0,
                                            pattern=[[1, P]], channel_multiplier=-1))
                    pool.wait_ge(g["sb_tables_loaded"], 16 * 5)
                    v = s_ws.rearrange("p (g i) -> p g i", g=SG)
                    step(pool.affine_select(out=v, in_=v, compare_op=ALU.is_ge, fill=0.0, base=0,
                                            pattern=[[0, SG], [1, P]], channel_multiplier=-1))
                    settle()
                    pool.memset(neg_row[:, :], 0.0).then_inc(g["sgu_w_ready"], 1)

        @block.scalar
        def _(act):
            n, u = [0], [0]
            A = nc.scalar.activation

            def norm(k):
                for j in range(4):
                    if k == 0:
                        if j == 0:
                            act.wait_ge(g["x_loaded"], 16)
                    else:
                        act.wait_ge(g["x_ready"], 4 * (k - 1) + j + 1)
                    A(sq[:, j * 512:(j + 1) * 512], xT[:, j * 512:(j + 1) * 512], ACT.Square).then_inc(g["norm_squared"], 1)
                act.wait_ge(g["norm_mean"], k + 1)
                A(rt, ms, ACT.Sqrt).then_inc(g["norm_root"], 1)

            def unit(outs, func=ACT.Copy, pieces=2, scale=1.0, view=None):
                n[0] += pieces
                act.wait_ge(g["pieces_used"], n[0])
                src = unit_bank(u[0])[:, 0:pieces * T]
                if view:
                    src = view(src)
                A(outs, src, func, scale=scale).then_inc(g["units_out"], 1)
                u[0] += 1

            def token_major(dst, width, piece, pieces):
                v = dst.rearrange("p (b n) -> p b n", b=TB)[:, :, piece * P:(piece + pieces) * P]
                return v.rearrange("p b (a n) -> p a b n", a=pieces)

            def tm_view(pieces):
                return lambda s: s.rearrange("p (a b n) -> p a b n", a=pieces, b=TB)

            def unit_loop(loops, dst_of, func=ACT.Copy):
                with act.Fori(0, loops) as i:
                    for q in range(4):
                        act.wait_ge(g["pieces_used"], i * 8 + (n[0] + 2 * q + 2))
                        A(dst_of(i, q), unit_bank(u[0] + q)[:, :], func).then_inc(g["units_out"], 1)
                n[0] += 8 * loops
                u[0] += 4 * loops

            act.dma_start(ev_small[:, 0:139], a["ev_small"]).then_inc(g["ev_tables_loaded"], 16)
            act.dma_start(w_rank, a["w_rank"]).then_inc(g["ev_tables_loaded"], 16)
            act.dma_start(w_gate2[0:RANK, :], a["w_gate2"]).then_inc(g["ev_tables_loaded"], 16)
            act.dma_start(qk_gain[:, :], a["qk_gain"]).then_inc(g["tables_loaded"], 16)
            act.dma_start(sinks[:, :], a["sinks"]).then_inc(g["tables_loaded"], 16)
            act.dma_start(keysb, a["keys0"]).then_inc(g["keys_loaded"], 16)

            norm(G_EV)
            act.wait_ge(g["ev_rank_ready"], 1)
            A(e_glr[0:RANK, :], bank[5][0:RANK, 0:T], ACT.Copy).then_inc(g["ev_rank_out"], 1)
            for j in range(2):
                unit(e_val[:, j * 512:(j + 1) * 512])
            for j in range(2):
                unit(e_sig[:, j * 512:(j + 1) * 512], ACT.Sigmoid)
            unit(e_q, scale=DK ** -0.5)
            unit(e_k)
            for j in range(2):
                unit(e_r[:, j * 512:(j + 1) * 512], ACT.Silu)
            for j in range(2):
                unit(token_major(e_v, 512, 2 * j, 2), view=tm_view(2))
            act.wait_ge(g["ev_z_in"], 2)
            A(e_az, e_zb, ACT.Abs).then_inc(g["act_step"], 1)
            act.wait_ge(g["act_step"], 1)
            A(e_az, e_az, ACT.Exp, scale=-1.0).then_inc(g["act_step"], 1)
            act.wait_ge(g["act_step"], 2)
            A(e_ln, e_az, ACT.Ln, bias=1.0).then_inc(g["ev_z_log"], 1)
            act.wait_ge(g["ev_decay_part"], 2)
            A(e_eb, e_b, ACT.Exp).then_inc(g["ev_expb"], 1)
            act.wait_ge(g["ev_fade"], 1)
            A(e_kd, e_nd, ACT.Exp).then_inc(g["ev_expk"], 1)
            for lv in range(6):
                act.wait_ge(g["ev_dif"], 2 * lv + 2)
                if lv >= 2:
                    act.wait_ge(g["ev_qk_level"], 2 * (lv - 1))
                A(e_exp[lv % 2], e_dif[lv % 2], ACT.Exp).then_inc(g["ev_difexp"], 1)
            act.wait_ge(g["ev_kdec_turned"], 1)
            A(e_kdt, bank[0][:, :], ACT.Copy).then_inc(g["ev_kdt"], 1)
            act.wait_ge(g["ln_centred"], 4)
            A(e_sq2, e_xc, ACT.Square).then_inc(g["ln_sq"], 1)
            act.wait_ge(g["ev_o_out"], 2)
            A(e_osq, e_o, ACT.Square).then_inc(g["ev_o_sq"], 1)
            act.wait_ge(g["ln_mean"], 1)
            A(e_mu[:, T:2 * T], e_mu[:, 0:T], ACT.Sqrt).then_inc(g["ln_root"], 1)
            act.wait_ge(g["ev_o_mean"], 2)
            A(e_orr, e_osq, ACT.Sqrt).then_inc(g["ev_o_root"], 1)
            act.wait_ge(g["ln_normed"], 1)
            for c in range(CC):
                A(e_y[:, c * T:(c + 1) * T], e_xn[:, c * T:(c + 1) * T], ACT.Silu, bias=lnb[:, c:c + 1],
                  scale=lng[:, c:c + 1]).then_inc(g["ev_ya"], 1)
            n[0] += 8

            def experts(layer):
                norm(1 + 2 * layer)
                unit_loop(2, lambda i, q: big[:, bass.ds(i * 2048 + q * 512, 512)])
                for s in range(8):
                    act.wait_ge(g["key_scored"], 8 * layer + s + 1)
                    A(sco[:, s * 512:(s + 1) * 512], bank[4 + s % 4][:, :], ACT.Copy).then_inc(g["scores_out"], 1)
                unit_loop(6, lambda i, q: big[:, bass.ds(i * 2048 + q * 512, 512)], ACT.Gelu)
                for tb in range(TB):
                    act.wait_ge(g["gate_shifted"], TB * layer + tb + 1)
                    v = slot3[:, (2 * TB + tb) * P:(2 * TB + tb + 1) * P]
                    A(v, v, ACT.Exp).then_inc(g["gate_exped"], 1)
                unit_loop(10, lambda i, q: big[:, bass.ds(i * 2048 + (6 * 2048 + q * 512), 512)], ACT.Gelu)
                n[0] += NK

            def attention(p, filler):
                for h in range(p["heads"]):
                    c = p["base"] + h
                    S, PR, PT, sm = p["s"][h % 2], p["p"][h % 2], p["pt"][h % 2], p["small"][:, (h % 2) * 8:(h % 2) * 8 + 8]
                    act.wait_ge(g["at_masked"], c + 1)
                    A(PR[:, 0:P], S[:, 0:P], ACT.Exp, bias=sm[:, 0:1], accum_out=sm[:, 2:3])
                    last = A(PR[:, P:3 * P], S[:, P:3 * P], ACT.Exp, bias=sm[:, 1:2], accum_out=sm[:, 3:4])
                    if p["tag"]:
                        last = A(sm[:, 4:6], sm[:, 0:2], ACT.Exp, bias=sinks[:, h:h + 1])
                    last.then_inc(g["at_exped"], 1)
                    filler(h)
                    act.wait_ge(g["at_turned"], c + 1)
                    if h >= 2:
                        act.wait_ge(g["at_mixed"], c - 1)
                    A(PT, bank[6][:, 0:3 * P], ACT.Copy).then_inc(g["at_pt"], 1)
                    if h % 2:
                        act.wait_ge(g["at_mixed"], c + 1)
                        A(p["y"][:, h // 2, :], bank[7][:, 0:T], ACT.Copy).then_inc(g["at_y"], 1)

            experts(0)

            act.wait_ge(g["x_ready"], 4 * 2)
            act.dma_start(o_fz, a["od_fz"]).then_inc(g["od_tables_loaded"], 16)
            act.dma_start(o_fb[:, 0:1], a["od_fb"]).then_inc(g["od_tables_loaded"], 16)
            act.dma_start(keysb, a["keys1"]).then_inc(g["keys_loaded"], 16)
            norm(G_OD)
            act.wait_ge(g["od_z_in"], 1)
            A(o_z[1], o_z[0], ACT.Abs).then_inc(g["act_step"], 1)
            act.wait_ge(g["act_step"], 3)
            A(o_z[1], o_z[1], ACT.Exp, scale=-1.0).then_inc(g["act_step"], 1)
            act.wait_ge(g["act_step"], 4)
            A(o_z[2], o_z[1], ACT.Ln, bias=1.0).then_inc(g["od_z_log"], 1)
            unit_loop(2, lambda i, q: o_qk[:, bass.ds(i * 2048 + q * 512, 512)])
            act.wait_ge(g["units_out"], u[0])
            for s in range(8):
                A(o_sq[:, s * 512:(s + 1) * 512], o_qk[:, s * 512:(s + 1) * 512], ACT.Square).then_inc(g["od_sq"], 1)
            for j in range(4):
                unit(token_major(o_v, D, 2 * j, 2), view=tm_view(2))
                for s in (2 * j, 2 * j + 1):
                    act.wait_ge(g["od_mean"], s + 1)
                    v = o_tmp[:, (s % 3) * 512:(s % 3 + 1) * 512]
                    A(v, v, ACT.Sqrt).then_inc(g["od_root"], 1)
            attention(odd_att, lambda h: None)
            n[0] += 8

            experts(1)

            act.wait_ge(g["x_ready"], 4 * 4)
            act.dma_start(s_ws, a["sb_ws"]).then_inc(g["sb_tables_loaded"], 16)
            act.dma_start(s_bs, a["sb_bs"]).then_inc(g["sb_tables_loaded"], 16)
            act.dma_start(s_norm, a["sb_norm"]).then_inc(g["sb_tables_loaded"], 16)
            act.dma_start(f_cw, a["ff_cw"]).then_inc(g["sb_tables_loaded"], 16)
            act.dma_start(f_cb, a["ff_cb"]).then_inc(g["sb_tables_loaded"], 16)
            norm(G_MIX2)
            for s in range(3):
                unit(s_qk[:, s * 512:(s + 1) * 512])
            unit(token_major(s_v, P, 0, 1), pieces=1, view=tm_view(1))
            act.wait_ge(g["units_out"], u[0])
            for s in range(3):
                A(s_sq[:, s * 512:(s + 1) * 512], s_qk[:, s * 512:(s + 1) * 512], ACT.Square).then_inc(g["sb_sq"], 1)
            for j in range(2):
                unit(token_major(s_gv, 512, 2 * j, 2), ACT.Gelu_apprx_tanh, view=tm_view(2))
            for j in range(2):
                unit(s_u[:, j * 512:(j + 1) * 512], ACT.Gelu_apprx_tanh)
            for s in range(3):
                act.wait_ge(g["sb_mean"], s + 1)
                v = s_tmp[:, s * 512:(s + 1) * 512]
                A(v, v, ACT.Sqrt).then_inc(g["sb_root"], 1)
            act.wait_ge(g["sgu_mean"], 1)
            A(s_small[:, 4:6], s_small[:, 2:4], ACT.Sqrt).then_inc(g["sgu_root"], 1)
            attention(swa_att, lambda h: unit(s_gate[:, h * 512:(h + 1) * 512], ACT.Sigmoid))
            n[0] += 16

            norm(G_FFN2)

            def z_out(i, q):
                act.wait_ge(g["pieces_used"], i * 8 + (n[0] + 2 * q + 2))
                act.wait_ge(g["ff_gated"], i * 4 + (q + 1))
                A(b3(f_z[q], 2)[:, :, 2:ZW], b3(unit_bank(u[0] + q)[:, :], 2), ACT.Copy).then_inc(g["units_out"], 1)
                act.wait_ge(g["ff_z"], i * 4 + (q + 1))
                A(f_sil[q], f_zc[q][:, 0:T], ACT.Silu).then_inc(g["ff_silu"], 1)

            with act.Fori(0, FC // 4) as i:
                for q in range(4):
                    z_out(i, q)
            for q in range(FC % 4):
                z_out(FC // 4, q)

        @block.vector
        def _(dve):
            V = nc.vector
            steps = [0]
            n, u = [0], [0]

            def step(ins):
                steps[0] += 1
                ins.then_inc(g["dve_step"], 1)

            def settle():
                dve.wait_ge(g["dve_step"], steps[0])

            def norm(k):
                dve.wait_ge(g["norm_summed"], k + 1)
                V.tensor_scalar(ms, bank[4][:, 0:T], 1.0 / D, EPS, ALU.mult, ALU.add).then_inc(g["norm_mean"], 1)
                dve.wait_ge(g["norm_root"], k + 1)
                step(V.reciprocal(rr, rt))
                settle()
                for c in range(KC):
                    V.scalar_tensor_tensor(hv[:, c, :], xv[:, c, :], gains[:, k * KC + c:k * KC + c + 1], rr,
                                           ALU.mult, ALU.mult).then_inc(g["h_ready"], 1)

            def residual(pieces, each):
                n[0] += pieces
                for j in range(4):
                    dve.wait_ge(g["pieces_used"], n[0] - (6 - 2 * j if each else 0))
                    v = xT[:, j * 512:(j + 1) * 512]
                    V.tensor_tensor(v, bank[4 + j][:, :], v, ALU.add).then_inc(g["x_ready"], 1)

            dve.wait_ge(g["consts"], 1)
            step(V.tensor_tensor(e_xr[:, 0:P], e_si, e_ti, ALU.bitwise_xor))
            settle()
            for lv, m in enumerate(LEVELS):
                sh = m.bit_length() - 1
                step(V.tensor_scalar(e_xr[:, P:2 * P], e_xr[:, 0:P], sh, None, ALU.arith_shift_right))
                settle()
                step(V.tensor_scalar(e_mask[:, 6 * P:7 * P], e_ti, sh, 1, ALU.arith_shift_right, ALU.bitwise_and))
                step(V.tensor_scalar(e_mask[:, lv * P:(lv + 1) * P], e_xr[:, P:2 * P], 1.0, None, ALU.is_equal))
                settle()
                step(V.tensor_tensor(e_mask[:, lv * P:(lv + 1) * P], e_mask[:, lv * P:(lv + 1) * P],
                                     e_mask[:, 6 * P:7 * P], ALU.bitwise_and))
            settle()
            step(V.tensor_scalar(e_mask[:, 6 * P:7 * P], e_xr[:, 0:P], 0.0, None, ALU.is_equal))

            dve.wait_ge(g["tables_loaded"], 48)
            norm(G_EV)
            n[0] += 20
            dve.wait_ge(g["units_out"], 4)
            uv = e_u.rearrange("p (c t) -> p c t", c=CC)
            step(V.tensor_tensor(uv[:, :, CONV_W - 1:UW], b3(e_val, CC), b3(e_sig, CC), ALU.mult))
            settle()
            dve.wait_ge(g["ev_tables_loaded"], 48)
            cv = b3(e_conv, CC)
            for c in range(CC):
                V.tensor_scalar(cv[:, c, :], uv[:, c, 0:T], cw[:, c:c + 1], cb[:, c:c + 1], ALU.mult,
                                ALU.add).then_inc(g["conv_step"], 1)
            with dve.Fori(0, (CONV_W - 1) // 2) as i:
                for w in range(2):
                    for c in range(CC):
                        dve.wait_ge(g["conv_step"], i * 2 * CC + (w * CC + c + 1))
                        V.scalar_tensor_tensor(cv[:, c, :], e_u[:, bass.ds(i * 2 + (c * UW + w + 1), T)],
                                               cw[:, bass.ds(i * 2 * CC + ((w + 1) * CC + c), 1)], cv[:, c, :],
                                               ALU.mult, ALU.add).then_inc(g["conv_step"], 1)
            dve.wait_ge(g["ev_z_ready"], 1)
            for f in range(2):
                V.tensor_scalar(e_zb[:, f * T:(f + 1) * T], bank[5][:, f * T:(f + 1) * T], gb[:, f:f + 1], None,
                                ALU.add).then_inc(g["ev_z_in"], 1)
            dve.wait_ge(g["ev_z_in"], 2)
            step(V.tensor_scalar(e_mn, e_zb, 0.0, 1.0 / TAU, ALU.min, ALU.mult))
            settle()
            dve.wait_ge(g["ev_z_log"], 1)
            step(V.scalar_tensor_tensor(e_la, e_ln, -1.0 / TAU, e_mn, ALU.mult, ALU.add))
            settle()
            for f in range(2):
                V.tensor_tensor_scan(e_b[:, f * T:(f + 1) * T], e_reset, e_la[:, f * T:(f + 1) * T], 0.0,
                                     ALU.mult, ALU.add).then_inc(g["ev_decay_part"], 1)
            dve.wait_ge(g["ev_decay_part"], 2)
            b8 = b3(e_b, 2 * NCH)
            V.tensor_tensor(b3(e_nd, 2 * NCH), b8[:, :, CHUNK - 1:CHUNK].to_broadcast([P, 2 * NCH, CHUNK]), b8,
                            ALU.subtract).then_inc(g["ev_fade"], 1)
            atv = e_at.rearrange("p (r c t) -> p r c t", r=2, t=P)

            def take(lv):
                if lv:
                    dve.wait_ge(g["ev_level_in"], 2 * lv)
                for r in range(2):
                    dve.wait_ge(g["ev_level"], lv + 1)
                    V.copy_predicated(atv[:, r], e_mask[:, lv * P:(lv + 1) * P].rearrange("p (o t) -> p o t", o=1).to_broadcast([P, 4, P]),
                                      b3(bank[4 + 2 * (lv % 2) + r][:, :], 4)).then_inc(g["ev_level_in"], 1)

            for lv, m in enumerate(LEVELS):
                if lv >= 2:
                    dve.wait_ge(g["ev_difexp"], lv - 1)
                bm = e_b.rearrange("p (a m) -> p a m", m=2 * m)
                dm = e_dif[lv % 2].rearrange("p (a m) -> p a m", m=2 * m)
                ref = bm[:, :, m - 1:m].to_broadcast([P, 2 * T // (2 * m), m])
                V.tensor_tensor(dm[:, :, 0:m], ref, bm[:, :, 0:m], ALU.subtract).then_inc(g["ev_dif"], 1)
                V.tensor_tensor(dm[:, :, m:2 * m], bm[:, :, m:2 * m], ref, ALU.subtract).then_inc(g["ev_dif"], 1)
                dve.wait_ge(g["ev_difexp"], lv + 1)
                if lv == 0:
                    dve.wait_ge(g["units_out"], 8)
                if lv >= 2:
                    dve.wait_ge(g["ev_level"], lv - 1)
                V.tensor_tensor(e_qe[lv % 2], e_q, e_exp[lv % 2], ALU.mult).then_inc(g["ev_qk_level"], 1)
                V.tensor_tensor(e_ke[lv % 2], e_k, e_exp[lv % 2], ALU.mult).then_inc(g["ev_qk_level"], 1)
                if lv >= 1:
                    take(lv - 1)
            dve.wait_ge(g["ev_expk"], 1)
            V.tensor_tensor(e_kd, e_k, e_kd, ALU.mult).then_inc(g["ev_kdec"], 1)
            dve.wait_ge(g["ev_expb"], 1)
            V.tensor_tensor(e_qb, e_q, e_eb, ALU.mult).then_inc(g["ev_kdec"], 1)
            take(5)
            take(6)
            dve.wait_ge(g["ev_chunk_sums"], 1)
            st = e_state.rearrange("p (c f n) -> p c f n", c=3, f=2)
            step(V.tensor_copy(st[:, 0], bank[1][:, 0:256].rearrange("p (f n) -> p f n", f=2)))
            settle()
            for c, src in ((1, bank[2][:, 0:256]), (2, bank[1][:, 256:512])):
                for f in range(2):
                    e = f * T + c * CHUNK + CHUNK - 1
                    step(V.scalar_tensor_tensor(st[:, c, f], st[:, c - 1, f], e_eb[:, e:e + 1], src[:, f * DV:(f + 1) * DV],
                                                ALU.mult, ALU.add))
                settle()
            V.memset(neg_row[:, 0:1], 0.0).then_inc(g["ev_states"], 1)
            dve.wait_ge(g["ln_sum"], 1)
            for c in range(CC):
                V.scalar_tensor_tensor(b3(e_xc, CC)[:, c, :], bank[3][:, 0:T], -1.0 / CONV_CH, cv[:, c, :],
                                       ALU.mult, ALU.add).then_inc(g["ln_centred"], 1)
            dve.wait_ge(g["ev_o"], 1)
            for r in range(2):
                V.tensor_copy(e_o[:, r * 512:(r + 1) * 512], bank[6 + r][:, :]).then_inc(g["ev_o_out"], 1)
            dve.wait_ge(g["ln_var"], 1)
            V.tensor_scalar(e_mu[:, 0:T], bank[3][:, 0:T], 1.0 / CONV_CH, EPS, ALU.mult, ALU.add).then_inc(g["ln_mean"], 1)
            dve.wait_ge(g["ev_o_sum"], 1)
            for r in range(2):
                V.tensor_scalar(e_osq[:, r * 512:(r + 1) * 512], bank[4 + r][:, :], 1.0 / DV, EPS, ALU.mult,
                                ALU.add).then_inc(g["ev_o_mean"], 1)
            dve.wait_ge(g["ln_root"], 1)
            step(V.reciprocal(e_mu[:, 2 * T:3 * T], e_mu[:, T:2 * T]))
            settle()
            V.tensor_tensor(b3(e_xn, CC), b3(e_xc, CC),
                            e_mu[:, 2 * T:3 * T].rearrange("p (o t) -> p o t", o=1).to_broadcast([P, CC, T]),
                            ALU.mult).then_inc(g["ln_normed"], 1)
            dve.wait_ge(g["ev_o_root"], 1)
            step(V.reciprocal(e_orr, e_orr))
            settle()
            step(V.scalar_tensor_tensor(e_o, e_o, glag, e_orr, ALU.mult, ALU.mult))
            settle()
            for r in range(2):
                dst = e_y[:, 4 * T:8 * T].rearrange("p (f r t) -> p r f t", f=2, r=2)[:, r]
                gate = e_r.rearrange("p (f r t) -> p r f t", f=2, r=2)[:, r]
                V.tensor_tensor(dst, e_o[:, r * 512:(r + 1) * 512].rearrange("p (f t) -> p f t", f=2), gate,
                                ALU.mult).then_inc(g["ev_y"], 1)
            u[0] = 10
            residual(8, True)

            def top16(vals, idx, src, groups, width):
                def at(ap, j, half):
                    return ap[:, j * 16 + 8 * half:j * 16 + 8 * half + 8]

                def row(j):
                    return src[:, j * width:(j + 1) * width]

                for half in range(2):
                    for j in range(groups):
                        step(V.max(at(vals, j, half), row(j)))
                    settle()
                    for j in range(groups):
                        step(V.max_index(at(idx, j, half), at(vals, j, half), row(j)))
                    if not half:
                        settle()
                        for j in range(groups):
                            step(V.match_replace(row(j), at(vals, j, 0), row(j), NEG_BIG))
                        settle()

            def experts(layer):
                norm(1 + 2 * layer)
                n[0] += 16 + NK
                for tb in range(TB):
                    dve.wait_ge(g["scores_out"], 8 * layer + 4 * (tb + 1))
                    top16(top_v[:, tb * 256:(tb + 1) * 256], top_i[:, tb * 256:(tb + 1) * 256],
                          sco[:, tb * 2048:(tb + 1) * 2048], 16, NK)
                settle()
                step(V.tensor_copy(top_if[:, :], top_i[:, :]))
                cand, oh = sco[:, 0:2048], sco[:, 2048:4096]
                for tb in range(TB):
                    tv = top_v[:, tb * 256:(tb + 1) * 256].rearrange("p (h c k) -> p h c k", h=PH, c=2)
                    ti = top_if[:, tb * 256:(tb + 1) * 256].rearrange("p (h c k) -> p h c k", h=PH, c=2)
                    settle()
                    for h in range(PH):
                        step(V.tensor_tensor(cand[:, h * 256:(h + 1) * 256].rearrange("p (a b) -> p a b", a=16),
                                             tv[:, h, 0, :].rearrange("p (k o) -> p k o", o=1).to_broadcast([P, 16, 16]),
                                             tv[:, h, 1, :].rearrange("p (o k) -> p o k", o=1).to_broadcast([P, 16, 16]), ALU.add))
                    settle()
                    top16(cand_v[:, :], cand_i[:, :], cand, PH, 256)
                    settle()
                    step(V.tensor_scalar(rank_u[:, 0:P], cand_i[:, :], 4, None, ALU.logical_shift_right))
                    step(V.tensor_scalar(rank_u[:, P:2 * P], cand_i[:, :], 15, None, ALU.bitwise_and))
                    settle()
                    step(V.tensor_copy(rank_f[:, :], rank_u[:, :]))
                    for c in range(2):
                        settle()
                        step(V.tensor_tensor(oh.rearrange("p (s k) -> p s k", k=16),
                                             rank_f[:, c * P:(c + 1) * P].rearrange("p (s o) -> p s o", o=1).to_broadcast([P, P, 16]),
                                             iota[:, 0:16].rearrange("p (o k) -> p o k", o=1).to_broadcast([P, P, 16]), ALU.is_equal))
                        settle()
                        for h in range(PH):
                            v = oh[:, h * 256:(h + 1) * 256].rearrange("p (s k) -> p s k", k=16)
                            step(V.tensor_tensor(v, v, ti[:, h, c, :].rearrange("p (o k) -> p o k", o=1).to_broadcast([P, 16, 16]), ALU.mult))
                        settle()
                        step(V.tensor_reduce(slot3[:, (c * TB + tb) * P:(c * TB + tb + 1) * P],
                                             oh.rearrange("p (s k) -> p s k", k=16), AX.X, ALU.add))
                    cvv = cand_v[:, :].rearrange("p (h k) -> p h k", h=PH)
                    V.tensor_tensor(slot3[:, (2 * TB + tb) * P:(2 * TB + tb + 1) * P].rearrange("p (h k) -> p h k", h=PH),
                                    cvv, cvv[:, :, 0:1].to_broadcast([P, PH, 16]), ALU.subtract).then_inc(g["gate_shifted"], 1)
                for tb in range(TB):
                    gt = slot3[:, (2 * TB + tb) * P:(2 * TB + tb + 1) * P].rearrange("p (h k) -> p h k", h=PH)
                    gs = gate_s[:, tb * PH:(tb + 1) * PH]
                    dve.wait_ge(g["gate_exped"], TB * layer + tb + 1)
                    step(V.tensor_reduce(gs, gt, AX.X, ALU.add))
                    settle()
                    step(V.reciprocal(gs, gs))
                    settle()
                    V.tensor_tensor(gt, gt, gs.rearrange("p (h o) -> p h o", o=1).to_broadcast([P, PH, 16]),
                                    ALU.mult).then_inc(g["slots_ready"], 1)
                settle()
                dve.wait_ge(g["slots_turned"], layer + 1)
                V.tensor_copy(e1T, bank[4][:, 0:T]).then_inc(g["turned"], 1)
                V.tensor_copy(e2T, bank[4][:, T:2 * T]).then_inc(g["turned"], 1)
                V.tensor_copy(gT[:, :], bank[5][:, 0:T]).then_inc(g["turned"], 1)
                dve.wait_ge(g["turned"], 3 * layer + 3)
                acts = big[:, :].rearrange("p (e t) -> p e t", t=T)
                base = 64 * layer

                def build(slot, t0):
                    for j in range(4):
                        last = V.tensor_scalar(hot(4 * slot + j, 0), iota[:, :], e1T[:, bass.ds(t0 + j, 1)],
                                               gT[:, bass.ds(t0 + j, 1)], ALU.is_equal, ALU.mult)
                    last.then_inc(g["first_hot"], 1)

                def gate(b, t0):
                    v = acts[:, :, bass.ds(t0, 4)]
                    V.tensor_tensor(v, bank[b][:, :].rearrange("p (j e) -> p e j", j=4), v, ALU.mult).then_inc(g["gated"], 1)

                u[0] += 8 + 64
                build(0, 0)
                build(1, 4)
                dve.wait_ge(g["units_out"], u[0])
                dve.wait_ge(g["gates_spread"], base + 1)
                gate(0, 0)
                build(2, 8)
                dve.wait_ge(g["gates_spread"], base + 2)
                gate(1, 4)
                with dve.Fori(0, 20) as i:
                    for q in range(3):
                        dve.wait_ge(g["gates_spread"], i * 3 + (base + q + 1))
                        build(q, i * 12 + (4 * (q + 3)))
                        dve.wait_ge(g["gates_spread"], i * 3 + (base + q + 3))
                        gate((q + 2) % 3, i * 12 + (4 * (q + 2)))
                dve.wait_ge(g["gates_spread"], base + 61)
                build(0, 4 * 63)
                dve.wait_ge(g["gates_spread"], base + 63)
                gate(62 % 3, 4 * 62)
                dve.wait_ge(g["gates_spread"], base + 64)
                gate(63 % 3, 4 * 63)
                residual(NK, False)

            experts(0)

            def log_sigmoid_rows():
                dve.wait_ge(g["od_z_ready"], 1)
                dve.wait_ge(g["od_tables_loaded"], 32)
                V.tensor_scalar(o_z[0], bank[5][:, 0:T], o_fb[:, 0:1], None, ALU.add).then_inc(g["od_z_in"], 1)
                dve.wait_ge(g["od_z_in"], 1)
                step(V.tensor_scalar(o_z[3], o_z[0], 0.0, None, ALU.min))
                settle()
                dve.wait_ge(g["od_z_log"], 1)
                step(V.tensor_tensor(o_z[4], o_z[3], o_z[2], ALU.subtract))
                settle()
                step(V.memset(o_z[0], 1.0))
                settle()
                step(V.tensor_tensor_scan(o_z[5], o_z[0], o_z[4], 0.0, ALU.mult, ALU.add))
                settle()
                dve.wait_ge(g["od_sel"], 1)
                for rows in (0, 64):
                    step(V.tensor_scalar(o_right.rearrange("p (h t) -> p h t", h=FH)[rows:rows + 32],
                                         o_z[5][rows:rows + 32].rearrange("p (o t) -> p o t", o=1).to_broadcast([32, FH, T]),
                                         -1.0, None, ALU.mult))
                    step(V.tensor_copy(o_left.rearrange("p (h t) -> p h t", h=FH)[rows + 32:rows + 48],
                                       o_z[5][rows + 32:rows + 48].rearrange("p (o t) -> p o t", o=1).to_broadcast([16, FH, T])))
                settle()
                V.memset(neg_row[:, 0:1], 0.0).then_inc(g["od_bias_ready"], 1)

            def head_norm(count, raw, tmp, dst, gain, done, mean, root, ready):
                for s in range(count):
                    v = tmp[:, (s % 3) * 512:(s % 3 + 1) * 512]
                    dve.wait_ge(g[done], s + 1)
                    if s >= 3:
                        dve.wait_ge(g[ready], s - 2)
                    V.tensor_scalar(v, bank[4 + s % 4][:, :], 1.0 / HD, EPS, ALU.mult, ALU.add).then_inc(g[mean], 1)
                    dve.wait_ge(g[root], s + 1)
                    step(V.reciprocal(v, v))
                    settle()
                    V.scalar_tensor_tensor(dst[:, s * 512:(s + 1) * 512], raw[:, s * 512:(s + 1) * 512], gain(s), v,
                                           ALU.mult, ALU.mult).then_inc(g[ready], 1)

            def attention(p):
                for h in range(p["heads"] + 1):
                    if h < p["heads"]:
                        c = p["base"] + h
                        S, sm = p["s"][h % 2], p["small"][:, (h % 2) * 8:(h % 2) * 8 + 8]
                        dve.wait_ge(g["at_score"], c + 1)
                        if h >= 2:
                            dve.wait_ge(g["at_exped"], c - 1)
                        step(V.scalar_tensor_tensor(S, p["table"], p["factor"](h), bank[4 + h % 2][:, 0:3 * P],
                                                    ALU.mult, ALU.add))
                        settle()
                        first = V.tensor_reduce(sm[:, 0:1], S[:, 0:P], AX.X, ALU.max, negate=True)
                        step(first)
                        if p["tag"]:
                            step(V.tensor_reduce(sm[:, 1:2], S[:, P:3 * P], AX.X, ALU.max, negate=True))
                            settle()
                            V.tensor_scalar(sm[:, 0:2], sm[:, 0:2], slot3[:, h:h + 1], None, ALU.min).then_inc(g["at_masked"], 1)
                        else:
                            settle()
                            V.tensor_reduce(sm[:, 1:2], S[:, P:3 * P], AX.X, ALU.max, negate=True).then_inc(g["at_masked"], 1)
                    if h >= 1:
                        c = p["base"] + h - 1
                        PR, sm = p["p"][(h - 1) % 2], p["small"][:, ((h - 1) % 2) * 8:((h - 1) % 2) * 8 + 8]
                        dve.wait_ge(g["at_exped"], c + 1)
                        if p["tag"]:
                            step(V.tensor_tensor(sm[:, 2:4], sm[:, 2:4], sm[:, 4:6], ALU.add))
                            settle()
                        step(V.reciprocal(sm[:, 6:8], sm[:, 2:4]))
                        settle()
                        step(V.tensor_scalar(PR[:, 0:P], PR[:, 0:P], sm[:, 6:7], None, ALU.mult))
                        settle()
                        V.tensor_scalar(PR[:, P:3 * P], PR[:, P:3 * P], sm[:, 7:8], None, ALU.mult).then_inc(g["at_prob"], 1)

            norm(G_OD)
            step(V.tensor_scalar(qk_gain[:, 0:1], qk_gain[:, 0:1], HD ** -0.5, None, ALU.mult))
            step(V.tensor_scalar(qk_gain[:, 2:3], qk_gain[:, 2:3], HD ** -0.5, None, ALU.mult))
            log_sigmoid_rows()
            head_norm(8, o_qk, o_tmp, o_n, lambda s: qk_gain[:, 0:1] if s < 4 else qk_gain[:, 1:2],
                      "od_sum", "od_mean", "od_root", "od_qk_ready")
            attention(odd_att)
            u[0] += 12
            n[0] += 24
            residual(8, True)

            experts(1)

            norm(G_MIX2)
            step(V.tensor_scalar(slot3[:, 0:QH], sinks[:, :], -1.0, None, ALU.mult))
            dve.wait_ge(g["sb_tables_loaded"], 80)
            head_norm(3, s_qk, s_tmp, s_n, lambda s: qk_gain[:, 2:3] if s < 2 else qk_gain[:, 3:4],
                      "sb_sum", "sb_mean", "sb_root", "sb_qk_ready")
            dve.wait_ge(g["units_out"], u[0] + 8)
            for tb in range(TB):
                v = s_gv[:, tb * 512:(tb + 1) * 512]
                step(V.tensor_tensor(s_gv2[:, tb * 512:(tb + 1) * 512], v, v, ALU.mult))
            settle()
            step(V.tensor_reduce(s_small[:, 0:2], b3(s_gv2, TB), AX.X, ALU.add))
            settle()
            V.tensor_scalar(s_small[:, 2:4], s_small[:, 0:2], 1.0 / 512, EPS, ALU.mult, ALU.add).then_inc(g["sgu_mean"], 1)
            dve.wait_ge(g["sgu_root"], 1)
            step(V.reciprocal(s_small[:, 6:8], s_small[:, 4:6]))
            settle()
            for tb in range(TB):
                V.scalar_tensor_tensor(s_vn[:, tb * 512:(tb + 1) * 512], s_gv[:, tb * 512:(tb + 1) * 512],
                                       s_small[:, 6 + tb:7 + tb], s_norm, ALU.mult, ALU.mult).then_inc(g["sgu_v_ready"], 1)
            dve.wait_ge(g["sgu_mixed"], 1)
            for j in range(2):
                step(V.tensor_tensor(s_mix[:, j * 512:(j + 1) * 512].rearrange("p (c b t) -> p c b t", c=2, b=TB),
                                     bank[6 + j][:, :].rearrange("p (c b t) -> p c b t", c=2, b=TB),
                                     s_bs[:, j * 256:(j + 1) * 256].rearrange("p (c o t) -> p c o t", c=2, o=1).to_broadcast([P, 2, TB, P]),
                                     ALU.add))
            settle()
            V.tensor_tensor(s_yb, s_mix, s_u, ALU.mult).then_inc(g["sgu_y"], 1)
            attention(swa_att)
            u[0] += 16
            dve.wait_ge(g["units_out"], u[0])
            n[0] += 31
            gates = s_gate.rearrange("p (b c t) -> p b c t", b=2, c=KC)
            for c in range(KC):
                dve.wait_ge(g["pieces_used"], n[0] + c + 1)
                pr = s_prod[:, (c % 2) * 512:(c % 2 + 1) * 512]
                V.tensor_tensor(b3(pr, 2), b3(bank[c % 4][:, :], 2), gates[:, :, c, :], ALU.mult).then_inc(g["merged_out"], 1)
                dve.wait_ge(g["merged_out"], c + 1)
                V.tensor_tensor(s_m[:, c * T:(c + 1) * T], pr[:, 0:T], pr[:, T:2 * T], ALU.add).then_inc(g["merged"], 1)
            n[0] += 8
            residual(8, True)

            norm(G_FFN2)
            for q in range(4):
                V.memset(b3(f_z[q], 2)[:, :, 0:2], 0.0).then_inc(g["ff_gated"], 1)

            def convolve(i, q):
                dve.wait_ge(g["units_out"], i * 4 + (u[0] + q + 1))
                z, zc = b3(f_z[q], 2), b3(f_zc[q], 2)
                for half in range(2):
                    col = q * 2 + half
                    V.tensor_scalar(zc[:, half, :], z[:, half, 0:T], f_cw[:, bass.ds(i * 24 + 3 * col, 1)],
                                    f_cb[:, bass.ds(i * 8 + col, 1)], ALU.mult, ALU.add).then_inc(g["ff_tap"], 1)
                for tap in (1, 2):
                    dve.wait_ge(g["ff_tap"], i * 16 + (q * 4 + 2 * tap))
                    for half in range(2):
                        col = q * 2 + half
                        ins = V.scalar_tensor_tensor(zc[:, half, :], z[:, half, tap:tap + T],
                                                     f_cw[:, bass.ds(i * 24 + (3 * col + tap), 1)], zc[:, half, :],
                                                     ALU.mult, ALU.add)
                        if tap == 1:
                            ins.then_inc(g["ff_tap"], 1)
                ins.then_inc(g["ff_z"], 1)
                dve.wait_ge(g["ff_silu"], i * 4 + (q + 1))
                V.tensor_tensor(f_act[:, bass.ds(i * 4 * T + q * T, T)], f_sil[q], f_zc[q][:, T:2 * T],
                                ALU.mult).then_inc(g["ff_gated"], 1)

            with dve.Fori(0, FC // 4) as i:
                for q in range(4):
                    convolve(i, q)
            for q in range(FC % 4):
                convolve(FC // 4, q)
            n[0] += 2 * FC
            residual(FC, False)

        @block.tensor
        def _(pe):
            n, u = [0], [0]
            mm = nc.tensor.matmul

            def norm(k):
                for j in range(4):
                    pe.wait_ge(g["norm_squared"], 4 * k + j + 1)
                    for c in (2 * j, 2 * j + 1):
                        last = mm(bank[4][:, 0:T], ones[:, :], sqv[:, c, :], start=(c == 0), stop=(c == KC - 1))
                last.then_inc(g["norm_summed"], 1)

            def weights(at, i):
                k = n[0] + at
                pe.wait_ge(slot_loaded[k % RING], i * 16 + 16 * (k // RING + 1))
                return ring[:, k % RING, :]

            def features(dst, w, x):
                for c in range(KC):
                    last = mm(dst, w[:, c * P:(c + 1) * P], x[:, c, :], start=(c == 0), stop=(c == KC - 1))
                return last

            def tokens(dst, w, x):
                for b in range(TB):
                    for c in range(KC):
                        last = mm(dst[:, b * P:(b + 1) * P], x[:, c, b * P:(b + 1) * P], w[:, c * P:(c + 1) * P],
                                  start=(c == 0), stop=(c == KC - 1))
                return last

            def unit(make, x, pieces=2, at=0, q=0, i=0):
                if u[0] + q >= 4:
                    pe.wait_ge(g["units_out"], i * 4 + (u[0] + q - 3))
                for j in range(pieces):
                    w = weights(at + j, i)
                    make(unit_bank(u[0] + q)[:, j * T:(j + 1) * T], w, x).then_inc(g["pieces_used"], 1)

            def one_unit(make, x, pieces=2):
                unit(make, x, pieces)
                n[0] += pieces
                u[0] += 1

            def unit_loop(loops, x, first_peeled=False):
                with pe.Fori(0, loops) as i:
                    for q in range(4):
                        unit(features, x, 2, 2 * q, q, i)
                n[0] += 8 * loops
                u[0] += 4 * loops

            def add_to_stream(x):
                for j in range(8):
                    w = weights(0, 0)
                    features(bank[4 + j // 2][:, (j % 2) * T:(j % 2 + 1) * T], w, x).then_inc(g["pieces_used"], 1)
                    n[0] += 1

            def clear_banks():
                for j in range(4):
                    mm(bank[4 + j][:, :], zeros[:, 0:P], zeros[:, :], start=True, stop=False, skip_group_check=True)

            def accumulate(count, x_of):
                def piece(at, i):
                    w = weights(at, i)
                    x = x_of(i, at)
                    for c in range(KC):
                        last = mm(bank[4 + c // 2][:, (c % 2) * T:(c % 2 + 1) * T], w[:, c * P:(c + 1) * P], x,
                                  start=False, stop=False, skip_group_check=True)
                    last.then_inc(g["pieces_used"], 1)

                with pe.Fori(0, count // RING) as i:
                    for j in range(RING):
                        piece(j, i)
                for j in range(count % RING):
                    piece(j, count // RING)
                n[0] += count

            pe.wait_ge(g["consts"], 1)
            norm(G_EV)
            pe.wait_ge(g["h_ready"], KC)
            pe.wait_ge(g["ev_tables_loaded"], 48)
            for c in range(KC):
                last = mm(bank[5][0:RANK, 0:T], w_rank[:, c * RANK:(c + 1) * RANK], hv[:, c, :], start=(c == 0), stop=(c == KC - 1))
            last.then_inc(g["ev_rank_ready"], 1)
            for j in range(4):
                one_unit(features, hv)
            unit_loop(1, hv)
            for j in range(2):
                one_unit(tokens, hv)
            pe.wait_ge(g["ev_rank_out"], 1)
            for f in range(2):
                last = mm(bank[5][:, f * T:(f + 1) * T], w_gate2[0:RANK, f * P:(f + 1) * P], e_glr[0:RANK, :], start=True, stop=True)
            last.then_inc(g["ev_z_ready"], 1)
            for lv in range(7):
                if lv < 6:
                    pe.wait_ge(g["ev_qk_level"], 2 * (lv + 1))
                    qe, ke = e_qe[lv % 2], e_ke[lv % 2]
                else:
                    qe, ke = e_q, e_k
                if lv >= 2:
                    pe.wait_ge(g["ev_level_in"], 2 * (lv - 1))
                for f in range(2):
                    for b in range(TB):
                        for r in range(2):
                            rows = slice(64 * r, 64 * r + 64)
                            cols = slice(f * T + b * P, f * T + b * P + P)
                            last = mm(bank[4 + 2 * (lv % 2) + r][:, (f * TB + b) * P:(f * TB + b + 1) * P],
                                      ke[rows, cols], qe[rows, cols], start=True, stop=True)
                last.then_inc(g["ev_level"], 1)
            pe.wait_ge(g["ev_kdec"], 2)
            pe.wait_ge(g["units_out"], 10)
            for b in range(TB):
                for f in range(2):
                    last = nc.tensor.transpose(bank[0][:, (b * 2 + f) * P:(b * 2 + f + 1) * P],
                                               e_kd[:, f * T + b * P:f * T + b * P + P], ident[:, :])
            last.then_inc(g["ev_kdec_turned"], 1)
            pe.wait_ge(g["conv_step"], CC * CONV_W)
            for c in range(CC):
                last = mm(bank[3][:, 0:T], ones[:, :], b3(e_conv, CC)[:, c, :], start=(c == 0), stop=(c == CC - 1))
            last.then_inc(g["ln_sum"], 1)
            pe.wait_ge(g["ev_kdt"], 1)
            for c, dst in ((0, bank[1][:, 0:256]), (2, bank[1][:, 256:512]), (1, bank[2][:, 0:256])):
                for h in range(GH):
                    rows = slice(64 * (c % 2), 64 * (c % 2) + 64)
                    last = mm(dst[64 * (h % 2):64 * (h % 2) + 64, (h // 2) * DV:(h // 2 + 1) * DV],
                              e_kdt[rows, (c // 2) * 256 + h * DK:(c // 2) * 256 + (h + 1) * DK],
                              e_v[rows, (c // 2) * 512 + h * DV:(c // 2) * 512 + (h + 1) * DV], start=True, stop=True)
            last.then_inc(g["ev_chunk_sums"], 1)
            pe.wait_ge(g["ev_level_in"], 14)
            pe.wait_ge(g["ev_states"], 1)
            st = e_state.rearrange("p (c f n) -> p c f n", c=3, f=2)
            atv = e_at.rearrange("p (r f b t) -> p r f b t", r=2, f=2, b=TB)
            for h in range(GH):
                f, r = h // 2, h % 2
                rows = slice(64 * r, 64 * r + 64)
                for b in range(TB):
                    dst = bank[6 + r][:, (f * TB + b) * P:(f * TB + b + 1) * P]
                    last = mm(dst, e_v[:, b * 512 + h * DV:b * 512 + (h + 1) * DV], atv[:, r, f, b, :], start=True, stop=False)
                    for c in (2 * b, 2 * b + 1):
                        if c:
                            last = mm(dst[:, (c % 2) * CHUNK:(c % 2 + 1) * CHUNK], st[rows, c - 1, f, :],
                                      e_qb[rows, f * T + c * CHUNK:f * T + (c + 1) * CHUNK], start=False, stop=(c % 2 == 1))
            last.then_inc(g["ev_o"], 1)
            pe.wait_ge(g["ln_sq"], 1)
            for c in range(CC):
                last = mm(bank[3][:, 0:T], ones[:, :], b3(e_sq2, CC)[:, c, :], start=(c == 0), stop=(c == CC - 1))
            last.then_inc(g["ln_var"], 1)
            pe.wait_ge(g["ev_o_sq"], 1)
            for r in range(2):
                last = mm(bank[4 + r][:, :], ones[:, :], e_osq[:, r * 512:(r + 1) * 512], start=True, stop=True)
            last.then_inc(g["ev_o_sum"], 1)
            pe.wait_ge(g["ev_y"], 2)
            pe.wait_ge(g["ev_ya"], 4)
            add_to_stream(b3(e_y, KC))

            def experts(layer):
                norm(1 + 2 * layer)
                pe.wait_ge(g["h_ready"], KC * (2 + 2 * layer))
                unit_loop(2, hv)
                pe.wait_ge(g["units_out"], u[0])
                pe.wait_ge(g["keys_loaded"], 16 * (layer + 1))
                for s in range(8):
                    if s >= 4:
                        pe.wait_ge(g["scores_out"], 8 * layer + s - 3)
                    for j in range(4):
                        k = (s % 4) * 4 + j
                        last = mm(bank[4 + s % 4][:, j * P:(j + 1) * P], qT[:, k * T + (s // 4) * P:k * T + (s // 4) * P + P],
                                  keysb[:, k * NK:(k + 1) * NK], start=True, stop=True)
                    last.then_inc(g["key_scored"], 1)
                unit_loop(16, hv)
                pe.wait_ge(g["slots_ready"], TB * (layer + 1))
                pe.wait_ge(g["scores_out"], 8 * (layer + 1))
                for c in range(3):
                    for b in range(TB):
                        dst = (bank[4][:, 0:T], bank[4][:, T:2 * T], bank[5][:, 0:T])[c]
                        last = nc.tensor.transpose(dst[:, b * P:(b + 1) * P], slot3[:, (c * TB + b) * P:(c * TB + b + 1) * P],
                                                   ident[:, :])
                last.then_inc(g["slots_turned"], 1)
                pe.wait_ge(g["units_out"], u[0])
                base = 64 * layer

                def spread(slot, quad):
                    pe.wait_ge(g["first_hot"], quad + (base + 1))
                    pe.wait_ge(g["second_hot"], quad + (base + 1))
                    for j in range(4):
                        last = mm(bank[slot][:, j * P:(j + 1) * P], hot(4 * slot + j, 1), hot(4 * slot + j, 0), start=True, stop=True)
                    last.then_inc(g["gates_spread"], 1)

                for q in range(3):
                    spread(q, q)
                with pe.Fori(1, 21) as i:
                    for q in range(3):
                        pe.wait_ge(g["gated"], i * 3 + (base + q - 2))
                        spread(q, i * 3 + q)
                pe.wait_ge(g["gated"], base + 61)
                spread(0, 63)
                pe.wait_ge(g["turned"], 3 * layer + 3)
                clear_banks()
                pe.wait_ge(g["gated"], base + 64)
                accumulate(NK, lambda i, j: big[:, bass.ds(i * 8 * T + j * T, T)])

            def attention(p, filler):
                def score(h):
                    c = p["base"] + h
                    rows = slice(64 * (h % 2), 64 * (h % 2) + 64)
                    (q, qc), (k, kc) = p["q"](h), p["k"](h)
                    if h >= 2:
                        pe.wait_ge(g["at_masked"], c - 1)
                    dst = bank[4 + h % 2]
                    last = None
                    for lo, b, keys in ((0, 0, P), (P, 1, 2 * P)):
                        last = mm(dst[:, lo:lo + keys], q[rows, qc, b * P:(b + 1) * P], k[rows, kc, 0:keys],
                                  start=True, stop=bool(p["tag"]))
                        if not p["tag"]:
                            rb = slice(64 * (h % 2), 64 * (h % 2) + 48)
                            last = mm(dst[:, lo:lo + keys], o_left[rb, h * T + b * P:h * T + (b + 1) * P],
                                      o_right[rb, h * T:h * T + keys], start=False, stop=True)
                    last.then_inc(g["at_score"], 1)

                score(0)
                score(1)
                for h in range(p["heads"]):
                    c = p["base"] + h
                    PR, PT = p["p"][h % 2], p["pt"][h % 2]
                    filler(h)
                    pe.wait_ge(g["at_prob"], c + 1)
                    if h:
                        pe.wait_ge(g["at_pt"], c)
                    for j in range(3):
                        last = nc.tensor.transpose(bank[6][:, j * P:(j + 1) * P], PR[:, j * P:(j + 1) * P], ident[:, :])
                    last.then_inc(g["at_turned"], 1)
                    if h + 2 < p["heads"]:
                        score(h + 2)
                    pe.wait_ge(g["at_pt"], c + 1)
                    if h % 2 == 0 and h:
                        pe.wait_ge(g["at_y"], (p["base"] + h) // 2)
                    dst = bank[7][64 * (h % 2):64 * (h % 2) + 64, 0:T]
                    mm(dst, p["v"](0, h), PT[:, 0:T], start=True, stop=False)
                    mm(dst[:, P:T], p["v"](1, h), PT[:, T:3 * P], start=False, stop=True).then_inc(g["at_mixed"], 1)

            def head_sums(s, src, done, mean):
                if s >= 4:
                    pe.wait_ge(g[mean], s - 3)
                mm(bank[4 + s % 4][:, :], halves[:, :], src[:, s * 512:(s + 1) * 512], start=True, stop=True).then_inc(g[done], 1)

            experts(0)

            norm(G_OD)
            pe.wait_ge(g["h_ready"], KC * 3)
            pe.wait_ge(g["od_tables_loaded"], 32)
            features(bank[5][:, 0:T], o_fz, hv).then_inc(g["od_z_ready"], 1)
            unit_loop(2, hv)
            for j in range(4):
                one_unit(tokens, hv)
                if j == 0:
                    pe.wait_ge(g["od_z_in"], 1)
                for s in (2 * j, 2 * j + 1):
                    pe.wait_ge(g["od_sq"], s + 1)
                    head_sums(s, o_sq, "od_sum", "od_mean")
            pe.wait_ge(g["od_qk_ready"], 8)
            pe.wait_ge(g["od_bias_ready"], 1)
            pe.wait_ge(g["units_out"], u[0])
            attention(odd_att, lambda h: None)
            pe.wait_ge(g["at_y"], 8)
            add_to_stream(b3(o_y, KC))

            experts(1)

            norm(G_MIX2)
            pe.wait_ge(g["h_ready"], KC * 5)
            for s in range(3):
                one_unit(features, hv)
            one_unit(tokens, hv, 1)
            for s in range(2):
                one_unit(tokens, hv)
            for s in range(2):
                one_unit(features, hv)
            for s in range(3):
                pe.wait_ge(g["sb_sq"], s + 1)
                head_sums(s, s_sq, "sb_sum", "sb_mean")
            pe.wait_ge(g["sgu_v_ready"], 2)
            pe.wait_ge(g["sgu_w_ready"], 1)
            pe.wait_ge(g["sb_qk_ready"], 3)
            for gr in range(SG):
                for b in range(TB):
                    c = gr // 2
                    last = mm(bank[6 + c // 2][64 * (gr % 2):64 * (gr % 2) + 64, ((c % 2) * TB + b) * P:((c % 2) * TB + b + 1) * P],
                              s_vn[:, b * 512 + gr * SGD:b * 512 + (gr + 1) * SGD], s_ws[:, gr * P:(gr + 1) * P],
                              start=True, stop=True)
            last.then_inc(g["sgu_mixed"], 1)
            pe.wait_ge(g["sgu_y"], 1)
            attention(swa_att, lambda h: one_unit(features, hv))
            pe.wait_ge(g["at_y"], 8 + 4)
            pe.wait_ge(g["units_out"], u[0])
            ya, yb = b3(s_ya, 4), b3(s_yb, 4)
            for c in range(KC):
                if c >= 4:
                    pe.wait_ge(g["merged_out"], c - 3)
                w = weights(0, 0)
                for half, y in enumerate((ya, yb)):
                    for k in range(4):
                        last = mm(bank[c % 4][:, half * T:(half + 1) * T], w[:, (half * 4 + k) * P:(half * 4 + k + 1) * P],
                                  y[:, k, :], start=(k == 0), stop=(k == 3))
                last.then_inc(g["pieces_used"], 1)
                n[0] += 1
            pe.wait_ge(g["merged"], KC)
            add_to_stream(b3(s_m, KC))

            norm(G_FFN2)
            pe.wait_ge(g["h_ready"], KC * 6)
            unit_loop(FC // 4, hv)
            for q in range(FC % 4):
                one_unit(features, hv)
            pe.wait_ge(g["x_ready"], 20)
            pe.wait_ge(g["norm_mean"], 6)
            clear_banks()
            pe.wait_ge(g["ff_gated"], 4 + FC)
            accumulate(FC, lambda i, j: f_act[:, bass.ds(i * 8 * T + j * T, T)])


def columns(w, order=None):
    w = np.asarray(w)
    n = w.shape[1] // P
    p = w.reshape(w.shape[0] // P, P, n, P).transpose(2, 1, 0, 3).reshape(n, P, -1)
    return p if order is None else p[order]


def chunked(v):
    return np.asarray(v).reshape(-1, P).T


def layout(i):
    o = {}
    o["x"] = np.asarray(i["x"])[0].T.reshape(KC, P, T).transpose(1, 0, 2).reshape(P, KC * T)
    o["gains"] = np.concatenate([chunked(v) for v in (i["ev_norm_mix"][0], i["ffn_norm"][0], i["od_norm_mix"][0],
                                                      i["ffn_norm"][1], i["mix_norm_2"][0], i["ffn_norm_2"][0])], 1)
    w = np.asarray(i["ev_w_in"])[0]
    val, gate, q, k, v, r = 0, 512, 1024, 1280, 1536, 2048
    o["ev_in"] = np.concatenate([columns(w[:, val:v]), columns(w[:, r:r + 512]), columns(w[:, v:r])])
    o["w_rank"] = w[:, 2560:].reshape(KC, P, RANK).transpose(1, 0, 2).reshape(P, KC * RANK)
    o["w_gate2"] = np.asarray(i["ev_gate_w2"])[0]
    o["ev_small"] = np.concatenate(
        [np.asarray(i["ev_conv_w"])[0].reshape(CONV_W, CC, P).transpose(2, 0, 1).reshape(P, -1),
         chunked(i["ev_conv_b"][0]), chunked(i["ev_conv_ln_g"][0]), chunked(i["ev_conv_ln_b"][0]),
         chunked(i["ev_gate_b"][0]), chunked(i["ev_gla_norm_g"][0])], 1)
    o["ev_out"] = columns(i["ev_w_out"][0])
    for l in range(2):
        o[f"wq{l}"] = columns(i["peer_wq"][l])
        o[f"keys{l}"] = np.asarray(i["peer_keys"])[l].transpose(3, 0, 1, 2).reshape(P, 16 * NK)
        o[f"u{l}"] = np.asarray(i["peer_u"])[l].reshape(NK, NK, KC, P).transpose(0, 3, 2, 1).reshape(NK, P, D)
        o[f"v{l}"] = np.asarray(i["peer_v"])[l].reshape(NK, P, D)
    w = np.asarray(i["od_w_in"])[0]
    o["od_in"] = columns(w[:, :3 * D])
    fz = np.zeros((KC, P, P), w.dtype)
    fb = np.zeros((P, 1), w.dtype)
    for at in (0, 32, 64, 96):
        fz[:, :, at:at + FH] = w[:, 3 * D:].reshape(KC, P, FH)
        fb[at:at + FH, 0] = np.asarray(i["od_fgate_b"])[0]
    o["od_fz"] = fz.transpose(1, 0, 2).reshape(P, KC * P)
    o["od_fb"] = fb
    o["od_out"] = columns(i["od_w_out"][0])
    o["qk_gain"] = np.stack([np.tile(np.asarray(v)[0], 2) for v in
                             (i["od_q_norm_g"], i["od_k_norm_g"], i["q_norm_2"], i["k_norm_2"])], 1)
    o["sinks"] = np.broadcast_to(np.asarray(i["sinks_2"])[0], (P, QH))
    w = np.asarray(i["w_in_2"])[0]
    kk = w[:, 512:640].reshape(D, 2, 1, HD)
    kk = np.broadcast_to(kk, (D, 2, 2, HD)).reshape(D, 256)
    o["sb_in"] = np.concatenate([columns(w[:, 0:512]), columns(kk), columns(w[:, 640:768]), columns(w[:, 1280:1792]),
                                 columns(w[:, 768:1280]), columns(w[:, 1792:])])
    o["sb_ab"] = columns(np.concatenate([np.asarray(i["w_oa_2"])[0], np.asarray(i["w_ob_2"])[0]]))
    o["sb_out"] = columns(i["w_out_2"][0])
    o["sb_ws"] = np.asarray(i["w_s_2"])[0].transpose(2, 0, 1).reshape(P, SG * P)
    o["sb_bs"] = np.repeat(np.asarray(i["b_s_2"])[0], SGD, 0).reshape(4, P, P).transpose(1, 0, 2).reshape(P, 4 * P)
    o["sb_norm"] = np.broadcast_to(np.asarray(i["sgu_norm_2"])[0], (P, 512))
    both = np.arange(2 * FC).reshape(2, FC).T.reshape(-1)
    o["up"] = columns(i["w_up_2"][0], both)
    o["ff_cw"] = np.asarray(i["conv_w_2"])[0].reshape(3, 2 * FC, P)[:, both].transpose(2, 1, 0).reshape(P, -1)
    o["ff_cb"] = np.asarray(i["conv_b_2"])[0].reshape(2 * FC, P)[both].T
    o["down"] = np.asarray(i["w_down_2"])[0].reshape(FC, P, D)
    return {k: np.ascontiguousarray(v) for k, v in o.items()}


def kernel(**inputs):
    import concourse.bacc as _bacc
    from concourse.bass_utils import run_bass_kernel_spmd as _run

    arrays = layout(inputs)
    nc = _bacc.Bacc("TRN2", target_bir_lowering=False, num_devices=1)
    dram = {name: nc.dram_tensor(name + "_dram", v.shape, mybir.dt.from_np(v.dtype), kind="ExternalInput").ap()
            for name, v in arrays.items()}
    out = nc.dram_tensor("out_dram", (P, KC * T), F32, kind="ExternalOutput").ap()
    build(nc, dram, out)
    r = _run(nc, [{name + "_dram": v for name, v in arrays.items()}], core_ids=[0])
    got = r.results[0]["out_dram"]
    return got.reshape(P, KC, T).transpose(2, 1, 0).reshape(1, T, D)
```

```python
from contextlib import ExitStack

import numpy as np

import concourse.bass as bass
from concourse import mybir

F32 = mybir.dt.float32
F32R = mybir.dt.float32r
BF16 = mybir.dt.bfloat16
I32 = mybir.dt.int32
U16 = mybir.dt.uint16
U32 = mybir.dt.uint32
ALU = mybir.AluOpType
ACT = mybir.ActivationFunctionType
AX = mybir.AxisListType

P = 128
T = 256
TB = T // P
D = 1024
KC = D // P
EPS = 1e-6
RING = 3
BODY = 6
GROUP_T = 8
UNITS = 3
PIECE = 1024

CONV_CH, CONV_W = 512, 31
CC = CONV_CH // P
GH, DK, DV, CHUNK, RANK, TAU = 4, 64, 128, 64, 16, 16.0
NCH = T // CHUNK
LEVELS = [32, 16, 8, 4, 2, 1]

FH, HD = 16, 64

PH, NK, TOPK = 8, 128, 16
NEG_BIG = -3.0e38

QH, KVH, GROUP = 8, 2, 4
SG, SGD = 8, 64
D_FF = 2816
FC = D_FF // P
FAR = 1e33

G_EV, G_PEER0, G_OD, G_PEER1, G_MIX2, G_FFN2 = range(6)
NORMS = 6


def build(nc, a, out):
    ctx = ExitStack()
    with ctx:
        def sb(name, shape, dt=F32):
            return ctx.enter_context(nc.sbuf_tensor(name, shape, dt))

        def sem(name):
            return ctx.enter_context(nc.semaphore(name))

        bank = [ctx.enter_context(nc.psum_tensor(f"bank{i}", [P, 512], F32)) for i in range(8)]

        big = sb("big", [P, 128 * T])
        ring = sb("ring", [P, RING, PIECE])
        w_hi = sb("w_hi", [P, RING, PIECE], F32R)
        w_lo = sb("w_lo", [P, RING, PIECE], F32R)
        xT = sb("xT", [P, KC * T])
        x_hi = sb("x_hi", [P, KC * T], F32R)
        x_lo = sb("x_lo", [P, KC * T], F32R)
        sco = sb("sco", [P, TB * 16 * NK])
        ones = sb("ones", [P, P])
        ident = sb("ident", [P, P])
        halves = sb("halves", [P, P])
        iota16 = sb("iota16", [P, P], BF16)
        zeros = sb("zeros", [P, P], BF16)
        gains = sb("gains", [P, NORMS * KC])
        qk_gain = sb("qk_gain", [P, 4])
        sinks = sb("sinks", [P, QH])
        neg_row = sb("neg_row", [P, 2])
        gate_s = sb("gate_s", [P, 2 * PH])
        at = 24576
        top_v = big[:, at:at + 512]
        top_i = big[:, at + 512:at + 768].bitcast(U16)
        top_if = big[:, at + 768:at + 1280]
        cand_v = big[:, at + 1280:at + 1408]
        cand_i = big[:, at + 1408:at + 1536].bitcast(U32)
        rank_u = big[:, at + 1536:at + 1792].bitcast(U32)
        rank_f = big[:, at + 1792:at + 2048]
        slot3 = big[:, at + 2048:at + 2816]
        g_parts = sb("g_parts", [P, 3 * T], BF16)
        g_part = [g_parts[:, j * T:(j + 1) * T] for j in range(3)]
        sco16 = sco[:, :].bitcast(BF16)
        hot2 = [sco16[:, b * GROUP_T * NK:(b + 1) * GROUP_T * NK] for b in range(3)]
        hot1 = [[sco16[:, 3 * GROUP_T * NK + (3 * b + p) * GROUP_T * NK // 2:3 * GROUP_T * NK + (3 * b + p + 1) * GROUP_T * NK // 2]
                 for p in range(3)] for b in range(3)]
        e1T, e2T = (sco16[:, j * T:(j + 1) * T] for j in (30, 31))
        nsink = gate_s[:, 0:QH]

        cursor = [0]

        def carve(n, size=1):
            at = cursor[0]
            cursor[0] += n
            assert cursor[0] <= 27904, cursor
            return big[:, at:at + n]

        ms, rt, rr = (big[:, 27904 + i * T:27904 + (i + 1) * T] for i in range(3))
        sq = big[:, 28672:28672 + KC * T]
        keysb = big[:, 30720:30720 + 16 * NK]
        qT = big[:, 0:16 * T]

        def b3(ap, n):
            return ap.rearrange("p (a b) -> p a b", a=n)

        xv, sqv = b3(xT[:, :], KC), b3(sq, KC)
        h32 = sq

        cursor[0] = 0
        ev_small = carve(4 * CONV_W + 4 * 3 + 2 + 2)
        o = 4 * CONV_W
        cw, cb, lng, lnb = ev_small[:, 0:o], ev_small[:, o:o + 4], ev_small[:, o + 4:o + 8], ev_small[:, o + 8:o + 12]
        gb, glag = ev_small[:, o + 12:o + 14], ev_small[:, o + 14:o + 15]
        w_gate2 = carve(GH * DK)
        e_val, e_sig = carve(CC * T), carve(CC * T)
        UW = T + CONV_W - 1
        e_u = carve(CC * UW)
        e_conv, e_xc = carve(CC * T), carve(CC * T)
        e_sq2, e_xn = e_sig, e_val
        e_q, e_k, e_r = carve(2 * T), carve(2 * T), carve(4 * T)
        e_v = carve(TB * GH * DV)
        e_glr = carve(T)
        at_zb = cursor[0]
        e_zb, e_az, e_mn, e_ln, e_la, e_b, e_eb, e_nd, e_kd, e_qb = (carve(2 * T) for _ in range(10))
        e_reset = carve(T)
        e_dif = [carve(2 * T) for _ in range(2)]
        e_exp = [carve(2 * T) for _ in range(2)]
        e_qe = [carve(2 * T) for _ in range(2)]
        e_ke = [carve(2 * T) for _ in range(2)]
        e_at = carve(2 * 2 * TB * P)
        e_kdt = carve(TB * 2 * P)
        e_state = carve(3 * 2 * DV)
        e_o, e_osq, e_orr = carve(4 * T), carve(4 * T), carve(4 * T)
        e_y = carve(KC * T)
        e_mask = carve(7 * P).bitcast(I32)
        e_si, e_ti, e_xr = carve(P).bitcast(I32), carve(P).bitcast(I32), carve(2 * P).bitcast(I32)
        e_mu = big[:, at_zb:at_zb + 3 * T]

        cursor[0] = 0
        o_fb = carve(4)
        o_qk, o_sq = carve(16 * T), carve(16 * T)
        o_n = o_sq
        o_v = carve(TB * D)
        o_left, o_right = carve(FH * T), carve(FH * T)
        o_z = [carve(T) for _ in range(6)]
        causal = carve(3 * P)
        at_s = [carve(3 * P) for _ in range(2)]
        at_p = [carve(3 * P) for _ in range(2)]
        at_pt = [carve(3 * P) for _ in range(2)]
        at_small = carve(2 * 8)
        o_tmp = carve(3 * 512)
        o_y = carve(KC * T)

        cursor[0] = 0
        s_ws = carve(SG * P)
        s_bs = carve(4 * P)
        s_norm = carve(512)
        f_cw = carve(2 * FC * 3)
        f_cb = carve(2 * FC)
        s_qk, s_sq, s_n = carve(6 * T), carve(6 * T), carve(6 * T)
        s_v = carve(TB * P)
        s_u = carve(4 * T)
        s_gv, s_gv2, s_vn = carve(TB * 512), carve(TB * 512), carve(TB * 512)
        s_small = carve(8)
        s_gate = carve(16 * T)
        s_mix = carve(4 * T)
        at_y = cursor[0]
        s_ya, s_yb = carve(4 * T), carve(4 * T)
        s_prod = carve(2 * 2 * T)
        s_m = carve(KC * T)
        f_act = None
        assert cursor[0] <= 24000, cursor
        cursor[0] = max(cursor[0], 0)
        dist = carve(3 * P)
        s_at_s = [carve(3 * P) for _ in range(2)]
        s_at_p = [carve(3 * P) for _ in range(2)]
        s_at_pt = [carve(3 * P) for _ in range(2)]
        s_at_small = carve(2 * 8)
        s_tmp = carve(3 * 512)
        ZW = T + 2
        f_at = 2688
        f_z = [big[:, f_at + i * 2 * ZW:f_at + (i + 1) * 2 * ZW] for i in range(3)]
        f_at += 3 * 2 * ZW
        f_zc = [big[:, f_at + i * 2 * T:f_at + (i + 1) * 2 * T] for i in range(3)]
        f_at += 3 * 2 * T
        f_sil = [big[:, f_at + i * T:f_at + (i + 1) * T] for i in range(3)]
        f_at += 3 * T
        f_act = big[:, f_at:f_at + FC * T]
        assert f_at + FC * T <= 27904

        names = """x_loaded ev_tables_loaded tables_loaded keys_loaded od_tables_loaded sb_tables_loaded stored
            consts masks_built
            pieces_used units_out w_hi_done lo_pool lo_dve x_hi_done x_lo_done ax_hi ax_lo
            norm_squared norm_summed norm_mean norm_root h_ready x_ready
            key_scored scores_out ranked gate_shifted gate_exped slots_ready slots_turned turned
            matched first_hot second_hot gates_spread gated pool_waits pool_step dve_step act_step
            ev_rank_ready ev_rank_out ev_z_ready ev_z_in ev_z_log ev_decay_part ev_fade ev_fade_in
            ev_expb ev_expk ev_dif ev_difexp ev_qk_level ev_level ev_level_in ev_kdec ev_kdec_turned ev_kdt
            ev_chunk_sums ev_states ev_o ev_o_out ev_o_sq ev_o_sum ev_o_mean ev_o_root ev_y
            conv_step conv_done ln_sum ln_centred ln_sq ln_var ln_mean ln_root ln_normed ev_ya ev_u_in
            od_z_ready od_z_in od_z_log od_bias_ready od_sq od_sum od_mean od_root od_qk_ready od_sel
            at_score at_masked at_exped at_prob at_turned at_pt at_mixed at_y
            sb_sq sb_sum sb_mean sb_root sb_qk_ready sgu_sq sgu_mean sgu_root sgu_v_ready sgu_w_ready
            sgu_mixed sgu_y merge_ready merged_out merged ff_silu ff_z ff_gated ff_tap""".split()
        g = {n: sem(n) for n in names}
        slot_loaded = [sem(f"slot_loaded{i}") for i in range(RING)]

        POOL, DVE = range(2)
        HALF = NK // 2
        RUNS = [("ev_in", "ev_in", 21, POOL), ("ev_out", "ev_out", 8, POOL),
                ("wq0", "wq0", 16, POOL), ("u0", "u0", HALF, POOL), ("u0b", "u0", HALF, DVE),
                ("v0", "v0", HALF, DVE), ("v0b", "v0", HALF, DVE),
                ("od_in", "od_in", 25, POOL), ("od_out", "od_out", 8, POOL),
                ("wq1", "wq1", 16, POOL), ("u1", "u1", HALF, POOL), ("u1b", "u1", HALF, DVE),
                ("v1", "v1", HALF, DVE), ("v1b", "v1", HALF, DVE),
                ("sb_in", "sb_in", 31, POOL), ("sb_ab", "sb_ab", 8, POOL), ("sb_out", "sb_out", 8, POOL),
                ("up", "up", 2 * FC, POOL), ("down", "down", FC, DVE)]
        starts, by_dve = {}, []
        for name, _, count, who in RUNS:
            starts[name] = len(by_dve)
            by_dve += [who == DVE] * count
        total_pieces = len(by_dve)

        def low_bits(k, i=0):
            so_far = by_dve[:k + 1].count(by_dve[k])
            return g["lo_dve" if by_dve[k] else "lo_pool"], i * BODY + so_far


        def unit_bank(u):
            return bank[u % UNITS]

        odd_att = dict(heads=FH, tag=0, s=at_s, p=at_p, pt=at_pt, small=at_small, y=b3(o_y, KC),
                       q=lambda h: (b3(o_n, 16), h // 2), k=lambda h: (b3(o_n, 16), 8 + h // 2),
                       v=lambda tb, h: o_v[:, tb * D + h * HD:tb * D + h * HD + HD],
                       table=causal, factor=lambda h: 1.0, base=0)
        swa_att = dict(heads=QH, tag=1, s=s_at_s, p=s_at_p, pt=s_at_pt, small=s_at_small, y=b3(s_ya, 4),
                       q=lambda h: (b3(s_n, 6), h // 2), k=lambda h: (b3(s_n, 6), 4 + h // GROUP),
                       v=lambda tb, h: s_v[:, tb * P + (h // GROUP) * HD:tb * P + (h // GROUP) * HD + HD],
                       table=dist, factor=lambda h: -(2.0 ** (-8.0 * (h + 1.0) / QH)), base=FH)

        block = ctx.enter_context(nc.Block())

        @block.sync
        def _(sp):
            def load(src, k):
                sp.dma_start(ring[:, k % RING, :], src).then_inc(slot_loaded[k % RING], 16)

            def stream(name, array, count):
                k0, at = starts[name], 0
                while (array, at) in loaded:
                    at += 1
                loaded.update((array, at + j) for j in range(count))
                done = 0
                while done < min(RING, count):
                    if k0 + done >= RING:
                        sp.wait_ge(*low_bits(k0 + done - RING))
                    load(a[array][at + done], k0 + done)
                    done += 1
                loops = (count - done) // BODY
                if loops:
                    with sp.Fori(0, loops) as i:
                        for j in range(BODY):
                            sp.wait_ge(*low_bits(k0 + j, i))
                            load(a[array][bass.ds(i * BODY + (at + done + j), 1)].rearrange("o p n -> (o p) n"), k0 + done + j)
                    done += BODY * loops
                for j in range(done, count):
                    sp.wait_ge(*low_bits(k0 + j - RING))
                    load(a[array][at + j], k0 + j)

            loaded = set()
            sp.dma_start(xT[:, :], a["x"]).then_inc(g["x_loaded"], 16)
            sp.dma_start(gains[:, :], a["gains"]).then_inc(g["tables_loaded"], 16)
            for name, array, count, _ in RUNS:
                stream(name, array, count)
            for j in range(4):
                sp.wait_ge(g["x_ready"], 4 * 5 + j + 1)
                sp.dma_start(out[:, j * 512:(j + 1) * 512], xT[:, j * 512:(j + 1) * 512]).then_inc(g["stored"], 16)
            sp.wait_ge(g["stored"], 64)

        @block.gpsimd
        def _(pool):
            steps = [0]

            def step(ins):
                steps[0] += 1
                ins.then_inc(g["pool_step"], 1)

            def settle():
                pool.wait_ge(g["pool_step"], steps[0])

            step(pool.memset(zeros[:, :], 0.0))
            step(pool.memset(ones[:, :], 1.0))
            step(pool.memset(ident[:, :], 0.0))
            step(pool.memset(halves[:, :], 0.0))
            step(pool.iota(sco[:, 0:P], [[1, P]], base=0, channel_multiplier=0, allow_small_or_imprecise_dtypes=True))
            step(pool.iota(e_si, [[0, P]], base=0, channel_multiplier=1))
            step(pool.iota(e_ti, [[1, P]], base=0, channel_multiplier=0))
            step(pool.memset(e_reset, 1.0))
            step(pool.memset(e_u, 0.0))
            step(pool.memset(e_at, 0.0))
            settle()
            step(pool.tensor_copy(iota16[:, :], sco[:, 0:P]))
            step(pool.affine_select(out=ident[:, :], in_=ident[:, :], compare_op=ALU.not_equal, fill=1.0,
                                    base=0, pattern=[[-1, P]], channel_multiplier=1))
            step(pool.memset(halves[0:64, 0:64], 1.0))
            settle()
            step(pool.memset(halves[64:128, 64:128], 1.0))
            settle()
            step(pool.memset(b3(e_reset, NCH)[:, :, 0:1], 0.0))
            settle()
            pool.memset(neg_row[:, :], 0.0).then_inc(g["consts"], 1)

            def low(k, i=0, w=0):
                pool.wait_ge(g["w_hi_done"], i * BODY + (k + 1))
                pool.tensor_tensor(w_lo[:, k % RING, :], ring[:, k % RING, :], w_hi[:, k % RING, :].bitcast(F32),
                                   ALU.subtract).then_inc(g["lo_pool"], 1)

            def scale(layer, m, i=0):
                count, t0 = 2 * (T // GROUP_T) * layer + m, i * (3 * GROUP_T) + (m % (T // GROUP_T)) * GROUP_T
                parts = [b3(x, GROUP_T) for x in hot1[count % 3]]
                pool.wait_ge(g["matched"], i * 3 + (count + 1))
                for p in range(3):
                    of_token = g_part[p][:, bass.ds(t0, GROUP_T)].rearrange("p (t o) -> p t o", o=1)
                    last = pool.tensor_tensor(parts[p], parts[2], of_token.to_broadcast([P, GROUP_T, HALF]), ALU.mult)
                last.then_inc(g["first_hot"], 1)

            def lows(name, first, end):
                k0 = starts[name] + first
                loops = (end - first) // BODY
                if loops > 1:
                    with pool.Fori(0, loops) as i:
                        for j in range(BODY):
                            low(k0 + j, i)
                else:
                    loops = 0
                for j in range(BODY * loops, end - first):
                    low(k0 + j)

            lows("ev_in", 0, 21)
            lows("ev_out", 0, 8)
            for layer in range(2):
                lows(f"wq{layer}", 0, 16)
                lows(f"u{layer}", 0, HALF)
                groups = T // GROUP_T
                pool.wait_ge(g["turned"], 3 * (layer + 1))
                for half in range(2):
                    scale(layer, groups * half)
                    scale(layer, groups * half + 1)
                    with pool.Fori(0, groups // 3) as i:
                        for q in range(3):
                            scale(layer, groups * half + q + 2, i)

                if layer == 0:
                    lows("od_in", 0, 16)
                    pool.wait_ge(g["x_ready"], 4 * 2)
                    for tab in (o_left, o_right):
                        step(pool.memset(tab, 0.0))
                    step(pool.memset(causal, 0.0))
                    settle()
                    for tab, rows in ((o_left, 0), (o_left, 64), (o_right, 32), (o_right, 96)):
                        v = tab.rearrange("p (h t) -> p h t", h=FH)[rows:rows + 32]
                        step(pool.affine_select(out=v, in_=v, compare_op=ALU.not_equal, fill=1.0, base=0,
                                                pattern=[[-1, FH], [0, T]], channel_multiplier=1))
                        settle()
                    for c in (0, 2):
                        v = causal[:, c * P:(c + 1) * P]
                        step(pool.affine_select(out=v, in_=v, compare_op=ALU.is_ge, fill=-1e30, base=0,
                                                pattern=[[-1, P]], channel_multiplier=1))
                    settle()
                    pool.memset(neg_row[:, :], 0.0).then_inc(g["od_sel"], 1)
                    lows("od_in", 16, 25)
                    lows("od_out", 0, 8)
                else:
                    lows("sb_in", 0, 11)
                    pool.wait_ge(g["x_ready"], 4 * 4)
                    for c, base in ((0, 0), (1, P), (2, 0)):
                        step(pool.iota(dist[:, c * P:(c + 1) * P], [[-1, P]], base=base, channel_multiplier=1,
                                       allow_small_or_imprecise_dtypes=True))
                    settle()
                    for c in (0, 2):
                        v = dist[:, c * P:(c + 1) * P]
                        step(pool.affine_select(out=v, in_=v, compare_op=ALU.is_ge, fill=FAR, base=0,
                                                pattern=[[-1, P]], channel_multiplier=1))
                    v = dist[:, P:2 * P]
                    step(pool.affine_select(out=v, in_=v, compare_op=ALU.is_gt, fill=FAR, base=0,
                                            pattern=[[1, P]], channel_multiplier=-1))
                    pool.wait_ge(g["sb_tables_loaded"], 16 * 5)
                    v = s_ws.rearrange("p (g i) -> p g i", g=SG)
                    step(pool.affine_select(out=v, in_=v, compare_op=ALU.is_ge, fill=0.0, base=0,
                                            pattern=[[0, SG], [1, P]], channel_multiplier=-1))
                    settle()
                    pool.memset(neg_row[:, :], 0.0).then_inc(g["sgu_w_ready"], 1)
                    lows("sb_in", 11, 31)
                    lows("sb_ab", 0, 8)
                    lows("sb_out", 0, 8)
                    lows("up", 0, 2 * FC)

        @block.scalar
        def _(act):
            n, u = [0], [0]
            nh, xh = [0], [0]
            A = nc.scalar.activation

            def high(k, i=0):
                act.wait_ge(slot_loaded[k % RING], i * (16 * BODY // RING) + 16 * (k // RING + 1))
                if k >= RING:
                    act.wait_ge(g["pieces_used"], i * BODY + (k - RING + 1))
                A(w_hi[:, k % RING, :], ring[:, k % RING, :], ACT.Copy).then_inc(g["w_hi_done"], 1)

            def highs(to):
                while nh[0] < min(to, total_pieces):
                    high(nh[0])
                    nh[0] += 1

            def split(src, ready):
                if n[0]:
                    act.wait_ge(g["pieces_used"], n[0])
                for j in range(4):
                    ready(j)
                    A(x_hi[:, j * 512:(j + 1) * 512], src[:, j * 512:(j + 1) * 512], ACT.Copy).then_inc(g["x_hi_done"], 1)

            def norm(k):
                for j in range(4):
                    if k == 0:
                        if j == 0:
                            act.wait_ge(g["x_loaded"], 16)
                    else:
                        act.wait_ge(g["x_ready"], 4 * (k - 1) + j + 1)
                    A(sq[:, j * 512:(j + 1) * 512], xT[:, j * 512:(j + 1) * 512], ACT.Square).then_inc(g["norm_squared"], 1)
                act.wait_ge(g["norm_mean"], k + 1)
                A(rt, ms, ACT.Sqrt).then_inc(g["norm_root"], 1)
                split(h32, lambda j: act.wait_ge(g["h_ready"], KC * k + 2 * j + 2))

            def unit(outs, func=ACT.Copy, pieces=2, scale=1.0, view=None):
                n[0] += pieces
                highs(n[0] + 2)
                act.wait_ge(g["pieces_used"], n[0])
                src = unit_bank(u[0])[:, 0:pieces * T]
                if view:
                    src = view(src)
                A(outs, src, func, scale=scale).then_inc(g["units_out"], 1)
                u[0] += 1

            def token_major(dst, width, piece, pieces):
                v = dst.rearrange("p (b n) -> p b n", b=TB)[:, :, piece * P:(piece + pieces) * P]
                return v.rearrange("p b (a n) -> p a b n", a=pieces)

            def tm_view(pieces):
                return lambda s: s.rearrange("p (a b n) -> p a b n", a=pieces, b=TB)

            def unit_loop(units, dst_of, func=ACT.Copy):
                loops = units // UNITS
                highs(n[0] + 2)
                if loops:
                    with act.Fori(0, loops) as i:
                        for q in range(UNITS):
                            for j in range(2):
                                high(n[0] + 2 * q + 2 + j, i)
                            act.wait_ge(g["pieces_used"], i * BODY + (n[0] + 2 * q + 2))
                            A(dst_of(i, q), unit_bank(u[0] + q)[:, :], func).then_inc(g["units_out"], 1)
                n[0] += BODY * loops
                nh[0] += BODY * loops
                u[0] += UNITS * loops
                for q in range(units % UNITS):
                    unit(dst_of(loops, q), func)

            def others(pieces):
                n[0] += pieces
                highs(n[0] + 2)

            def accumulated(count, src, ready, first=True):
                if first:
                    act.wait_ge(g["pieces_used"], n[0])
                ready()

                def chunk(k, i=0):
                    A(x_hi[:, ((n[0] + k) % RING) * T:((n[0] + k) % RING + 1) * T], src(k, i), ACT.Copy).then_inc(g["ax_hi"], 1)

                for k in range(RING):
                    highs(n[0] + k + 1)
                    chunk(k)
                loops = (count - RING) // BODY
                with act.Fori(0, loops) as i:
                    for j in range(BODY):
                        high(n[0] + RING + j, i)
                        chunk(RING + j, i)
                nh[0] += BODY * loops
                for k in range(RING + BODY * loops, count):
                    highs(n[0] + k + 1)
                    chunk(k)
                n[0] += count
                highs(n[0] + 2)

            act.dma_start(ev_small[:, 0:139], a["ev_small"]).then_inc(g["ev_tables_loaded"], 16)
            act.dma_start(w_gate2[0:RANK, :], a["w_gate2"]).then_inc(g["ev_tables_loaded"], 16)
            act.dma_start(qk_gain[:, :], a["qk_gain"]).then_inc(g["tables_loaded"], 16)
            act.dma_start(sinks[:, :], a["sinks"]).then_inc(g["tables_loaded"], 16)
            act.dma_start(keysb, a["keys0"]).then_inc(g["keys_loaded"], 16)

            highs(2)
            norm(G_EV)
            for j in range(2):
                unit(e_val[:, j * 512:(j + 1) * 512])
            for j in range(2):
                unit(e_sig[:, j * 512:(j + 1) * 512], ACT.Sigmoid)
            unit(e_q, scale=DK ** -0.5)
            unit(e_k)
            for j in range(2):
                unit(e_r[:, j * 512:(j + 1) * 512], ACT.Silu)
            unit(e_glr[:, :], pieces=1)
            for j in range(2):
                unit(token_major(e_v, 512, 2 * j, 2), view=tm_view(2))
            act.wait_ge(g["ev_z_in"], 2)
            A(e_az, e_zb, ACT.Abs).then_inc(g["act_step"], 1)
            act.wait_ge(g["act_step"], 1)
            A(e_az, e_az, ACT.Exp, scale=-1.0).then_inc(g["act_step"], 1)
            act.wait_ge(g["act_step"], 2)
            A(e_ln, e_az, ACT.Ln, bias=1.0).then_inc(g["ev_z_log"], 1)
            act.wait_ge(g["ev_decay_part"], 2)
            A(e_eb, e_b, ACT.Exp).then_inc(g["ev_expb"], 1)
            act.wait_ge(g["ev_fade"], 1)
            A(e_kd, e_nd, ACT.Exp).then_inc(g["ev_expk"], 1)
            for lv in range(6):
                act.wait_ge(g["ev_dif"], 2 * lv + 2)
                if lv >= 2:
                    act.wait_ge(g["ev_qk_level"], 2 * (lv - 1))
                A(e_exp[lv % 2], e_dif[lv % 2], ACT.Exp).then_inc(g["ev_difexp"], 1)
            act.wait_ge(g["ev_kdec_turned"], 1)
            A(e_kdt, bank[0][:, :], ACT.Copy).then_inc(g["ev_kdt"], 1)
            act.wait_ge(g["ln_centred"], 4)
            A(e_sq2, e_xc, ACT.Square).then_inc(g["ln_sq"], 1)
            act.wait_ge(g["ev_o_out"], 2)
            A(e_osq, e_o, ACT.Square).then_inc(g["ev_o_sq"], 1)
            act.wait_ge(g["ln_mean"], 1)
            A(e_mu[:, T:2 * T], e_mu[:, 0:T], ACT.Sqrt).then_inc(g["ln_root"], 1)
            act.wait_ge(g["ev_o_mean"], 2)
            A(e_orr, e_osq, ACT.Sqrt).then_inc(g["ev_o_root"], 1)
            act.wait_ge(g["ln_normed"], 1)
            for c in range(CC):
                A(e_y[:, c * T:(c + 1) * T], e_xn[:, c * T:(c + 1) * T], ACT.Silu, bias=lnb[:, c:c + 1],
                  scale=lng[:, c:c + 1]).then_inc(g["ev_ya"], 1)
            split(e_y, lambda j: act.wait_ge(g["ev_ya"] if j < 2 else g["ev_y"], 2 * j + 2 if j < 2 else 2))
            others(8)

            def experts(layer):
                norm(1 + 2 * layer)
                unit_loop(8, lambda i, q: big[:, bass.ds(i * 1536 + q * 512, 512)])
                for s in range(8):
                    act.wait_ge(g["key_scored"], 8 * layer + s + 1)
                    A(sco[:, s * 512:(s + 1) * 512], bank[4 + s % 4][:, :], ACT.Copy).then_inc(g["scores_out"], 1)
                unit_loop(24, lambda i, q: big[:, bass.ds(i * 1536 + q * 512, 512)], ACT.Gelu)
                for tb in range(TB):
                    act.wait_ge(g["gate_shifted"], TB * layer + tb + 1)
                    v = slot3[:, (2 * TB + tb) * P:(2 * TB + tb + 1) * P]
                    A(v, v, ACT.Exp).then_inc(g["gate_exped"], 1)
                unit_loop(40, lambda i, q: big[:, bass.ds(i * 1536 + (24 * 512 + q * 512), 512)], ACT.Gelu)
                for half in range(2):
                    accumulated(HALF, lambda k, i: big[:, bass.ds(i * BODY * T + (HALF * half + k) * T, T)],
                                lambda: act.wait_ge(g["gated"], 64 * layer + 32 * (half + 1)), half == 0)

            def attention(p, filler):
                for h in range(p["heads"]):
                    c = p["base"] + h
                    S, PR, PT, sm = p["s"][h % 2], p["p"][h % 2], p["pt"][h % 2], p["small"][:, (h % 2) * 8:(h % 2) * 8 + 8]
                    act.wait_ge(g["at_masked"], c + 1)
                    A(PR[:, 0:P], S[:, 0:P], ACT.Exp, bias=sm[:, 0:1], accum_out=sm[:, 2:3])
                    last = A(PR[:, P:3 * P], S[:, P:3 * P], ACT.Exp, bias=sm[:, 1:2], accum_out=sm[:, 3:4])
                    if p["tag"]:
                        last = A(sm[:, 4:6], sm[:, 0:2], ACT.Exp, bias=sinks[:, h:h + 1])
                    last.then_inc(g["at_exped"], 1)
                    filler(h)
                    act.wait_ge(g["at_turned"], c + 1)
                    if h >= 2:
                        act.wait_ge(g["at_mixed"], c - 1)
                    A(PT, bank[6][:, 0:3 * P], ACT.Copy).then_inc(g["at_pt"], 1)
                    if h % 2:
                        act.wait_ge(g["at_mixed"], c + 1)
                        A(p["y"][:, h // 2, :], bank[7][:, 0:T], ACT.Copy).then_inc(g["at_y"], 1)

            experts(0)

            act.wait_ge(g["x_ready"], 4 * 2)
            act.dma_start(o_fb[:, 0:1], a["od_fb"]).then_inc(g["od_tables_loaded"], 16)
            act.dma_start(keysb, a["keys1"]).then_inc(g["keys_loaded"], 16)
            norm(G_OD)
            unit_loop(8, lambda i, q: o_qk[:, bass.ds(i * 1536 + q * 512, 512)])
            unit(o_z[0], pieces=1)
            act.wait_ge(g["od_z_in"], 1)
            A(o_z[1], o_z[0], ACT.Abs).then_inc(g["act_step"], 1)
            act.wait_ge(g["act_step"], 3)
            A(o_z[1], o_z[1], ACT.Exp, scale=-1.0).then_inc(g["act_step"], 1)
            act.wait_ge(g["act_step"], 4)
            A(o_z[2], o_z[1], ACT.Ln, bias=1.0).then_inc(g["od_z_log"], 1)
            act.wait_ge(g["units_out"], u[0])
            for s in range(8):
                A(o_sq[:, s * 512:(s + 1) * 512], o_qk[:, s * 512:(s + 1) * 512], ACT.Square).then_inc(g["od_sq"], 1)
            for j in range(4):
                unit(token_major(o_v, D, 2 * j, 2), view=tm_view(2))
                for s in (2 * j, 2 * j + 1):
                    act.wait_ge(g["od_mean"], s + 1)
                    v = o_tmp[:, (s % 3) * 512:(s % 3 + 1) * 512]
                    A(v, v, ACT.Sqrt).then_inc(g["od_root"], 1)
            attention(odd_att, lambda h: None)
            act.wait_ge(g["at_y"], 8)
            split(o_y, lambda j: None)
            others(8)

            experts(1)

            act.wait_ge(g["x_ready"], 4 * 4)
            act.dma_start(s_ws, a["sb_ws"]).then_inc(g["sb_tables_loaded"], 16)
            act.dma_start(s_bs, a["sb_bs"]).then_inc(g["sb_tables_loaded"], 16)
            act.dma_start(s_norm, a["sb_norm"]).then_inc(g["sb_tables_loaded"], 16)
            act.dma_start(f_cw, a["ff_cw"]).then_inc(g["sb_tables_loaded"], 16)
            act.dma_start(f_cb, a["ff_cb"]).then_inc(g["sb_tables_loaded"], 16)
            norm(G_MIX2)
            for s in range(3):
                unit(s_qk[:, s * 512:(s + 1) * 512])
            unit(token_major(s_v, P, 0, 1), pieces=1, view=tm_view(1))
            act.wait_ge(g["units_out"], u[0])
            for s in range(3):
                A(s_sq[:, s * 512:(s + 1) * 512], s_qk[:, s * 512:(s + 1) * 512], ACT.Square).then_inc(g["sb_sq"], 1)
            for j in range(2):
                unit(token_major(s_gv, 512, 2 * j, 2), ACT.Gelu_apprx_tanh, view=tm_view(2))
            for j in range(2):
                unit(s_u[:, j * 512:(j + 1) * 512], ACT.Gelu_apprx_tanh)
            for s in range(3):
                act.wait_ge(g["sb_mean"], s + 1)
                v = s_tmp[:, s * 512:(s + 1) * 512]
                A(v, v, ACT.Sqrt).then_inc(g["sb_root"], 1)
            act.wait_ge(g["sgu_mean"], 1)
            A(s_small[:, 4:6], s_small[:, 2:4], ACT.Sqrt).then_inc(g["sgu_root"], 1)
            attention(swa_att, lambda h: unit(s_gate[:, h * 512:(h + 1) * 512], ACT.Sigmoid))
            act.wait_ge(g["at_y"], 8 + 4)
            act.wait_ge(g["sgu_y"], 1)
            split(big[:, at_y:at_y + 8 * T], lambda j: None)
            others(8)
            split(s_m, lambda j: act.wait_ge(g["merged"], 2 * j + 2))
            others(8)

            norm(G_FFN2)

            def z_out(i, q):
                act.wait_ge(g["pieces_used"], i * BODY + (n[0] + 2 * q + 2))
                act.wait_ge(g["ff_gated"], i * UNITS + (q + 1))
                A(b3(f_z[q], 2)[:, :, 2:ZW], b3(unit_bank(u[0] + q)[:, :], 2), ACT.Copy).then_inc(g["units_out"], 1)
                act.wait_ge(g["ff_z"], i * UNITS + (q + 1))
                A(f_sil[q], f_zc[q][:, 0:T], ACT.Silu).then_inc(g["ff_silu"], 1)

            with act.Fori(0, FC // UNITS) as i:
                for q in range(UNITS):
                    for j in range(2):
                        high(n[0] + 2 * q + 2 + j, i)
                    z_out(i, q)
            nh[0] += BODY * (FC // UNITS)
            for q in range(FC % UNITS):
                highs(n[0] + BODY * (FC // UNITS) + 2 * q + 4)
                z_out(FC // UNITS, q)
            n[0] += 2 * FC
            accumulated(FC, lambda k, i: f_act[:, bass.ds(i * BODY * T + k * T, T)],
                        lambda: act.wait_ge(g["ff_gated"], UNITS + FC))

        @block.vector
        def _(dve):
            V = nc.vector
            steps = [0]
            n, u = [0], [0]

            def step(ins):
                steps[0] += 1
                ins.then_inc(g["dve_step"], 1)

            def settle():
                dve.wait_ge(g["dve_step"], steps[0])

            xs, ax = [0], [0]

            def lows_of(src):
                for j in range(4):
                    dve.wait_ge(g["x_hi_done"], 4 * xs[0] + j + 1)
                    c = slice(j * 512, (j + 1) * 512)
                    V.tensor_tensor(x_lo[:, c], src[:, c], x_hi[:, c].bitcast(F32), ALU.subtract).then_inc(g["x_lo_done"], 1)
                xs[0] += 1

            def low(k, i=0):
                dve.wait_ge(g["w_hi_done"], i * BODY + (k + 1))
                V.tensor_tensor(w_lo[:, k % RING, :], ring[:, k % RING, :], w_hi[:, k % RING, :].bitcast(F32),
                                ALU.subtract).then_inc(g["lo_dve"], 1)

            def chunk(k0, k, src, i=0):
                dve.wait_ge(g["ax_hi"], i * BODY + (ax[0] + k + 1))
                c = slice(((k0 + k) % RING) * T, ((k0 + k) % RING + 1) * T)
                V.tensor_tensor(x_lo[:, c], src(k, i), x_hi[:, c].bitcast(F32), ALU.subtract).then_inc(g["ax_lo"], 1)

            def accumulated(name, count, src):
                k0 = starts[name]
                for k in range(RING):
                    low(k0 + k)
                    chunk(k0, k, src)
                loops = (count - RING) // BODY
                with dve.Fori(0, loops) as i:
                    for j in range(BODY):
                        low(k0 + RING + j, i)
                        chunk(k0, RING + j, src, i)
                for k in range(RING + BODY * loops, count):
                    low(k0 + k)
                    chunk(k0, k, src)
                ax[0] += count

            def norm(k):
                dve.wait_ge(g["norm_summed"], k + 1)
                V.tensor_scalar(ms, bank[4][:, 0:T], 1.0 / D, EPS, ALU.mult, ALU.add).then_inc(g["norm_mean"], 1)
                dve.wait_ge(g["norm_root"], k + 1)
                step(V.reciprocal(rr, rt))
                settle()
                for c in range(KC):
                    V.scalar_tensor_tensor(b3(h32, KC)[:, c, :], xv[:, c, :], gains[:, k * KC + c:k * KC + c + 1], rr,
                                           ALU.mult, ALU.mult).then_inc(g["h_ready"], 1)
                lows_of(h32)

            def residual(pieces, each):
                n[0] += pieces
                for j in range(4):
                    dve.wait_ge(g["pieces_used"], n[0] - (6 - 2 * j if each else 0))
                    v = xT[:, j * 512:(j + 1) * 512]
                    V.tensor_tensor(v, bank[4 + j][:, :], v, ALU.add).then_inc(g["x_ready"], 1)

            dve.wait_ge(g["consts"], 1)
            step(V.tensor_tensor(e_xr[:, 0:P], e_si, e_ti, ALU.bitwise_xor))
            settle()
            for lv, m in enumerate(LEVELS):
                sh = m.bit_length() - 1
                step(V.tensor_scalar(e_xr[:, P:2 * P], e_xr[:, 0:P], sh, None, ALU.arith_shift_right))
                settle()
                step(V.tensor_scalar(e_mask[:, 6 * P:7 * P], e_ti, sh, 1, ALU.arith_shift_right, ALU.bitwise_and))
                step(V.tensor_scalar(e_mask[:, lv * P:(lv + 1) * P], e_xr[:, P:2 * P], 1.0, None, ALU.is_equal))
                settle()
                step(V.tensor_tensor(e_mask[:, lv * P:(lv + 1) * P], e_mask[:, lv * P:(lv + 1) * P],
                                     e_mask[:, 6 * P:7 * P], ALU.bitwise_and))
            settle()
            step(V.tensor_scalar(e_mask[:, 6 * P:7 * P], e_xr[:, 0:P], 0.0, None, ALU.is_equal))

            dve.wait_ge(g["tables_loaded"], 48)
            norm(G_EV)
            n[0] += 21
            dve.wait_ge(g["units_out"], 4)
            uv = e_u.rearrange("p (c t) -> p c t", c=CC)
            step(V.tensor_tensor(uv[:, :, CONV_W - 1:UW], b3(e_val, CC), b3(e_sig, CC), ALU.mult))
            settle()
            dve.wait_ge(g["ev_tables_loaded"], 32)
            cv = b3(e_conv, CC)
            for c in range(CC):
                V.tensor_scalar(cv[:, c, :], uv[:, c, 0:T], cw[:, c:c + 1], cb[:, c:c + 1], ALU.mult,
                                ALU.add).then_inc(g["conv_step"], 1)
            with dve.Fori(0, (CONV_W - 1) // 2) as i:
                for w in range(2):
                    for c in range(CC):
                        dve.wait_ge(g["conv_step"], i * 2 * CC + (w * CC + c + 1))
                        V.scalar_tensor_tensor(cv[:, c, :], e_u[:, bass.ds(i * 2 + (c * UW + w + 1), T)],
                                               cw[:, bass.ds(i * 2 * CC + ((w + 1) * CC + c), 1)], cv[:, c, :],
                                               ALU.mult, ALU.add).then_inc(g["conv_step"], 1)
            dve.wait_ge(g["ev_z_ready"], 1)
            for f in range(2):
                V.tensor_scalar(e_zb[:, f * T:(f + 1) * T], bank[5][:, f * T:(f + 1) * T], gb[:, f:f + 1], None,
                                ALU.add).then_inc(g["ev_z_in"], 1)
            dve.wait_ge(g["ev_z_in"], 2)
            step(V.tensor_scalar(e_mn, e_zb, 0.0, 1.0 / TAU, ALU.min, ALU.mult))
            settle()
            dve.wait_ge(g["ev_z_log"], 1)
            step(V.scalar_tensor_tensor(e_la, e_ln, -1.0 / TAU, e_mn, ALU.mult, ALU.add))
            settle()
            for f in range(2):
                V.tensor_tensor_scan(e_b[:, f * T:(f + 1) * T], e_reset, e_la[:, f * T:(f + 1) * T], 0.0,
                                     ALU.mult, ALU.add).then_inc(g["ev_decay_part"], 1)
            dve.wait_ge(g["ev_decay_part"], 2)
            b8 = b3(e_b, 2 * NCH)
            V.tensor_tensor(b3(e_nd, 2 * NCH), b8[:, :, CHUNK - 1:CHUNK].to_broadcast([P, 2 * NCH, CHUNK]), b8,
                            ALU.subtract).then_inc(g["ev_fade"], 1)
            atv = e_at.rearrange("p (r c t) -> p r c t", r=2, t=P)

            def take(lv):
                if lv:
                    dve.wait_ge(g["ev_level_in"], 2 * lv)
                for r in range(2):
                    dve.wait_ge(g["ev_level"], lv + 1)
                    V.copy_predicated(atv[:, r], e_mask[:, lv * P:(lv + 1) * P].rearrange("p (o t) -> p o t", o=1).to_broadcast([P, 4, P]),
                                      b3(bank[4 + 2 * (lv % 2) + r][:, :], 4)).then_inc(g["ev_level_in"], 1)

            for lv, m in enumerate(LEVELS):
                if lv >= 2:
                    dve.wait_ge(g["ev_difexp"], lv - 1)
                bm = e_b.rearrange("p (a m) -> p a m", m=2 * m)
                dm = e_dif[lv % 2].rearrange("p (a m) -> p a m", m=2 * m)
                ref = bm[:, :, m - 1:m].to_broadcast([P, 2 * T // (2 * m), m])
                V.tensor_tensor(dm[:, :, 0:m], ref, bm[:, :, 0:m], ALU.subtract).then_inc(g["ev_dif"], 1)
                V.tensor_tensor(dm[:, :, m:2 * m], bm[:, :, m:2 * m], ref, ALU.subtract).then_inc(g["ev_dif"], 1)
                dve.wait_ge(g["ev_difexp"], lv + 1)
                if lv == 0:
                    dve.wait_ge(g["units_out"], 8)
                if lv >= 2:
                    dve.wait_ge(g["ev_level"], lv - 1)
                V.tensor_tensor(e_qe[lv % 2], e_q, e_exp[lv % 2], ALU.mult).then_inc(g["ev_qk_level"], 1)
                V.tensor_tensor(e_ke[lv % 2], e_k, e_exp[lv % 2], ALU.mult).then_inc(g["ev_qk_level"], 1)
                if lv >= 1:
                    take(lv - 1)
            dve.wait_ge(g["ev_expk"], 1)
            V.tensor_tensor(e_kd, e_k, e_kd, ALU.mult).then_inc(g["ev_kdec"], 1)
            dve.wait_ge(g["ev_expb"], 1)
            V.tensor_tensor(e_qb, e_q, e_eb, ALU.mult).then_inc(g["ev_kdec"], 1)
            take(5)
            take(6)
            dve.wait_ge(g["ev_chunk_sums"], 1)
            st = e_state.rearrange("p (c f n) -> p c f n", c=3, f=2)
            step(V.tensor_copy(st[:, 0], bank[1][:, 0:256].rearrange("p (f n) -> p f n", f=2)))
            settle()
            for c, src in ((1, bank[2][:, 0:256]), (2, bank[1][:, 256:512])):
                for f in range(2):
                    e = f * T + c * CHUNK + CHUNK - 1
                    step(V.scalar_tensor_tensor(st[:, c, f], st[:, c - 1, f], e_eb[:, e:e + 1], src[:, f * DV:(f + 1) * DV],
                                                ALU.mult, ALU.add))
                settle()
            V.memset(neg_row[:, 0:1], 0.0).then_inc(g["ev_states"], 1)
            dve.wait_ge(g["ln_sum"], 1)
            for c in range(CC):
                V.scalar_tensor_tensor(b3(e_xc, CC)[:, c, :], bank[3][:, 0:T], -1.0 / CONV_CH, cv[:, c, :],
                                       ALU.mult, ALU.add).then_inc(g["ln_centred"], 1)
            dve.wait_ge(g["ev_o"], 1)
            for r in range(2):
                V.tensor_copy(e_o[:, r * 512:(r + 1) * 512], bank[6 + r][:, :]).then_inc(g["ev_o_out"], 1)
            dve.wait_ge(g["ln_var"], 1)
            V.tensor_scalar(e_mu[:, 0:T], bank[3][:, 0:T], 1.0 / CONV_CH, EPS, ALU.mult, ALU.add).then_inc(g["ln_mean"], 1)
            dve.wait_ge(g["ev_o_sum"], 1)
            for r in range(2):
                V.tensor_scalar(e_osq[:, r * 512:(r + 1) * 512], bank[4 + r][:, :], 1.0 / DV, EPS, ALU.mult,
                                ALU.add).then_inc(g["ev_o_mean"], 1)
            dve.wait_ge(g["ln_root"], 1)
            step(V.reciprocal(e_mu[:, 2 * T:3 * T], e_mu[:, T:2 * T]))
            settle()
            V.tensor_tensor(b3(e_xn, CC), b3(e_xc, CC),
                            e_mu[:, 2 * T:3 * T].rearrange("p (o t) -> p o t", o=1).to_broadcast([P, CC, T]),
                            ALU.mult).then_inc(g["ln_normed"], 1)
            dve.wait_ge(g["ev_o_root"], 1)
            step(V.reciprocal(e_orr, e_orr))
            settle()
            step(V.scalar_tensor_tensor(e_o, e_o, glag, e_orr, ALU.mult, ALU.mult))
            settle()
            for r in range(2):
                dst = e_y[:, 4 * T:8 * T].rearrange("p (f r t) -> p r f t", f=2, r=2)[:, r]
                gate = e_r.rearrange("p (f r t) -> p r f t", f=2, r=2)[:, r]
                V.tensor_tensor(dst, e_o[:, r * 512:(r + 1) * 512].rearrange("p (f t) -> p f t", f=2), gate,
                                ALU.mult).then_inc(g["ev_y"], 1)
            u[0] = 11
            lows_of(e_y)
            residual(8, True)

            def top16(vals, idx, src, groups, width):
                def at(ap, j, half):
                    return ap[:, j * 16 + 8 * half:j * 16 + 8 * half + 8]

                def row(j):
                    return src[:, j * width:(j + 1) * width]

                for half in range(2):
                    for j in range(groups):
                        step(V.max(at(vals, j, half), row(j)))
                    settle()
                    for j in range(groups):
                        step(V.max_index(at(idx, j, half), at(vals, j, half), row(j)))
                    if not half:
                        settle()
                        for j in range(groups):
                            step(V.match_replace(row(j), at(vals, j, 0), row(j), NEG_BIG))
                        settle()

            def experts(layer):
                norm(1 + 2 * layer)
                n[0] += 16 + NK
                for tb in range(TB):
                    dve.wait_ge(g["scores_out"], 8 * layer + 4 * (tb + 1))
                    top16(top_v[:, tb * 256:(tb + 1) * 256], top_i[:, tb * 256:(tb + 1) * 256],
                          sco[:, tb * 2048:(tb + 1) * 2048], 16, NK)
                settle()
                step(V.tensor_copy(top_if, top_i))
                cand, oh = sco[:, 0:2048], sco[:, 2048:4096]
                for tb in range(TB):
                    tv = top_v[:, tb * 256:(tb + 1) * 256].rearrange("p (h c k) -> p h c k", h=PH, c=2)
                    ti = top_if[:, tb * 256:(tb + 1) * 256].rearrange("p (h c k) -> p h c k", h=PH, c=2)
                    settle()
                    for h in range(PH):
                        step(V.tensor_tensor(cand[:, h * 256:(h + 1) * 256].rearrange("p (a b) -> p a b", a=16),
                                             tv[:, h, 0, :].rearrange("p (k o) -> p k o", o=1).to_broadcast([P, 16, 16]),
                                             tv[:, h, 1, :].rearrange("p (o k) -> p o k", o=1).to_broadcast([P, 16, 16]), ALU.add))
                    settle()
                    top16(cand_v, cand_i, cand, PH, 256)
                    settle()
                    step(V.tensor_scalar(rank_u[:, 0:P], cand_i, 4, None, ALU.logical_shift_right))
                    step(V.tensor_scalar(rank_u[:, P:2 * P], cand_i, 15, None, ALU.bitwise_and))
                    settle()
                    step(V.tensor_copy(rank_f, rank_u))
                    for c in range(2):
                        settle()
                        step(V.tensor_tensor(oh.rearrange("p (s k) -> p s k", k=16),
                                             rank_f[:, c * P:(c + 1) * P].rearrange("p (s o) -> p s o", o=1).to_broadcast([P, P, 16]),
                                             iota16[:, 0:16].rearrange("p (o k) -> p o k", o=1).to_broadcast([P, P, 16]), ALU.is_equal))
                        settle()
                        for h in range(PH):
                            v = oh[:, h * 256:(h + 1) * 256].rearrange("p (s k) -> p s k", k=16)
                            step(V.tensor_tensor(v, v, ti[:, h, c, :].rearrange("p (o k) -> p o k", o=1).to_broadcast([P, 16, 16]), ALU.mult))
                        settle()
                        step(V.tensor_reduce(slot3[:, (c * TB + tb) * P:(c * TB + tb + 1) * P],
                                             oh.rearrange("p (s k) -> p s k", k=16), AX.X, ALU.add))
                    cvv = cand_v.rearrange("p (h k) -> p h k", h=PH)
                    V.tensor_tensor(slot3[:, (2 * TB + tb) * P:(2 * TB + tb + 1) * P].rearrange("p (h k) -> p h k", h=PH),
                                    cvv, cvv[:, :, 0:1].to_broadcast([P, PH, 16]), ALU.subtract).then_inc(g["gate_shifted"], 1)
                for tb in range(TB):
                    gt = slot3[:, (2 * TB + tb) * P:(2 * TB + tb + 1) * P].rearrange("p (h k) -> p h k", h=PH)
                    gs = gate_s[:, tb * PH:(tb + 1) * PH]
                    dve.wait_ge(g["gate_exped"], TB * layer + tb + 1)
                    step(V.tensor_reduce(gs, gt, AX.X, ALU.add))
                    settle()
                    step(V.reciprocal(gs, gs))
                    settle()
                    V.tensor_tensor(gt, gt, gs.rearrange("p (h o) -> p h o", o=1).to_broadcast([P, PH, 16]),
                                    ALU.mult).then_inc(g["slots_ready"], 1)
                settle()
                dve.wait_ge(g["slots_turned"], layer + 1)
                V.tensor_copy(e1T, bank[4][:, 0:T]).then_inc(g["turned"], 1)
                V.tensor_copy(e2T, bank[4][:, T:2 * T]).then_inc(g["turned"], 1)
                rest = sco[:, 0:T]
                step(V.tensor_copy(g_part[0], bank[5][:, 0:T]))
                settle()
                step(V.tensor_tensor(rest, bank[5][:, 0:T], g_part[0], ALU.subtract))
                settle()
                step(V.tensor_copy(g_part[1], rest))
                settle()
                V.tensor_tensor(g_part[2], rest, g_part[1], ALU.subtract).then_inc(g["turned"], 1)
                dve.wait_ge(g["turned"], 3 * layer + 3)
                acts = big[:, :].rearrange("p (e t) -> p e t", t=T)
                groups = T // GROUP_T
                base = 2 * groups * layer

                def build(m, i=0):
                    half, t0 = m // groups, i * (3 * GROUP_T) + (m % groups) * GROUP_T
                    if base + m >= 3:
                        dve.wait_ge(g["gates_spread"], i * 3 + (base + m - 2))

                    def match(dst, keys, row):
                        n = keys.shape[1]
                        return V.tensor_tensor(b3(dst, GROUP_T), keys.rearrange("p (o e) -> p o e", o=1).to_broadcast([P, GROUP_T, n]),
                                               row[:, bass.ds(t0, GROUP_T)].rearrange("p (t o) -> p t o", o=1)
                                               .to_broadcast([P, GROUP_T, n]), ALU.is_equal)

                    match(hot1[(base + m) % 3][2], iota16[:, half * HALF:(half + 1) * HALF], e1T).then_inc(g["matched"], 1)
                    match(hot2[(base + m) % 3], iota16[:, :], e2T).then_inc(g["second_hot"], 1)

                def gate(m, i=0):
                    half, t0 = m // groups, i * (3 * GROUP_T) + (m % groups) * GROUP_T
                    dve.wait_ge(g["gates_spread"], i * 3 + (base + m + 1))
                    v = acts[:, half * HALF:(half + 1) * HALF, bass.ds(t0, GROUP_T)]
                    b = m % 3 if half else 4 + m % 3
                    V.tensor_tensor(v, bank[b][:, :].rearrange("p (j e) -> p e j", j=GROUP_T), v, ALU.mult).then_inc(g["gated"], 1)

                u[0] += 8 + 64
                k0 = starts[f"u{layer}b"]
                build(0)
                build(1)
                dve.wait_ge(g["units_out"], u[0] - 32)
                with dve.Fori(0, groups // 3) as i:
                    for q in range(3):
                        low(k0 + 2 * q, i)
                        low(k0 + 2 * q + 1, i)
                        gate(q, i)
                        build(q + 2, i)
                for m in (groups - 2, groups - 1):
                    low(k0 + 2 * m)
                    low(k0 + 2 * m + 1)
                    gate(m)
                build(groups)
                build(groups + 1)
                dve.wait_ge(g["units_out"], u[0])
                k0 += HALF
                src = lambda k, i: big[:, bass.ds(i * BODY * T + k * T, T)]
                for k in range(RING):
                    low(k0 + k)
                    chunk(k0, k, src)
                with dve.Fori(0, groups // 3) as i:
                    for q in range(3):
                        gate(groups + q, i)
                        build(groups + q + 2, i)
                        for k in (2 * q + 3, 2 * q + 4):
                            low(k0 + k, i)
                            chunk(k0, k, src, i)
                gate(2 * groups - 2)
                gate(2 * groups - 1)
                low(k0 + HALF - 1)
                chunk(k0, HALF - 1, src)
                ax[0] += HALF
                accumulated(f"v{layer}b", HALF, lambda k, i: src(HALF + k, i))
                residual(NK, False)

            experts(0)

            def log_sigmoid_rows():
                dve.wait_ge(g["units_out"], u[0] + 9)
                dve.wait_ge(g["od_tables_loaded"], 16)
                V.tensor_scalar(o_z[0], o_z[0], o_fb[:, 0:1], None, ALU.add).then_inc(g["od_z_in"], 1)
                dve.wait_ge(g["od_z_in"], 1)
                step(V.tensor_scalar(o_z[3], o_z[0], 0.0, None, ALU.min))
                settle()
                dve.wait_ge(g["od_z_log"], 1)
                step(V.tensor_tensor(o_z[4], o_z[3], o_z[2], ALU.subtract))
                settle()
                step(V.memset(o_z[0], 1.0))
                settle()
                step(V.tensor_tensor_scan(o_z[5], o_z[0], o_z[4], 0.0, ALU.mult, ALU.add))
                settle()
                dve.wait_ge(g["od_sel"], 1)
                for rows in (0, 64):
                    step(V.tensor_scalar(o_right.rearrange("p (h t) -> p h t", h=FH)[rows:rows + 32],
                                         o_z[5][rows:rows + 32].rearrange("p (o t) -> p o t", o=1).to_broadcast([32, FH, T]),
                                         -1.0, None, ALU.mult))
                    step(V.tensor_copy(o_left.rearrange("p (h t) -> p h t", h=FH)[rows + 32:rows + 48],
                                       o_z[5][rows + 32:rows + 48].rearrange("p (o t) -> p o t", o=1).to_broadcast([16, FH, T])))
                settle()
                V.memset(neg_row[:, 0:1], 0.0).then_inc(g["od_bias_ready"], 1)

            def head_norm(count, raw, tmp, dst, gain, done, mean, root, ready):
                for s in range(count):
                    v = tmp[:, (s % 3) * 512:(s % 3 + 1) * 512]
                    dve.wait_ge(g[done], s + 1)
                    if s >= 3:
                        dve.wait_ge(g[ready], s - 2)
                    V.tensor_scalar(v, bank[4 + s % 4][:, :], 1.0 / HD, EPS, ALU.mult, ALU.add).then_inc(g[mean], 1)
                    dve.wait_ge(g[root], s + 1)
                    step(V.reciprocal(v, v))
                    settle()
                    V.scalar_tensor_tensor(dst[:, s * 512:(s + 1) * 512], raw[:, s * 512:(s + 1) * 512], gain(s), v,
                                           ALU.mult, ALU.mult).then_inc(g[ready], 1)

            def attention(p):
                for h in range(p["heads"] + 1):
                    if h < p["heads"]:
                        c = p["base"] + h
                        S, sm = p["s"][h % 2], p["small"][:, (h % 2) * 8:(h % 2) * 8 + 8]
                        dve.wait_ge(g["at_score"], c + 1)
                        if h >= 2:
                            dve.wait_ge(g["at_exped"], c - 1)
                        step(V.scalar_tensor_tensor(S, p["table"], p["factor"](h), bank[4 + h % 2][:, 0:3 * P],
                                                    ALU.mult, ALU.add))
                        settle()
                        first = V.tensor_reduce(sm[:, 0:1], S[:, 0:P], AX.X, ALU.max, negate=True)
                        step(first)
                        if p["tag"]:
                            step(V.tensor_reduce(sm[:, 1:2], S[:, P:3 * P], AX.X, ALU.max, negate=True))
                            settle()
                            V.tensor_scalar(sm[:, 0:2], sm[:, 0:2], nsink[:, h:h + 1], None, ALU.min).then_inc(g["at_masked"], 1)
                        else:
                            settle()
                            V.tensor_reduce(sm[:, 1:2], S[:, P:3 * P], AX.X, ALU.max, negate=True).then_inc(g["at_masked"], 1)
                    if h >= 1:
                        c = p["base"] + h - 1
                        PR, sm = p["p"][(h - 1) % 2], p["small"][:, ((h - 1) % 2) * 8:((h - 1) % 2) * 8 + 8]
                        dve.wait_ge(g["at_exped"], c + 1)
                        if p["tag"]:
                            step(V.tensor_tensor(sm[:, 2:4], sm[:, 2:4], sm[:, 4:6], ALU.add))
                            settle()
                        step(V.reciprocal(sm[:, 6:8], sm[:, 2:4]))
                        settle()
                        step(V.tensor_scalar(PR[:, 0:P], PR[:, 0:P], sm[:, 6:7], None, ALU.mult))
                        settle()
                        V.tensor_scalar(PR[:, P:3 * P], PR[:, P:3 * P], sm[:, 7:8], None, ALU.mult).then_inc(g["at_prob"], 1)

            norm(G_OD)
            step(V.tensor_scalar(qk_gain[:, 0:1], qk_gain[:, 0:1], HD ** -0.5, None, ALU.mult))
            step(V.tensor_scalar(qk_gain[:, 2:3], qk_gain[:, 2:3], HD ** -0.5, None, ALU.mult))
            log_sigmoid_rows()
            head_norm(8, o_qk, o_tmp, o_n, lambda s: qk_gain[:, 0:1] if s < 4 else qk_gain[:, 1:2],
                      "od_sum", "od_mean", "od_root", "od_qk_ready")
            attention(odd_att)
            u[0] += 13
            n[0] += 25
            lows_of(o_y)
            residual(8, True)

            experts(1)

            norm(G_MIX2)
            step(V.tensor_scalar(nsink[:, :], sinks[:, :], -1.0, None, ALU.mult))
            dve.wait_ge(g["sb_tables_loaded"], 80)
            head_norm(3, s_qk, s_tmp, s_n, lambda s: qk_gain[:, 2:3] if s < 2 else qk_gain[:, 3:4],
                      "sb_sum", "sb_mean", "sb_root", "sb_qk_ready")
            dve.wait_ge(g["units_out"], u[0] + 8)
            for tb in range(TB):
                v = s_gv[:, tb * 512:(tb + 1) * 512]
                step(V.tensor_tensor(s_gv2[:, tb * 512:(tb + 1) * 512], v, v, ALU.mult))
            settle()
            step(V.tensor_reduce(s_small[:, 0:2], b3(s_gv2, TB), AX.X, ALU.add))
            settle()
            V.tensor_scalar(s_small[:, 2:4], s_small[:, 0:2], 1.0 / 512, EPS, ALU.mult, ALU.add).then_inc(g["sgu_mean"], 1)
            dve.wait_ge(g["sgu_root"], 1)
            step(V.reciprocal(s_small[:, 6:8], s_small[:, 4:6]))
            settle()
            for tb in range(TB):
                V.scalar_tensor_tensor(s_vn[:, tb * 512:(tb + 1) * 512], s_gv[:, tb * 512:(tb + 1) * 512],
                                       s_small[:, 6 + tb:7 + tb], s_norm, ALU.mult, ALU.mult).then_inc(g["sgu_v_ready"], 1)
            dve.wait_ge(g["sgu_mixed"], 1)
            for j in range(2):
                step(V.tensor_tensor(s_mix[:, j * 512:(j + 1) * 512].rearrange("p (c b t) -> p c b t", c=2, b=TB),
                                     bank[6 + j][:, :].rearrange("p (c b t) -> p c b t", c=2, b=TB),
                                     s_bs[:, j * 256:(j + 1) * 256].rearrange("p (c o t) -> p c o t", c=2, o=1).to_broadcast([P, 2, TB, P]),
                                     ALU.add))
            settle()
            V.tensor_tensor(s_yb, s_mix, s_u, ALU.mult).then_inc(g["sgu_y"], 1)
            attention(swa_att)
            u[0] += 16
            lows_of(big[:, at_y:at_y + 8 * T])
            dve.wait_ge(g["units_out"], u[0])
            n[0] += 31
            gates = s_gate.rearrange("p (b c t) -> p b c t", b=2, c=KC)
            for c in range(KC):
                dve.wait_ge(g["pieces_used"], n[0] + c + 1)
                pr = s_prod[:, (c % 2) * 512:(c % 2 + 1) * 512]
                V.tensor_tensor(b3(pr, 2), b3(bank[c % 4][:, :], 2), gates[:, :, c, :], ALU.mult).then_inc(g["merged_out"], 1)
                dve.wait_ge(g["merged_out"], c + 1)
                V.tensor_tensor(s_m[:, c * T:(c + 1) * T], pr[:, 0:T], pr[:, T:2 * T], ALU.add).then_inc(g["merged"], 1)
            n[0] += 8
            lows_of(s_m)
            residual(8, True)

            norm(G_FFN2)
            for q in range(UNITS):
                V.memset(b3(f_z[q], 2)[:, :, 0:2], 0.0).then_inc(g["ff_gated"], 1)

            def convolve(i, q):
                dve.wait_ge(g["units_out"], i * UNITS + (u[0] + q + 1))
                z, zc = b3(f_z[q], 2), b3(f_zc[q], 2)
                for half in range(2):
                    col = q * 2 + half
                    V.tensor_scalar(zc[:, half, :], z[:, half, 0:T], f_cw[:, bass.ds(i * 18 + 3 * col, 1)],
                                    f_cb[:, bass.ds(i * 6 + col, 1)], ALU.mult, ALU.add).then_inc(g["ff_tap"], 1)
                for tap in (1, 2):
                    dve.wait_ge(g["ff_tap"], i * 12 + (q * 4 + 2 * tap))
                    for half in range(2):
                        col = q * 2 + half
                        ins = V.scalar_tensor_tensor(zc[:, half, :], z[:, half, tap:tap + T],
                                                     f_cw[:, bass.ds(i * 18 + (3 * col + tap), 1)], zc[:, half, :],
                                                     ALU.mult, ALU.add)
                        if tap == 1:
                            ins.then_inc(g["ff_tap"], 1)
                ins.then_inc(g["ff_z"], 1)
                dve.wait_ge(g["ff_silu"], i * UNITS + (q + 1))
                V.tensor_tensor(f_act[:, bass.ds(i * UNITS * T + q * T, T)], f_sil[q], f_zc[q][:, T:2 * T],
                                ALU.mult).then_inc(g["ff_gated"], 1)

            with dve.Fori(0, FC // UNITS) as i:
                for q in range(UNITS):
                    convolve(i, q)
            for q in range(FC % UNITS):
                convolve(FC // UNITS, q)
            n[0] += 2 * FC
            accumulated("down", FC, lambda k, i: f_act[:, bass.ds(i * BODY * T + k * T, T)])
            residual(FC, False)

        @block.tensor
        def _(pe):
            n, u = [0], [0]
            mm = nc.tensor.matmul

            def norm(k):
                for j in range(4):
                    pe.wait_ge(g["norm_squared"], 4 * k + j + 1)
                    for c in (2 * j, 2 * j + 1):
                        last = mm(bank[4][:, 0:T], ones[:, :], sqv[:, c, :], start=(c == 0), stop=(c == KC - 1))
                last.then_inc(g["norm_summed"], 1)

            xs, ax = [0], [0]
            xh, xl = b3(x_hi[:, :], KC), b3(x_lo[:, :], KC)

            def weights(at, i):
                k = n[0] + at
                pe.wait_ge(*low_bits(k, i))
                return w_hi[:, k % RING, :], w_lo[:, k % RING, :]

            def no_wait(c):
                pass

            def next_split():
                base = 4 * xs[0]
                xs[0] += 1

                def wait(c):
                    if c % 2 == 0:
                        pe.wait_ge(g["x_lo_done"], base + c // 2 + 1)
                return wait

            def features(dst, w, ready=no_wait):
                hi, lo = w
                for c in range(KC):
                    ready(c)
                    rows = slice(c * P, (c + 1) * P)
                    mm(dst, hi[:, rows], xh[:, c, :], start=(c == 0), stop=False)
                    mm(dst, hi[:, rows], xl[:, c, :], start=False, stop=False)
                    last = mm(dst, lo[:, rows], xh[:, c, :], start=False, stop=(c == KC - 1))
                return last

            def tokens(dst, w, ready=no_wait):
                hi, lo = w
                for b in range(TB):
                    for c in range(KC):
                        rows, t = slice(c * P, (c + 1) * P), slice(b * P, (b + 1) * P)
                        mm(dst[:, t], xh[:, c, t], hi[:, rows], start=(c == 0), stop=False)
                        mm(dst[:, t], xl[:, c, t], hi[:, rows], start=False, stop=False)
                        last = mm(dst[:, t], xh[:, c, t], lo[:, rows], start=False, stop=(c == KC - 1))
                return last

            def unit(make, pieces=2, at=0, q=0, i=0, ready=no_wait):
                if u[0] + q >= UNITS:
                    pe.wait_ge(g["units_out"], i * UNITS + (u[0] + q - UNITS + 1))
                for j in range(pieces):
                    w = weights(at + j, i)
                    make(unit_bank(u[0] + q)[:, j * T:(j + 1) * T], w, ready if j == 0 else no_wait).then_inc(g["pieces_used"], 1)

            def one_unit(make, pieces=2, ready=no_wait):
                unit(make, pieces, ready=ready)
                n[0] += pieces
                u[0] += 1

            def unit_loop(units):
                loops = units // UNITS
                if loops:
                    with pe.Fori(0, loops) as i:
                        for q in range(UNITS):
                            unit(features, 2, 2 * q, q, i)
                n[0] += BODY * loops
                u[0] += UNITS * loops
                for q in range(units % UNITS):
                    one_unit(features)

            def add_to_stream():
                ready = next_split()
                for j in range(8):
                    w = weights(0, 0)
                    features(bank[4 + j // 2][:, (j % 2) * T:(j % 2 + 1) * T], w, ready if j == 0 else no_wait).then_inc(g["pieces_used"], 1)
                    n[0] += 1

            def clear_banks():
                any_finite = ident[:, :].bitcast(BF16)
                for j in range(4):
                    for half in range(2):
                        mm(bank[4 + j][:, half * T:(half + 1) * T], zeros[:, :], any_finite, start=(half == 0), stop=False,
                           skip_group_check=True)

            def accumulate(count, spread=None):
                def piece(at, i=0):
                    hi, lo = weights(at, i)
                    pe.wait_ge(g["ax_lo"], i * BODY + (ax[0] + at + 1))
                    s = (n[0] + at) % RING
                    for c in range(KC):
                        dst, cols = bank[4 + c // 2][:, (c % 2) * T:(c % 2 + 1) * T], slice(c * P, (c + 1) * P)
                        mm(dst, hi[:, cols], xh[:, s, :], start=False, stop=False, skip_group_check=True)
                        mm(dst, hi[:, cols], xl[:, s, :], start=False, stop=False, skip_group_check=True)
                        last = mm(dst, lo[:, cols], xh[:, s, :], start=False, stop=False, skip_group_check=True)
                    last.then_inc(g["pieces_used"], 1)

                with pe.Fori(0, count // BODY) as i:
                    for j in range(BODY):
                        piece(j, i)
                        if spread and j % 2:
                            spread(j // 2 + 1, i)
                if spread:
                    spread(count // 2 - 1)
                for j in range(BODY * (count // BODY), count):
                    piece(j)
                n[0] += count
                ax[0] += count

            pe.wait_ge(g["consts"], 1)
            norm(G_EV)
            one_unit(features, ready=next_split())
            unit_loop(7)
            one_unit(features, 1)
            for j in range(2):
                one_unit(tokens)
            pe.wait_ge(g["ev_tables_loaded"], 32)
            pe.wait_ge(g["units_out"], 9)
            for f in range(2):
                last = mm(bank[5][:, f * T:(f + 1) * T], w_gate2[0:RANK, f * P:(f + 1) * P], e_glr[0:RANK, :], start=True, stop=True)
            last.then_inc(g["ev_z_ready"], 1)
            for lv in range(7):
                if lv < 6:
                    pe.wait_ge(g["ev_qk_level"], 2 * (lv + 1))
                    qe, ke = e_qe[lv % 2], e_ke[lv % 2]
                else:
                    qe, ke = e_q, e_k
                if lv >= 2:
                    pe.wait_ge(g["ev_level_in"], 2 * (lv - 1))
                for f in range(2):
                    for b in range(TB):
                        for r in range(2):
                            rows = slice(64 * r, 64 * r + 64)
                            cols = slice(f * T + b * P, f * T + b * P + P)
                            last = mm(bank[4 + 2 * (lv % 2) + r][:, (f * TB + b) * P:(f * TB + b + 1) * P],
                                      ke[rows, cols], qe[rows, cols], start=True, stop=True)
                last.then_inc(g["ev_level"], 1)
            pe.wait_ge(g["ev_kdec"], 2)
            pe.wait_ge(g["units_out"], 11)
            for b in range(TB):
                for f in range(2):
                    last = nc.tensor.transpose(bank[0][:, (b * 2 + f) * P:(b * 2 + f + 1) * P],
                                               e_kd[:, f * T + b * P:f * T + b * P + P], ident[:, :])
            last.then_inc(g["ev_kdec_turned"], 1)
            pe.wait_ge(g["conv_step"], CC * CONV_W)
            for c in range(CC):
                last = mm(bank[3][:, 0:T], ones[:, :], b3(e_conv, CC)[:, c, :], start=(c == 0), stop=(c == CC - 1))
            last.then_inc(g["ln_sum"], 1)
            pe.wait_ge(g["ev_kdt"], 1)
            for c, dst in ((0, bank[1][:, 0:256]), (2, bank[1][:, 256:512]), (1, bank[2][:, 0:256])):
                for h in range(GH):
                    rows = slice(64 * (c % 2), 64 * (c % 2) + 64)
                    last = mm(dst[64 * (h % 2):64 * (h % 2) + 64, (h // 2) * DV:(h // 2 + 1) * DV],
                              e_kdt[rows, (c // 2) * 256 + h * DK:(c // 2) * 256 + (h + 1) * DK],
                              e_v[rows, (c // 2) * 512 + h * DV:(c // 2) * 512 + (h + 1) * DV], start=True, stop=True)
            last.then_inc(g["ev_chunk_sums"], 1)
            pe.wait_ge(g["ev_level_in"], 14)
            pe.wait_ge(g["ev_states"], 1)
            st = e_state.rearrange("p (c f n) -> p c f n", c=3, f=2)
            atv = e_at.rearrange("p (r f b t) -> p r f b t", r=2, f=2, b=TB)
            for h in range(GH):
                f, r = h // 2, h % 2
                rows = slice(64 * r, 64 * r + 64)
                for b in range(TB):
                    dst = bank[6 + r][:, (f * TB + b) * P:(f * TB + b + 1) * P]
                    last = mm(dst, e_v[:, b * 512 + h * DV:b * 512 + (h + 1) * DV], atv[:, r, f, b, :], start=True, stop=False)
                    for c in (2 * b, 2 * b + 1):
                        if c:
                            last = mm(dst[:, (c % 2) * CHUNK:(c % 2 + 1) * CHUNK], st[rows, c - 1, f, :],
                                      e_qb[rows, f * T + c * CHUNK:f * T + (c + 1) * CHUNK], start=False, stop=(c % 2 == 1))
            last.then_inc(g["ev_o"], 1)
            pe.wait_ge(g["ln_sq"], 1)
            for c in range(CC):
                last = mm(bank[3][:, 0:T], ones[:, :], b3(e_sq2, CC)[:, c, :], start=(c == 0), stop=(c == CC - 1))
            last.then_inc(g["ln_var"], 1)
            pe.wait_ge(g["ev_o_sq"], 1)
            for r in range(2):
                last = mm(bank[4 + r][:, :], ones[:, :], e_osq[:, r * 512:(r + 1) * 512], start=True, stop=True)
            last.then_inc(g["ev_o_sum"], 1)
            pe.wait_ge(g["ev_o_mean"], 2)
            add_to_stream()

            def experts(layer):
                norm(1 + 2 * layer)
                one_unit(features, ready=next_split())
                unit_loop(7)
                pe.wait_ge(g["units_out"], u[0])
                pe.wait_ge(g["keys_loaded"], 16 * (layer + 1))
                for s in range(8):
                    if s >= 4:
                        pe.wait_ge(g["scores_out"], 8 * layer + s - 3)
                    for j in range(4):
                        k = (s % 4) * 4 + j
                        last = mm(bank[4 + s % 4][:, j * P:(j + 1) * P], qT[:, k * T + (s // 4) * P:k * T + (s // 4) * P + P],
                                  keysb[:, k * NK:(k + 1) * NK], start=True, stop=True)
                    last.then_inc(g["key_scored"], 1)
                unit_loop(28)
                pe.wait_ge(g["slots_ready"], TB * (layer + 1))
                pe.wait_ge(g["scores_out"], 8 * (layer + 1))
                for c in range(3):
                    for b in range(TB):
                        dst = (bank[4][:, 0:T], bank[4][:, T:2 * T], bank[5][:, 0:T])[c]
                        last = nc.tensor.transpose(dst[:, b * P:(b + 1) * P], slot3[:, (c * TB + b) * P:(c * TB + b + 1) * P],
                                                   ident[:, :])
                last.then_inc(g["slots_turned"], 1)
                unit_loop(4)
                groups = T // GROUP_T
                base = 2 * groups * layer

                def spread(m, banks, i=0):
                    count = base + m
                    pe.wait_ge(g["first_hot"], i * 3 + (count + 1))
                    pe.wait_ge(g["second_hot"], i * 3 + (count + 1))
                    if count >= 3:
                        pe.wait_ge(g["gated"], i * 3 + (count - 2))
                    second, parts = b3(hot2[count % 3], GROUP_T), [b3(x, GROUP_T) for x in hot1[count % 3]]
                    for j in range(GROUP_T):
                        for p in range(3):
                            last = mm(bank[banks + m % 3][:, j * HALF:(j + 1) * HALF], second[:, j, :], parts[p][:, j, :],
                                      start=(p == 0), stop=(p == 2))
                    last.then_inc(g["gates_spread"], 1)

                spread(0, 4)
                with pe.Fori(0, groups // 3) as i:
                    for q in range(3):
                        unit(features, 2, 2 * q, q, i)
                        spread(q + 1, 4, i)
                n[0] += 2 * (groups - 2)
                u[0] += groups - 2
                spread(groups - 1, 4)
                for _ in range(2):
                    one_unit(features)
                pe.wait_ge(g["units_out"], u[0])
                spread(groups, 0)
                pe.wait_ge(g["gated"], base + groups)
                clear_banks()
                accumulate(HALF, lambda m, i=0: spread(groups + m, 0, i))
                accumulate(HALF)

            def attention(p, filler):
                def score(h):
                    c = p["base"] + h
                    rows = slice(64 * (h % 2), 64 * (h % 2) + 64)
                    (q, qc), (k, kc) = p["q"](h), p["k"](h)
                    if h >= 2:
                        pe.wait_ge(g["at_masked"], c - 1)
                    dst = bank[4 + h % 2]
                    last = None
                    for lo, b, keys in ((0, 0, P), (P, 1, 2 * P)):
                        last = mm(dst[:, lo:lo + keys], q[rows, qc, b * P:(b + 1) * P], k[rows, kc, 0:keys],
                                  start=True, stop=bool(p["tag"]))
                        if not p["tag"]:
                            rb = slice(64 * (h % 2), 64 * (h % 2) + 48)
                            last = mm(dst[:, lo:lo + keys], o_left[rb, h * T + b * P:h * T + (b + 1) * P],
                                      o_right[rb, h * T:h * T + keys], start=False, stop=True)
                    last.then_inc(g["at_score"], 1)

                score(0)
                score(1)
                for h in range(p["heads"]):
                    c = p["base"] + h
                    PR, PT = p["p"][h % 2], p["pt"][h % 2]
                    filler(h)
                    pe.wait_ge(g["at_prob"], c + 1)
                    if h:
                        pe.wait_ge(g["at_pt"], c)
                    for j in range(3):
                        last = nc.tensor.transpose(bank[6][:, j * P:(j + 1) * P], PR[:, j * P:(j + 1) * P], ident[:, :])
                    last.then_inc(g["at_turned"], 1)
                    if h + 2 < p["heads"]:
                        score(h + 2)
                    pe.wait_ge(g["at_pt"], c + 1)
                    if h % 2 == 0 and h:
                        pe.wait_ge(g["at_y"], (p["base"] + h) // 2)
                    dst = bank[7][64 * (h % 2):64 * (h % 2) + 64, 0:T]
                    mm(dst, p["v"](0, h), PT[:, 0:T], start=True, stop=False)
                    mm(dst[:, P:T], p["v"](1, h), PT[:, T:3 * P], start=False, stop=True).then_inc(g["at_mixed"], 1)

            def head_sums(s, src, done, mean):
                if s >= 4:
                    pe.wait_ge(g[mean], s - 3)
                mm(bank[4 + s % 4][:, :], halves[:, :], src[:, s * 512:(s + 1) * 512], start=True, stop=True).then_inc(g[done], 1)

            experts(0)

            norm(G_OD)
            one_unit(features, ready=next_split())
            unit_loop(7)
            one_unit(features, 1)
            for j in range(4):
                one_unit(tokens)
                for s in (2 * j, 2 * j + 1):
                    pe.wait_ge(g["od_sq"], s + 1)
                    head_sums(s, o_sq, "od_sum", "od_mean")
            pe.wait_ge(g["od_qk_ready"], 8)
            pe.wait_ge(g["od_bias_ready"], 1)
            pe.wait_ge(g["units_out"], u[0])
            attention(odd_att, lambda h: None)
            add_to_stream()

            experts(1)

            norm(G_MIX2)
            one_unit(features, ready=next_split())
            for s in range(2):
                one_unit(features)
            one_unit(tokens, 1)
            for s in range(2):
                one_unit(tokens)
            for s in range(2):
                one_unit(features)
            for s in range(3):
                pe.wait_ge(g["sb_sq"], s + 1)
                head_sums(s, s_sq, "sb_sum", "sb_mean")
            pe.wait_ge(g["sgu_v_ready"], 2)
            pe.wait_ge(g["sgu_w_ready"], 1)
            pe.wait_ge(g["sb_qk_ready"], 3)
            for gr in range(SG):
                for b in range(TB):
                    c = gr // 2
                    last = mm(bank[6 + c // 2][64 * (gr % 2):64 * (gr % 2) + 64, ((c % 2) * TB + b) * P:((c % 2) * TB + b + 1) * P],
                              s_vn[:, b * 512 + gr * SGD:b * 512 + (gr + 1) * SGD], s_ws[:, gr * P:(gr + 1) * P],
                              start=True, stop=True)
            last.then_inc(g["sgu_mixed"], 1)
            pe.wait_ge(g["sgu_y"], 1)
            attention(swa_att, lambda h: one_unit(features))
            pe.wait_ge(g["units_out"], u[0])
            ready = next_split()
            for c in range(KC):
                if c >= 4:
                    pe.wait_ge(g["merged_out"], c - 3)
                hi, lo = weights(0, 0)
                for half in range(2):
                    for k in range(4 * half, 4 * half + 4):
                        if c == 0:
                            ready(k)
                        dst, rows = bank[c % 4][:, half * T:(half + 1) * T], slice(k * P, (k + 1) * P)
                        mm(dst, hi[:, rows], xh[:, k, :], start=(k % 4 == 0), stop=False)
                        mm(dst, hi[:, rows], xl[:, k, :], start=False, stop=False)
                        last = mm(dst, lo[:, rows], xh[:, k, :], start=False, stop=(k % 4 == 3))
                last.then_inc(g["pieces_used"], 1)
                n[0] += 1
            add_to_stream()

            norm(G_FFN2)
            one_unit(features, ready=next_split())
            unit_loop(FC - 1)
            pe.wait_ge(g["x_ready"], 20)
            pe.wait_ge(g["norm_mean"], 6)
            clear_banks()
            accumulate(FC)


def columns(w, order=None):
    w = np.asarray(w)
    n = w.shape[1] // P
    p = w.reshape(w.shape[0] // P, P, n, P).transpose(2, 1, 0, 3).reshape(n, P, -1)
    return p if order is None else p[order]


def chunked(v):
    return np.asarray(v).reshape(-1, P).T


def layout(i):
    o = {}
    o["x"] = np.asarray(i["x"])[0].T.reshape(KC, P, T).transpose(1, 0, 2).reshape(P, KC * T)
    o["gains"] = np.concatenate([chunked(v) for v in (i["ev_norm_mix"][0], i["ffn_norm"][0], i["od_norm_mix"][0],
                                                      i["ffn_norm"][1], i["mix_norm_2"][0], i["ffn_norm_2"][0])], 1)
    w = np.asarray(i["ev_w_in"])[0]
    val, gate, q, k, v, r = 0, 512, 1024, 1280, 1536, 2048
    rank = np.zeros((D, P), w.dtype)
    rank[:, :RANK] = w[:, 2560:]
    o["ev_in"] = np.concatenate([columns(w[:, val:v]), columns(w[:, r:r + 512]), columns(rank), columns(w[:, v:r])])
    o["w_gate2"] = np.asarray(i["ev_gate_w2"])[0]
    o["ev_small"] = np.concatenate(
        [np.asarray(i["ev_conv_w"])[0].reshape(CONV_W, CC, P).transpose(2, 0, 1).reshape(P, -1),
         chunked(i["ev_conv_b"][0]), chunked(i["ev_conv_ln_g"][0]), chunked(i["ev_conv_ln_b"][0]),
         chunked(i["ev_gate_b"][0]), chunked(i["ev_gla_norm_g"][0])], 1)
    o["ev_out"] = columns(i["ev_w_out"][0])
    for l in range(2):
        o[f"wq{l}"] = columns(i["peer_wq"][l])
        o[f"keys{l}"] = np.asarray(i["peer_keys"])[l].transpose(3, 0, 1, 2).reshape(P, 16 * NK)
        o[f"u{l}"] = np.asarray(i["peer_u"])[l].reshape(NK, NK, KC, P).transpose(0, 3, 2, 1).reshape(NK, P, D)
        o[f"v{l}"] = np.asarray(i["peer_v"])[l].reshape(NK, P, D)
    w = np.asarray(i["od_w_in"])[0]
    fz = np.zeros((D, P), w.dtype)
    fb = np.zeros((P, 1), w.dtype)
    for at in (0, 32, 64, 96):
        fz[:, at:at + FH] = w[:, 3 * D:]
        fb[at:at + FH, 0] = np.asarray(i["od_fgate_b"])[0]
    o["od_in"] = np.concatenate([columns(w[:, :2 * D]), columns(fz), columns(w[:, 2 * D:3 * D])])
    o["od_fb"] = fb
    o["od_out"] = columns(i["od_w_out"][0])
    o["qk_gain"] = np.stack([np.tile(np.asarray(v)[0], 2) for v in
                             (i["od_q_norm_g"], i["od_k_norm_g"], i["q_norm_2"], i["k_norm_2"])], 1)
    o["sinks"] = np.broadcast_to(np.asarray(i["sinks_2"])[0], (P, QH))
    w = np.asarray(i["w_in_2"])[0]
    kk = w[:, 512:640].reshape(D, 2, 1, HD)
    kk = np.broadcast_to(kk, (D, 2, 2, HD)).reshape(D, 256)
    o["sb_in"] = np.concatenate([columns(w[:, 0:512]), columns(kk), columns(w[:, 640:768]), columns(w[:, 1280:1792]),
                                 columns(w[:, 768:1280]), columns(w[:, 1792:])])
    o["sb_ab"] = columns(np.concatenate([np.asarray(i["w_oa_2"])[0], np.asarray(i["w_ob_2"])[0]]))
    o["sb_out"] = columns(i["w_out_2"][0])
    o["sb_ws"] = np.asarray(i["w_s_2"])[0].transpose(2, 0, 1).reshape(P, SG * P)
    o["sb_bs"] = np.repeat(np.asarray(i["b_s_2"])[0], SGD, 0).reshape(4, P, P).transpose(1, 0, 2).reshape(P, 4 * P)
    o["sb_norm"] = np.broadcast_to(np.asarray(i["sgu_norm_2"])[0], (P, 512))
    both = np.arange(2 * FC).reshape(2, FC).T.reshape(-1)
    o["up"] = columns(i["w_up_2"][0], both)
    o["ff_cw"] = np.asarray(i["conv_w_2"])[0].reshape(3, 2 * FC, P)[:, both].transpose(2, 1, 0).reshape(P, -1)
    o["ff_cb"] = np.asarray(i["conv_b_2"])[0].reshape(2 * FC, P)[both].T
    o["down"] = np.asarray(i["w_down_2"])[0].reshape(FC, P, D)
    return {k: np.ascontiguousarray(v) for k, v in o.items()}


def kernel(**inputs):
    import concourse.bacc as _bacc
    from concourse.bass_utils import run_bass_kernel_spmd as _run

    arrays = layout(inputs)
    nc = _bacc.Bacc("TRN2", target_bir_lowering=False, num_devices=1)
    dram = {name: nc.dram_tensor(name + "_dram", v.shape, mybir.dt.from_np(v.dtype), kind="ExternalInput").ap()
            for name, v in arrays.items()}
    out = nc.dram_tensor("out_dram", (P, KC * T), F32, kind="ExternalOutput").ap()
    build(nc, dram, out)
    r = _run(nc, [{name + "_dram": v for name, v in arrays.items()}], core_ids=[0])
    got = r.results[0]["out_dram"]
    return got.reshape(P, KC, T).transpose(2, 1, 0).reshape(1, T, D)
```

```python
from contextlib import ExitStack

import numpy as np

import concourse.bass as bass
from concourse import mybir

F32 = mybir.dt.float32
F32R = mybir.dt.float32r
BF16 = mybir.dt.bfloat16
I32 = mybir.dt.int32
U16 = mybir.dt.uint16
U32 = mybir.dt.uint32
ALU = mybir.AluOpType
ACT = mybir.ActivationFunctionType
AX = mybir.AxisListType

P = 128
T = 256
TB = T // P
D = 1024
KC = D // P
EPS = 1e-6
RING = 3
BODY = 6
GROUP_T = 8
UNITS = 3
PIECE = 1024

CONV_CH, CONV_W = 512, 31
CC = CONV_CH // P
GH, DK, DV, CHUNK, RANK, TAU = 4, 64, 128, 64, 16, 16.0
NCH = T // CHUNK
LEVELS = [32, 16, 8, 4, 2, 1]

FH, HD = 16, 64

PH, NK, TOPK = 8, 128, 16
NEG_BIG = -3.0e38

QH, KVH, GROUP = 8, 2, 4
SG, SGD = 8, 64
D_FF = 2816
FC = D_FF // P
FAR = 1e33

G_EV, G_PEER0, G_OD, G_PEER1, G_MIX2, G_FFN2 = range(6)
NORMS = 6


def build(nc, a, out):
    ctx = ExitStack()
    with ctx:
        def sb(name, shape, dt=F32):
            return ctx.enter_context(nc.sbuf_tensor(name, shape, dt))

        def sem(name):
            return ctx.enter_context(nc.semaphore(name))

        bank = [ctx.enter_context(nc.psum_tensor(f"bank{i}", [P, 512], F32)) for i in range(8)]

        big = sb("big", [P, 128 * T])
        ring = sb("ring", [P, RING, PIECE])
        w_hi = sb("w_hi", [P, RING, PIECE], F32R)
        w_lo = sb("w_lo", [P, RING, PIECE], F32R)
        xT = sb("xT", [P, KC * T])
        x_hi = sb("x_hi", [P, KC * T], F32R)
        x_lo = sb("x_lo", [P, KC * T], F32R)
        sco = sb("sco", [P, TB * 16 * NK])
        ones = sb("ones", [P, P])
        ident = sb("ident", [P, P])
        halves = sb("halves", [P, P])
        iota16 = sb("iota16", [P, P], BF16)
        zeros = sb("zeros", [P, P], BF16)
        gains = sb("gains", [P, NORMS * KC])
        qk_gain = sb("qk_gain", [P, 4])
        sinks = sb("sinks", [P, QH])
        eps_row = sb("eps_row", [P, 2])
        neg_row, eps = eps_row[:, 0:1], eps_row[:, 1:2]
        gate_s = sb("gate_s", [P, 2 * PH])
        at = 24576
        top_v = big[:, at:at + 512]
        top_i = big[:, at + 512:at + 768].bitcast(U16)
        top_if = big[:, at + 768:at + 1280]
        cand_v = big[:, at + 1280:at + 1408]
        cand_i = big[:, at + 1408:at + 1536].bitcast(U32)
        rank_u = big[:, at + 1536:at + 1792].bitcast(U32)
        rank_f = big[:, at + 1792:at + 2048]
        slot3 = big[:, at + 2048:at + 2816]
        g_parts = sb("g_parts", [P, 3 * T], BF16)
        g_part = [g_parts[:, j * T:(j + 1) * T] for j in range(3)]
        sco16 = sco[:, :].bitcast(BF16)
        hot2 = [sco16[:, b * GROUP_T * NK:(b + 1) * GROUP_T * NK] for b in range(3)]
        hot1 = [[sco16[:, 3 * GROUP_T * NK + (3 * b + p) * GROUP_T * NK // 2:3 * GROUP_T * NK + (3 * b + p + 1) * GROUP_T * NK // 2]
                 for p in range(3)] for b in range(3)]
        e1T, e2T = (sco16[:, j * T:(j + 1) * T] for j in (30, 31))
        nsink = gate_s[:, 0:QH]

        cursor = [0]

        def carve(n, size=1):
            at = cursor[0]
            cursor[0] += n
            assert cursor[0] <= 27904, cursor
            return big[:, at:at + n]

        rt, rr = (big[:, 27904 + i * T:27904 + (i + 1) * T] for i in range(2))
        sq = big[:, 28672:28672 + KC * T]
        keysb = big[:, 30720:30720 + 16 * NK]
        qT = big[:, 0:16 * T]

        def b3(ap, n):
            return ap.rearrange("p (a b) -> p a b", a=n)

        xv, sqv = b3(xT[:, :], KC), b3(sq, KC)
        h32 = sq

        cursor[0] = 0
        ev_small = carve(4 * CONV_W + 4 * 3 + 2 + 2)
        o = 4 * CONV_W
        cw, cb, lng, lnb = ev_small[:, 0:o], ev_small[:, o:o + 4], ev_small[:, o + 4:o + 8], ev_small[:, o + 8:o + 12]
        gb, glag = ev_small[:, o + 12:o + 14], ev_small[:, o + 14:o + 15]
        w_gate2 = carve(GH * DK)
        e_val, e_sig = carve(CC * T), carve(CC * T)
        UW = T + CONV_W - 1
        e_u = carve(CC * UW)
        e_conv, e_xc = carve(CC * T), carve(CC * T)
        tap_diag = [sco[:, w * P:(w + 1) * P] for w in range(CONV_W)]
        e_sq2, e_xn = e_sig, e_val
        e_q, e_k, e_r = carve(2 * T), carve(2 * T), carve(4 * T)
        e_v = carve(TB * GH * DV)
        e_glr = carve(T)
        at_zb = cursor[0]
        e_zb, e_az, e_mn, e_ln, e_la, e_b, e_eb, e_nd, e_kd, e_qb = (carve(2 * T) for _ in range(10))
        e_reset = carve(T)
        e_dif = [carve(2 * T) for _ in range(2)]
        e_exp = [carve(2 * T) for _ in range(2)]
        e_qe = [carve(2 * T) for _ in range(2)]
        e_ke = [carve(2 * T) for _ in range(2)]
        e_at = carve(2 * 2 * TB * P)
        e_kdt = carve(TB * 2 * P)
        e_state = carve(3 * 2 * DV)
        e_o, e_osq, e_orr = carve(4 * T), carve(4 * T), carve(4 * T)
        e_y = carve(KC * T)
        e_mask = carve(7 * P).bitcast(I32)
        e_si, e_ti, e_xr = carve(P).bitcast(I32), carve(P).bitcast(I32), carve(2 * P).bitcast(I32)
        e_mu = big[:, at_zb:at_zb + 3 * T]

        cursor[0] = 0
        o_fb = carve(4)
        o_qk, o_sq = carve(16 * T), carve(16 * T)
        o_n = o_sq
        o_v = carve(TB * D)
        o_left, o_right = carve(FH * T), carve(FH * T)
        o_z = [carve(T) for _ in range(6)]
        causal = carve(3 * P)
        at_s = [carve(3 * P) for _ in range(2)]
        at_p = [carve(3 * P) for _ in range(2)]
        at_pt = [carve(3 * P) for _ in range(2)]
        at_small = carve(2 * 8)
        o_y = carve(KC * T)

        cursor[0] = 0
        s_ws = carve(SG * P)
        s_bs = carve(4 * P)
        s_norm = carve(512)
        f_cw = carve(2 * FC * 3)
        f_cb = carve(2 * FC)
        s_qk, s_sq, s_n = carve(6 * T), carve(6 * T), carve(6 * T)
        s_v = carve(TB * P)
        s_u = carve(4 * T)
        s_gv, s_gv2, s_vn = carve(TB * 512), carve(TB * 512), carve(TB * 512)
        s_small = carve(8)
        s_gate = carve(16 * T)
        s_mix = carve(4 * T)
        at_y = cursor[0]
        s_ya, s_yb = carve(4 * T), carve(4 * T)
        s_prod = carve(2 * 2 * T)
        s_m = carve(KC * T)
        f_act = None
        assert cursor[0] <= 24000, cursor
        cursor[0] = max(cursor[0], 0)
        dist = carve(3 * P)
        s_at_s = [carve(3 * P) for _ in range(2)]
        s_at_p = [carve(3 * P) for _ in range(2)]
        s_at_pt = [carve(3 * P) for _ in range(2)]
        s_at_small = carve(2 * 8)
        ZW = T + 2
        f_at = 2688
        f_z = [big[:, f_at + i * 2 * ZW:f_at + (i + 1) * 2 * ZW] for i in range(3)]
        f_at += 3 * 2 * ZW
        f_zc = [big[:, f_at + i * 2 * T:f_at + (i + 1) * 2 * T] for i in range(3)]
        f_at += 3 * 2 * T
        f_sil = [big[:, f_at + i * T:f_at + (i + 1) * T] for i in range(3)]
        f_at += 3 * T
        f_act = big[:, f_at:f_at + FC * T]
        assert f_at + FC * T <= 27904

        names = """x_loaded ev_tables_loaded tables_loaded keys_loaded od_tables_loaded sb_tables_loaded stored
            consts
            pieces_used units_out w_hi_done lo_pool lo_dve x_hi_done x_lo_done ax_hi ax_lo
            norm_squared norm_summed norm_log norm_root bank_done h_ready x_ready
            key_scored scores_out gate_shifted gate_exped slots_ready slots_turned turned
            matched first_hot second_hot gates_spread gated pool_step dve_step act_step
            ev_z_ready ev_z_in ev_z_log ev_o_log ln_log ev_decay_part ev_fade
            ev_expb ev_expk ev_dif ev_difexp ev_qk_level ev_level ev_level_in ev_kdec ev_kdec_turned ev_kdt
            ev_chunk_sums ev_states ev_o ev_o_out ev_o_sq ev_o_sum ev_o_root ev_y
            conv_input conv_step taps_laid conv_mixed ln_sum ln_centred ln_sq ln_var ln_root ln_normed ev_ya
            od_z_in od_z_log od_bias_ready od_sq od_sum od_log od_root od_qk_ready od_sel
            at_score at_masked at_exped at_prob at_turned at_pt at_mixed at_y
            sb_sq sb_sum sb_log sb_root sb_qk_ready sgu_mean sgu_root sgu_v_ready sgu_w_ready
            sgu_mixed sgu_y merged_out merged ff_silu ff_z ff_gated ff_tap""".split()
        g = {n: sem(n) for n in names}
        slot_loaded = [sem(f"slot_loaded{i}") for i in range(RING)]

        POOL, DVE = range(2)
        HALF = NK // 2
        RUNS = [("ev_in", "ev_in", 21, POOL), ("ev_out", "ev_out", 8, POOL),
                ("wq0", "wq0", 16, POOL), ("u0", "u0", HALF, POOL), ("u0b", "u0", HALF, DVE),
                ("v0", "v0", HALF, DVE), ("v0b", "v0", HALF, DVE),
                ("od_in", "od_in", 2, POOL), ("od_in_b", "od_in", 12, DVE),
                ("od_in_c", "od_in", 11, POOL), ("od_out", "od_out", 8, POOL),
                ("wq1", "wq1", 16, POOL), ("u1", "u1", HALF, POOL), ("u1b", "u1", HALF, DVE),
                ("v1", "v1", HALF, DVE), ("v1b", "v1", HALF, DVE),
                ("sb_in", "sb_in", 31, POOL), ("sb_ab", "sb_ab", 8, POOL), ("sb_out", "sb_out", 8, POOL),
                ("up", "up", 2 * FC, POOL), ("down", "down", RING, POOL),
                ("down_b", "down", FC - RING, DVE)]
        starts, by_dve = {}, []
        for name, _, count, who in RUNS:
            starts[name] = len(by_dve)
            by_dve += [who == DVE] * count
        total_pieces = len(by_dve)

        def low_bits(k, i=0):
            so_far = by_dve[:k + 1].count(by_dve[k])
            return g["lo_dve" if by_dve[k] else "lo_pool"], i * BODY + so_far


        def unit_bank(u):
            return bank[u % UNITS]

        odd_att = dict(heads=FH, tag=0, s=at_s, p=at_p, pt=at_pt, small=at_small, y=b3(o_y, KC),
                       q=lambda h: (b3(o_n, 16), h // 2), k=lambda h: (b3(o_n, 16), 8 + h // 2),
                       v=lambda tb, h: o_v[:, tb * D + h * HD:tb * D + h * HD + HD],
                       table=causal, factor=lambda h: 1.0, base=0)
        swa_att = dict(heads=QH, tag=1, s=s_at_s, p=s_at_p, pt=s_at_pt, small=s_at_small, y=b3(s_ya, 4),
                       q=lambda h: (b3(s_n, 6), h // 2), k=lambda h: (b3(s_n, 6), 4 + h // GROUP),
                       v=lambda tb, h: s_v[:, tb * P + (h // GROUP) * HD:tb * P + (h // GROUP) * HD + HD],
                       table=dist, factor=lambda h: -(2.0 ** (-8.0 * (h + 1.0) / QH)), base=FH)

        block = ctx.enter_context(nc.Block())

        @block.sync
        def _(sp):
            def load(src, k):
                sp.dma_start(ring[:, k % RING, :], src).then_inc(slot_loaded[k % RING], 16)

            def stream(name, array, count):
                k0, at = starts[name], 0
                while (array, at) in loaded:
                    at += 1
                loaded.update((array, at + j) for j in range(count))
                done = 0
                while done < min(RING, count):
                    if k0 + done >= RING:
                        sp.wait_ge(*low_bits(k0 + done - RING))
                    load(a[array][at + done], k0 + done)
                    done += 1
                loops = (count - done) // BODY
                if loops:
                    with sp.Fori(0, loops) as i:
                        for j in range(BODY):
                            sp.wait_ge(*low_bits(k0 + j, i))
                            load(a[array][bass.ds(i * BODY + (at + done + j), 1)].rearrange("o p n -> (o p) n"), k0 + done + j)
                    done += BODY * loops
                for j in range(done, count):
                    sp.wait_ge(*low_bits(k0 + j - RING))
                    load(a[array][at + j], k0 + j)

            loaded = set()
            sp.dma_start(xT[:, :], a["x"]).then_inc(g["x_loaded"], 16)
            sp.dma_start(gains[:, :], a["gains"]).then_inc(g["tables_loaded"], 16)
            for name, array, count, _ in RUNS:
                stream(name, array, count)
            for j in range(4):
                sp.wait_ge(g["x_ready"], 4 * 5 + j + 1)
                sp.dma_start(out[:, j * 512:(j + 1) * 512], xT[:, j * 512:(j + 1) * 512]).then_inc(g["stored"], 16)
            sp.wait_ge(g["stored"], 64)

        @block.gpsimd
        def _(pool):
            steps = [0]

            def step(ins):
                steps[0] += 1
                ins.then_inc(g["pool_step"], 1)

            def settle():
                pool.wait_ge(g["pool_step"], steps[0])

            step(pool.memset(zeros[:, :], 0.0))
            step(pool.memset(ones[:, :], 1.0))
            step(pool.memset(ident[:, :], 0.0))
            step(pool.memset(halves[:, :], 0.0))
            step(pool.iota(sco[:, 0:P], [[1, P]], base=0, channel_multiplier=0, allow_small_or_imprecise_dtypes=True))
            step(pool.iota(e_si, [[0, P]], base=0, channel_multiplier=1))
            step(pool.iota(e_ti, [[1, P]], base=0, channel_multiplier=0))
            step(pool.memset(e_reset, 1.0))
            step(pool.memset(e_u, 0.0))
            step(pool.memset(e_at, 0.0))
            settle()
            step(pool.tensor_copy(iota16[:, :], sco[:, 0:P]))
            step(pool.affine_select(out=ident[:, :], in_=ident[:, :], compare_op=ALU.not_equal, fill=1.0,
                                    base=0, pattern=[[-1, P]], channel_multiplier=1))
            step(pool.memset(halves[0:64, 0:64], 1.0))
            settle()
            step(pool.memset(halves[64:128, 64:128], 1.0))
            settle()
            step(pool.memset(b3(e_reset, NCH)[:, :, 0:1], 0.0))
            settle()
            pool.memset(eps[:, :], EPS).then_inc(g["consts"], 1)

            def low(k, i=0, w=0):
                pool.wait_ge(g["w_hi_done"], i * BODY + (k + 1))
                pool.tensor_tensor(w_lo[:, k % RING, :], ring[:, k % RING, :], w_hi[:, k % RING, :].bitcast(F32),
                                   ALU.subtract).then_inc(g["lo_pool"], 1)

            def scale(layer, m, i=0):
                count, t0 = 2 * (T // GROUP_T) * layer + m, i * (3 * GROUP_T) + (m % (T // GROUP_T)) * GROUP_T
                parts = [b3(x, GROUP_T) for x in hot1[count % 3]]
                pool.wait_ge(g["matched"], i * 3 + (count + 1))
                for p in range(3):
                    of_token = g_part[p][:, bass.ds(t0, GROUP_T)].rearrange("p (t o) -> p t o", o=1)
                    last = pool.tensor_tensor(parts[p], parts[2], of_token.to_broadcast([P, GROUP_T, HALF]), ALU.mult)
                last.then_inc(g["first_hot"], 1)

            def lows(name, first, end):
                k0 = starts[name] + first
                loops = (end - first) // BODY
                if loops > 1:
                    with pool.Fori(0, loops) as i:
                        for j in range(BODY):
                            low(k0 + j, i)
                else:
                    loops = 0
                for j in range(BODY * loops, end - first):
                    low(k0 + j)

            lows("ev_in", 0, 21)
            lows("ev_out", 0, 8)
            for layer in range(2):
                lows(f"wq{layer}", 0, 16)
                lows(f"u{layer}", 0, HALF)
                groups = T // GROUP_T
                pool.wait_ge(g["turned"], 3 * (layer + 1))
                for half in range(2):
                    scale(layer, groups * half)
                    scale(layer, groups * half + 1)
                    with pool.Fori(0, groups // 3) as i:
                        for q in range(3):
                            scale(layer, groups * half + q + 2, i)

                if layer == 0:
                    lows("od_in", 0, 2)
                    pool.wait_ge(g["x_ready"], 4 * 2)
                    for tab in (o_left, o_right):
                        step(pool.memset(tab, 0.0))
                    step(pool.memset(causal, 0.0))
                    settle()
                    for tab, rows in ((o_left, 0), (o_left, 64), (o_right, 32), (o_right, 96)):
                        v = tab.rearrange("p (h t) -> p h t", h=FH)[rows:rows + 32]
                        step(pool.affine_select(out=v, in_=v, compare_op=ALU.not_equal, fill=1.0, base=0,
                                                pattern=[[-1, FH], [0, T]], channel_multiplier=1))
                        settle()
                    for c in (0, 2):
                        v = causal[:, c * P:(c + 1) * P]
                        step(pool.affine_select(out=v, in_=v, compare_op=ALU.is_ge, fill=-1e30, base=0,
                                                pattern=[[-1, P]], channel_multiplier=1))
                    settle()
                    pool.memset(neg_row[:, 0:1], 0.0).then_inc(g["od_sel"], 1)
                    lows("od_in_c", 0, 11)
                    lows("od_out", 0, 8)
                else:
                    lows("sb_in", 0, 11)
                    pool.wait_ge(g["x_ready"], 4 * 4)
                    for c, base in ((0, 0), (1, P), (2, 0)):
                        step(pool.iota(dist[:, c * P:(c + 1) * P], [[-1, P]], base=base, channel_multiplier=1,
                                       allow_small_or_imprecise_dtypes=True))
                    settle()
                    for c in (0, 2):
                        v = dist[:, c * P:(c + 1) * P]
                        step(pool.affine_select(out=v, in_=v, compare_op=ALU.is_ge, fill=FAR, base=0,
                                                pattern=[[-1, P]], channel_multiplier=1))
                    v = dist[:, P:2 * P]
                    step(pool.affine_select(out=v, in_=v, compare_op=ALU.is_gt, fill=FAR, base=0,
                                            pattern=[[1, P]], channel_multiplier=-1))
                    pool.wait_ge(g["sb_tables_loaded"], 16 * 5)
                    v = s_ws.rearrange("p (g i) -> p g i", g=SG)
                    step(pool.affine_select(out=v, in_=v, compare_op=ALU.is_ge, fill=0.0, base=0,
                                            pattern=[[0, SG], [1, P]], channel_multiplier=-1))
                    settle()
                    pool.memset(neg_row[:, 0:1], 0.0).then_inc(g["sgu_w_ready"], 1)
                    lows("sb_in", 11, 31)
                    lows("sb_ab", 0, 8)
                    lows("sb_out", 0, 8)
                    lows("up", 0, 2 * FC)
                    lows("down", 0, RING)

        @block.scalar
        def _(act):
            n, u = [0], [0]
            nh, xh = [0], [0]
            A = nc.scalar.activation

            def high(k, i=0):
                act.wait_ge(slot_loaded[k % RING], i * (16 * BODY // RING) + 16 * (k // RING + 1))
                if k >= RING:
                    act.wait_ge(g["pieces_used"], i * BODY + (k - RING + 1))
                A(w_hi[:, k % RING, :], ring[:, k % RING, :], ACT.Copy).then_inc(g["w_hi_done"], 1)

            def highs(to):
                while nh[0] < min(to, total_pieces):
                    high(nh[0])
                    nh[0] += 1

            def split(src, ready):
                if n[0]:
                    act.wait_ge(g["pieces_used"], n[0])
                for j in range(4):
                    ready(j)
                    A(x_hi[:, j * 512:(j + 1) * 512], src[:, j * 512:(j + 1) * 512], ACT.Copy).then_inc(g["x_hi_done"], 1)

            def roots(pairs, count, log, done, value, sums_ready=None):
                for k, (dst, sums) in enumerate(pairs):
                    if sums_ready:
                        act.wait_ge(g[sums_ready], value + k + 1)
                    A(dst, sums, ACT.Ln, bias=eps[:, 0:1], scale=1.0 / count).then_inc(g[log], 1)
                for k, (dst, _) in enumerate(pairs):
                    act.wait_ge(g[log], value + k + 1)
                    A(dst, dst, ACT.Exp, scale=-0.5).then_inc(g[done], 1)

            def norm(k):
                if k == 0:
                    act.wait_ge(g["consts"], 1)
                for j in range(4):
                    if k == 0:
                        if j == 0:
                            act.wait_ge(g["x_loaded"], 16)
                    else:
                        act.wait_ge(g["x_ready"], 4 * (k - 1) + j + 1)
                    A(sq[:, j * 512:(j + 1) * 512], xT[:, j * 512:(j + 1) * 512], ACT.Square).then_inc(g["norm_squared"], 1)
                act.wait_ge(g["norm_summed"], k + 1)
                roots([(rr, bank[4][:, 0:T])], D, "norm_log", "norm_root", k)
                split(h32, lambda j: act.wait_ge(g["h_ready"], KC * k + 2 * j + 2))

            def unit(outs, func=ACT.Copy, pieces=2, scale=1.0, view=None):
                n[0] += pieces
                highs(n[0] + 2)
                act.wait_ge(g["pieces_used"], n[0])
                src = unit_bank(u[0])[:, 0:pieces * T]
                if view:
                    src = view(src)
                A(outs, src, func, scale=scale).then_inc(g["units_out"], 1)
                u[0] += 1

            def token_major(dst, width, j):
                return dst.rearrange("p (b n) -> p b n", b=TB)[:, :, j * T:(j + 1) * T]

            def unit_loop(units, dst_of, func=ACT.Copy):
                loops = units // UNITS
                highs(n[0] + 2)
                if loops:
                    with act.Fori(0, loops) as i:
                        for q in range(UNITS):
                            for j in range(2):
                                high(n[0] + 2 * q + 2 + j, i)
                            act.wait_ge(g["pieces_used"], i * BODY + (n[0] + 2 * q + 2))
                            A(dst_of(i, q), unit_bank(u[0] + q)[:, :], func).then_inc(g["units_out"], 1)
                n[0] += BODY * loops
                nh[0] += BODY * loops
                u[0] += UNITS * loops
                for q in range(units % UNITS):
                    unit(dst_of(loops, q), func)

            def others(pieces):
                n[0] += pieces
                highs(n[0] + 2)

            def accumulated(count, src, ready, first=True, then=None):
                if first:
                    act.wait_ge(g["pieces_used"], n[0])
                ready()

                def chunk(k, i=0):
                    A(x_hi[:, ((n[0] + k) % RING) * T:((n[0] + k) % RING + 1) * T], src(k, i), ACT.Copy).then_inc(g["ax_hi"], 1)

                for k in range(RING):
                    highs(n[0] + k + 1)
                    chunk(k)
                if then:
                    then()
                loops = (count - RING) // BODY
                with act.Fori(0, loops) as i:
                    for j in range(BODY):
                        high(n[0] + RING + j, i)
                        chunk(RING + j, i)
                nh[0] += BODY * loops
                for k in range(RING + BODY * loops, count):
                    highs(n[0] + k + 1)
                    chunk(k)
                n[0] += count
                highs(n[0] + 2)

            act.dma_start(ev_small[:, 0:139], a["ev_small"]).then_inc(g["ev_tables_loaded"], 16)
            act.dma_start(w_gate2[0:RANK, :], a["w_gate2"]).then_inc(g["ev_tables_loaded"], 16)
            act.dma_start(qk_gain[:, :], a["qk_gain"]).then_inc(g["tables_loaded"], 16)
            act.dma_start(sinks[:, :], a["sinks"]).then_inc(g["tables_loaded"], 16)
            act.dma_start(keysb, a["keys0"]).then_inc(g["keys_loaded"], 16)

            highs(2)
            norm(G_EV)
            unit(e_glr[:, :], pieces=1)
            laid = [0]

            def lay_taps(count):
                for w in range(laid[0], min(laid[0] + count, CONV_W)):
                    A(tap_diag[w], ident[:, :], ACT.Copy, scale=cw[:, w * CC + CC - 1:w * CC + CC]).then_inc(g["taps_laid"], 1)
                laid[0] += count

            act.wait_ge(g["ev_tables_loaded"], 32)
            unit(e_q, scale=DK ** -0.5)
            lay_taps(5)
            unit(e_k)
            lay_taps(5)
            act.wait_ge(g["ev_z_in"], 2)
            A(e_az, e_zb, ACT.Abs).then_inc(g["act_step"], 1)
            act.wait_ge(g["act_step"], 1)
            A(e_az, e_az, ACT.Exp, scale=-1.0).then_inc(g["act_step"], 1)
            act.wait_ge(g["act_step"], 2)
            A(e_ln, e_az, ACT.Ln, bias=1.0).then_inc(g["ev_z_log"], 1)
            unit(e_val[:, 0:512])
            act.wait_ge(g["ev_decay_part"], 2)
            A(e_eb, e_b, ACT.Exp).then_inc(g["ev_expb"], 1)
            act.wait_ge(g["ev_fade"], 1)
            A(e_kd, e_nd, ACT.Exp).then_inc(g["ev_expk"], 1)

            def level(lv):
                act.wait_ge(g["ev_dif"], 2 * lv + 2)
                if lv >= 2:
                    act.wait_ge(g["ev_qk_level"], 2 * (lv - 1))
                A(e_exp[lv % 2], e_dif[lv % 2], ACT.Exp).then_inc(g["ev_difexp"], 1)

            level(0)
            level(1)
            unit(e_val[:, 512:1024])
            lay_taps(5)
            level(2)
            unit(e_sig[:, 0:512], ACT.Sigmoid)
            lay_taps(6)
            level(3)
            unit(e_sig[:, 512:1024], ACT.Sigmoid)
            lay_taps(6)
            level(4)
            unit(e_r[:, 0:512], ACT.Silu)
            lay_taps(6)
            level(5)
            unit(e_r[:, 512:1024], ACT.Silu)
            for j in range(2):
                unit(token_major(e_v, 512, j), view=lambda s: b3(s, TB))
            act.wait_ge(g["ev_kdec_turned"], 1)
            A(e_kdt, bank[0][:, :], ACT.Copy).then_inc(g["ev_kdt"], 1)
            act.wait_ge(g["ev_o_out"], 2)
            A(e_osq, e_o, ACT.Square).then_inc(g["ev_o_sq"], 1)
            act.wait_ge(g["ev_o_sum"], 1)
            roots([(e_orr[:, r * 512:(r + 1) * 512], bank[4 + r][:, :]) for r in range(2)], DV, "ev_o_log", "ev_o_root", 0)
            act.wait_ge(g["ln_centred"], 4)
            A(e_sq2, e_xc, ACT.Square).then_inc(g["ln_sq"], 1)
            act.wait_ge(g["ln_var"], 1)
            roots([(e_mu[:, 0:T], bank[3][:, 0:T])], CONV_CH, "ln_log", "ln_root", 0)
            act.wait_ge(g["ln_normed"], 1)
            for c in range(CC):
                A(e_y[:, c * T:(c + 1) * T], e_xn[:, c * T:(c + 1) * T], ACT.Silu, bias=lnb[:, c:c + 1],
                  scale=lng[:, c:c + 1]).then_inc(g["ev_ya"], 1)
            split(e_y, lambda j: act.wait_ge(g["ev_ya"] if j < 2 else g["ev_y"], 2 * j + 2 if j < 2 else 2))
            others(8)

            def experts(layer):
                norm(1 + 2 * layer)
                unit_loop(8, lambda i, q: big[:, bass.ds(i * 1536 + q * 512, 512)])
                for s in range(8):
                    act.wait_ge(g["key_scored"], 8 * layer + s + 1)
                    A(sco[:, s * 512:(s + 1) * 512], bank[4 + s % 4][:, :], ACT.Copy).then_inc(g["scores_out"], 1)
                unit_loop(24, lambda i, q: big[:, bass.ds(i * 1536 + q * 512, 512)], ACT.Gelu)
                for tb in range(TB):
                    act.wait_ge(g["gate_shifted"], TB * layer + tb + 1)
                    v = slot3[:, (2 * TB + tb) * P:(2 * TB + tb + 1) * P]
                    A(v, v, ACT.Exp).then_inc(g["gate_exped"], 1)
                unit_loop(40, lambda i, q: big[:, bass.ds(i * 1536 + (24 * 512 + q * 512), 512)], ACT.Gelu)
                for half in range(2):
                    accumulated(HALF, lambda k, i: big[:, bass.ds(i * BODY * T + (HALF * half + k) * T, T)],
                                lambda: act.wait_ge(g["gated"], 64 * layer + 32 * (half + 1)), half == 0)

            def attention(p, filler):
                def exps(h):
                    S, PR, sm = p["s"][h % 2], p["p"][h % 2], p["small"][:, (h % 2) * 8:(h % 2) * 8 + 8]
                    act.wait_ge(g["at_masked"], p["base"] + h + 1)
                    A(PR[:, 0:P], S[:, 0:P], ACT.Exp, bias=sm[:, 0:1], accum_out=sm[:, 2:3])
                    last = A(PR[:, P:3 * P], S[:, P:3 * P], ACT.Exp, bias=sm[:, 1:2], accum_out=sm[:, 3:4])
                    if p["tag"]:
                        last = A(sm[:, 4:6], sm[:, 0:2], ACT.Exp, bias=sinks[:, h:h + 1])
                    last.then_inc(g["at_exped"], 1)

                exps(0)
                for h in range(p["heads"]):
                    c = p["base"] + h
                    if h + 1 < p["heads"]:
                        exps(h + 1)
                    filler(h)
                    act.wait_ge(g["at_turned"], c + 1)
                    if h >= 2:
                        act.wait_ge(g["at_mixed"], c - 1)
                    A(p["pt"][h % 2], bank[6][:, 0:3 * P], ACT.Copy).then_inc(g["at_pt"], 1)
                    if h % 2:
                        act.wait_ge(g["at_mixed"], c + 1)
                        A(p["y"][:, h // 2, :], bank[7][:, 0:T], ACT.Copy).then_inc(g["at_y"], 1)

            experts(0)

            act.wait_ge(g["x_ready"], 4 * 2)
            act.dma_start(o_fb[:, 0:1], a["od_fb"]).then_inc(g["od_tables_loaded"], 16)
            act.dma_start(keysb, a["keys1"]).then_inc(g["keys_loaded"], 16)
            norm(G_OD)
            unit_loop(8, lambda i, q: o_qk[:, bass.ds(i * 1536 + q * 512, 512)])
            unit(o_z[0], pieces=1)
            act.wait_ge(g["od_z_in"], 1)
            A(o_z[1], o_z[0], ACT.Abs).then_inc(g["act_step"], 1)
            act.wait_ge(g["act_step"], 3)
            A(o_z[1], o_z[1], ACT.Exp, scale=-1.0).then_inc(g["act_step"], 1)
            act.wait_ge(g["act_step"], 4)
            A(o_z[2], o_z[1], ACT.Ln, bias=1.0).then_inc(g["od_z_log"], 1)
            act.wait_ge(g["units_out"], u[0])
            for j in range(4):
                for s in (2 * j, 2 * j + 1):
                    A(o_sq[:, s * 512:(s + 1) * 512], o_qk[:, s * 512:(s + 1) * 512], ACT.Square).then_inc(g["od_sq"], 1)
                unit(token_major(o_v, D, j), view=lambda s: b3(s, TB))
                roots([(o_n[:, s * 512:(s + 1) * 512], bank[4 + s % 4][:, :]) for s in (2 * j, 2 * j + 1)], HD,
                      "od_log", "od_root", 2 * j, "od_sum")
            attention(odd_att, lambda h: None)
            act.wait_ge(g["at_y"], 8)
            split(o_y, lambda j: None)
            others(8)

            experts(1)

            act.wait_ge(g["x_ready"], 4 * 4)
            act.dma_start(s_ws, a["sb_ws"]).then_inc(g["sb_tables_loaded"], 16)
            act.dma_start(s_bs, a["sb_bs"]).then_inc(g["sb_tables_loaded"], 16)
            act.dma_start(s_norm, a["sb_norm"]).then_inc(g["sb_tables_loaded"], 16)
            act.dma_start(f_cw, a["ff_cw"]).then_inc(g["sb_tables_loaded"], 16)
            act.dma_start(f_cb, a["ff_cb"]).then_inc(g["sb_tables_loaded"], 16)
            norm(G_MIX2)
            for s in range(3):
                unit(s_qk[:, s * 512:(s + 1) * 512])
            unit(s_v, pieces=1)
            act.wait_ge(g["units_out"], u[0])
            for s in range(3):
                A(s_sq[:, s * 512:(s + 1) * 512], s_qk[:, s * 512:(s + 1) * 512], ACT.Square).then_inc(g["sb_sq"], 1)
            for j in range(2):
                unit(token_major(s_gv, 512, j), ACT.Gelu_apprx_tanh, view=lambda s: b3(s, TB))
            for j in range(2):
                unit(s_u[:, j * 512:(j + 1) * 512], ACT.Gelu_apprx_tanh)
            roots([(s_n[:, s * 512:(s + 1) * 512], bank[4 + s][:, :]) for s in range(3)], HD,
                  "sb_log", "sb_root", 0, "sb_sum")
            def gate_unit(h):
                unit(s_gate[:, h * 512:(h + 1) * 512], ACT.Sigmoid)

            gate_unit(0)
            act.wait_ge(g["sgu_mean"], 1)
            A(s_small[:, 4:6], s_small[:, 2:4], ACT.Sqrt).then_inc(g["sgu_root"], 1)
            gate_unit(1)
            gate_unit(2)
            attention(swa_att, lambda h: gate_unit(h + 3) if h < 5 else None)
            act.wait_ge(g["at_y"], 8 + 4)
            act.wait_ge(g["sgu_y"], 1)
            split(big[:, at_y:at_y + 8 * T], lambda j: None)
            others(8)
            split(s_m, lambda j: act.wait_ge(g["merged"], 2 * j + 2))
            others(8)

            norm(G_FFN2)

            def z_out(m, i=0):
                act.wait_ge(g["pieces_used"], i * BODY + (n[0] + 2 * m + 2))
                act.wait_ge(g["ff_gated"], i * UNITS + (m + 1))
                A(b3(f_z[m % 3], 2)[:, :, 2:ZW], b3(unit_bank(u[0] + m)[:, :], 2), ACT.Copy).then_inc(g["units_out"], 1)

            def silu(m, i=0):
                act.wait_ge(g["ff_z"], i * UNITS + (m + 1))
                A(f_sil[m % 3], f_zc[m % 3][:, 0:T], ACT.Silu).then_inc(g["ff_silu"], 1)

            highs(n[0] + 4)
            z_out(0)
            loops = (FC - 1) // UNITS
            with act.Fori(0, loops) as i:
                for m in range(UNITS):
                    for j in range(2):
                        high(n[0] + 2 * m + 4 + j, i)
                    z_out(m + 1, i)
                    silu(m, i)
            nh[0] += BODY * loops
            for m in range(UNITS * loops, FC - 1):
                highs(n[0] + 2 * m + 6)
                z_out(m + 1)
                silu(m)
            n[0] += 2 * FC

            def last_unit():
                silu(FC - 1)
                act.wait_ge(g["ff_gated"], UNITS + FC)

            accumulated(FC, lambda k, i: f_act[:, bass.ds(i * BODY * T + k * T, T)],
                        lambda: act.wait_ge(g["ff_gated"], UNITS + RING), then=last_unit)

        @block.vector
        def _(dve):
            V = nc.vector
            steps = [0]
            n, u = [0], [0]

            def step(ins):
                steps[0] += 1
                ins.then_inc(g["dve_step"], 1)

            def settle():
                dve.wait_ge(g["dve_step"], steps[0])

            xs, ax = [0], [0]

            def low_pair(src, j):
                dve.wait_ge(g["x_hi_done"], 4 * xs[0] + j + 1)
                c = slice(j * 512, (j + 1) * 512)
                V.tensor_tensor(x_lo[:, c], src[:, c], x_hi[:, c].bitcast(F32), ALU.subtract).then_inc(g["x_lo_done"], 1)

            def lows_of(src):
                for j in range(4):
                    low_pair(src, j)
                xs[0] += 1

            def low(k, i=0):
                dve.wait_ge(g["w_hi_done"], i * BODY + (k + 1))
                V.tensor_tensor(w_lo[:, k % RING, :], ring[:, k % RING, :], w_hi[:, k % RING, :].bitcast(F32),
                                ALU.subtract).then_inc(g["lo_dve"], 1)

            def chunk(k0, k, src, i=0):
                dve.wait_ge(g["ax_hi"], i * BODY + (ax[0] + k + 1))
                c = slice(((k0 + k) % RING) * T, ((k0 + k) % RING + 1) * T)
                V.tensor_tensor(x_lo[:, c], src(k, i), x_hi[:, c].bitcast(F32), ALU.subtract).then_inc(g["ax_lo"], 1)

            def accumulated(name, count, src, then=None):
                k0 = starts[name]
                for k in range(RING):
                    if by_dve[k0 + k]:
                        low(k0 + k)
                    chunk(k0, k, src)
                if then:
                    then()
                loops = (count - RING) // BODY
                with dve.Fori(0, loops) as i:
                    for j in range(BODY):
                        low(k0 + RING + j, i)
                        chunk(k0, RING + j, src, i)
                for k in range(RING + BODY * loops, count):
                    low(k0 + k)
                    chunk(k0, k, src)
                ax[0] += count

            acc = [0]

            def norm(k):
                dve.wait_ge(g["norm_root"], k + 1)
                for j in range(5):
                    if j < 4:
                        for c in (2 * j, 2 * j + 1):
                            V.scalar_tensor_tensor(b3(h32, KC)[:, c, :], xv[:, c, :], gains[:, k * KC + c:k * KC + c + 1], rr,
                                                   ALU.mult, ALU.mult).then_inc(g["h_ready"], 1)
                    if j:
                        low_pair(h32, j - 1)
                xs[0] += 1

            def residual(pieces, each):
                n[0] += pieces
                for j in range(4):
                    if each or j == 3:
                        dve.wait_ge(g["pieces_used"], n[0] - (6 - 2 * j if each else 0))
                    else:
                        dve.wait_ge(g["bank_done"], 3 * acc[0] + j + 1)
                    v = xT[:, j * 512:(j + 1) * 512]
                    V.tensor_tensor(v, bank[4 + j][:, :], v, ALU.add).then_inc(g["x_ready"], 1)
                acc[0] += not each

            dve.wait_ge(g["consts"], 1)
            step(V.tensor_tensor(e_xr[:, 0:P], e_si, e_ti, ALU.bitwise_xor))
            settle()
            for lv, m in enumerate(LEVELS):
                sh = m.bit_length() - 1
                step(V.tensor_scalar(e_xr[:, P:2 * P], e_xr[:, 0:P], sh, None, ALU.arith_shift_right))
                settle()
                step(V.tensor_scalar(e_mask[:, 6 * P:7 * P], e_ti, sh, 1, ALU.arith_shift_right, ALU.bitwise_and))
                step(V.tensor_scalar(e_mask[:, lv * P:(lv + 1) * P], e_xr[:, P:2 * P], 1.0, None, ALU.is_equal))
                settle()
                step(V.tensor_tensor(e_mask[:, lv * P:(lv + 1) * P], e_mask[:, lv * P:(lv + 1) * P],
                                     e_mask[:, 6 * P:7 * P], ALU.bitwise_and))
            settle()
            step(V.tensor_scalar(e_mask[:, 6 * P:7 * P], e_xr[:, 0:P], 0.0, None, ALU.is_equal))

            dve.wait_ge(g["tables_loaded"], 48)
            norm(G_EV)
            n[0] += 21
            dve.wait_ge(g["ev_z_ready"], 1)
            for f in range(2):
                V.tensor_scalar(e_zb[:, f * T:(f + 1) * T], bank[5][:, f * T:(f + 1) * T], gb[:, f:f + 1], None,
                                ALU.add).then_inc(g["ev_z_in"], 1)
            dve.wait_ge(g["ev_z_in"], 2)
            step(V.tensor_scalar(e_mn, e_zb, 0.0, 1.0 / TAU, ALU.min, ALU.mult))
            settle()
            dve.wait_ge(g["ev_z_log"], 1)
            step(V.scalar_tensor_tensor(e_la, e_ln, -1.0 / TAU, e_mn, ALU.mult, ALU.add))
            settle()
            for f in range(2):
                V.tensor_tensor_scan(e_b[:, f * T:(f + 1) * T], e_reset, e_la[:, f * T:(f + 1) * T], 0.0,
                                     ALU.mult, ALU.add).then_inc(g["ev_decay_part"], 1)
            dve.wait_ge(g["ev_decay_part"], 2)
            b8 = b3(e_b, 2 * NCH)
            V.tensor_tensor(b3(e_nd, 2 * NCH), b8[:, :, CHUNK - 1:CHUNK].to_broadcast([P, 2 * NCH, CHUNK]), b8,
                            ALU.subtract).then_inc(g["ev_fade"], 1)
            atv = e_at.rearrange("p (r c t) -> p r c t", r=2, t=P)

            def take(lv):
                if lv:
                    dve.wait_ge(g["ev_level_in"], 2 * lv)
                for r in range(2):
                    dve.wait_ge(g["ev_level"], lv + 1)
                    V.copy_predicated(atv[:, r], e_mask[:, lv * P:(lv + 1) * P].rearrange("p (o t) -> p o t", o=1).to_broadcast([P, 4, P]),
                                      b3(bank[4 + 2 * (lv % 2) + r][:, :], 4)).then_inc(g["ev_level_in"], 1)

            cv, uv = b3(e_conv, CC), e_u.rearrange("p (c t) -> p c t", c=CC)

            def first_tap():
                dve.wait_ge(g["units_out"], 7)
                V.tensor_tensor(uv[:, :, CONV_W - 1:UW], b3(e_val, CC), b3(e_sig, CC), ALU.mult).then_inc(g["conv_input"], 1)
                dve.wait_ge(g["conv_input"], 1)
                dve.wait_ge(g["ev_tables_loaded"], 32)
                for c in range(CC - 1):
                    V.tensor_scalar(cv[:, c, :], uv[:, c, 0:T], cw[:, c:c + 1], cb[:, c:c + 1], ALU.mult,
                                    ALU.add).then_inc(g["conv_step"], 1)

            def taps(first, end):
                with dve.Fori(first, end) as i:
                    for w in range(2):
                        for c in range(CC - 1):
                            dve.wait_ge(g["conv_step"], i * 2 * (CC - 1) + (w * (CC - 1) + c + 1))
                            V.scalar_tensor_tensor(cv[:, c, :], e_u[:, bass.ds(i * 2 + (c * UW + w + 1), T)],
                                                   cw[:, bass.ds(i * 2 * CC + ((w + 1) * CC + c), 1)], cv[:, c, :],
                                                   ALU.mult, ALU.add).then_inc(g["conv_step"], 1)

            for lv, m in enumerate(LEVELS):
                if lv >= 2:
                    dve.wait_ge(g["ev_difexp"], lv - 1)
                bm = e_b.rearrange("p (a m) -> p a m", m=2 * m)
                dm = e_dif[lv % 2].rearrange("p (a m) -> p a m", m=2 * m)
                ref = bm[:, :, m - 1:m].to_broadcast([P, 2 * T // (2 * m), m])
                V.tensor_tensor(dm[:, :, 0:m], ref, bm[:, :, 0:m], ALU.subtract).then_inc(g["ev_dif"], 1)
                V.tensor_tensor(dm[:, :, m:2 * m], bm[:, :, m:2 * m], ref, ALU.subtract).then_inc(g["ev_dif"], 1)
                if lv == 4:
                    first_tap()
                if lv >= 4:
                    taps(3 * lv - 12, 3 * lv - 9)
                dve.wait_ge(g["ev_difexp"], lv + 1)
                if lv == 0:
                    dve.wait_ge(g["units_out"], 3)
                if lv >= 2:
                    dve.wait_ge(g["ev_level"], lv - 1)
                V.tensor_tensor(e_qe[lv % 2], e_q, e_exp[lv % 2], ALU.mult).then_inc(g["ev_qk_level"], 1)
                V.tensor_tensor(e_ke[lv % 2], e_k, e_exp[lv % 2], ALU.mult).then_inc(g["ev_qk_level"], 1)
                if lv >= 1:
                    take(lv - 1)
            dve.wait_ge(g["ev_expk"], 1)
            V.tensor_tensor(e_kd, e_k, e_kd, ALU.mult).then_inc(g["ev_kdec"], 1)
            dve.wait_ge(g["ev_expb"], 1)
            V.tensor_tensor(e_qb, e_q, e_eb, ALU.mult).then_inc(g["ev_kdec"], 1)
            take(5)
            take(6)
            taps(6, 8)
            dve.wait_ge(g["ev_chunk_sums"], 1)
            st = e_state.rearrange("p (c f n) -> p c f n", c=3, f=2)
            step(V.tensor_copy(st[:, 0], bank[1][:, 0:256].rearrange("p (f n) -> p f n", f=2)))
            settle()
            for c, src in ((1, bank[2][:, 0:256]), (2, bank[1][:, 256:512])):
                for f in range(2):
                    e = f * T + c * CHUNK + CHUNK - 1
                    step(V.scalar_tensor_tensor(st[:, c, f], st[:, c - 1, f], e_eb[:, e:e + 1], src[:, f * DV:(f + 1) * DV],
                                                ALU.mult, ALU.add))
                settle()
            V.memset(neg_row[:, 0:1], 0.0).then_inc(g["ev_states"], 1)
            taps(8, 10)
            dve.wait_ge(g["ev_o"], 1)
            for r in range(2):
                V.tensor_copy(e_o[:, r * 512:(r + 1) * 512], bank[6 + r][:, :]).then_inc(g["ev_o_out"], 1)
            taps(10, (CONV_W - 1) // 2)
            dve.wait_ge(g["conv_mixed"], 1)
            V.tensor_scalar(cv[:, CC - 1, :], bank[3][:, T:2 * T], cb[:, CC - 1:CC], None, ALU.add).then_inc(g["conv_step"], 1)
            dve.wait_ge(g["ev_o_root"], 2)
            dve.wait_ge(g["ev_o_out"], 2)
            step(V.scalar_tensor_tensor(e_o, e_o, glag, e_orr, ALU.mult, ALU.mult))
            dve.wait_ge(g["ln_sum"], 1)
            for c in range(CC):
                V.scalar_tensor_tensor(b3(e_xc, CC)[:, c, :], bank[3][:, 0:T], -1.0 / CONV_CH, cv[:, c, :],
                                       ALU.mult, ALU.add).then_inc(g["ln_centred"], 1)
            settle()
            dve.wait_ge(g["units_out"], 11)
            for r in range(2):
                dst = e_y[:, 4 * T:8 * T].rearrange("p (f r t) -> p r f t", f=2, r=2)[:, r]
                gate = e_r.rearrange("p (f r t) -> p r f t", f=2, r=2)[:, r]
                V.tensor_tensor(dst, e_o[:, r * 512:(r + 1) * 512].rearrange("p (f t) -> p f t", f=2), gate,
                                ALU.mult).then_inc(g["ev_y"], 1)
            dve.wait_ge(g["ln_root"], 1)
            V.tensor_tensor(b3(e_xn, CC), b3(e_xc, CC),
                            e_mu[:, 0:T].rearrange("p (o t) -> p o t", o=1).to_broadcast([P, CC, T]),
                            ALU.mult).then_inc(g["ln_normed"], 1)
            u[0] = 11
            lows_of(e_y)
            residual(8, True)

            def top16(vals, idx, src, groups, width):
                def at(ap, j, half):
                    return ap[:, j * 16 + 8 * half:j * 16 + 8 * half + 8]

                def row(j):
                    return src[:, j * width:(j + 1) * width]

                for half in range(2):
                    for j in range(groups):
                        step(V.max(at(vals, j, half), row(j)))
                    settle()
                    for j in range(groups):
                        step(V.max_index(at(idx, j, half), at(vals, j, half), row(j)))
                    if not half:
                        settle()
                        for j in range(groups):
                            step(V.match_replace(row(j), at(vals, j, 0), row(j), NEG_BIG))
                        settle()

            def experts(layer):
                norm(1 + 2 * layer)
                n[0] += 16 + NK
                for tb in range(TB):
                    dve.wait_ge(g["scores_out"], 8 * layer + 4 * (tb + 1))
                    top16(top_v[:, tb * 256:(tb + 1) * 256], top_i[:, tb * 256:(tb + 1) * 256],
                          sco[:, tb * 2048:(tb + 1) * 2048], 16, NK)
                settle()
                step(V.tensor_copy(top_if, top_i))
                cand, oh = sco[:, 0:2048], sco[:, 2048:4096]
                for tb in range(TB):
                    tv = top_v[:, tb * 256:(tb + 1) * 256].rearrange("p (h c k) -> p h c k", h=PH, c=2)
                    ti = top_if[:, tb * 256:(tb + 1) * 256].rearrange("p (h c k) -> p h c k", h=PH, c=2)
                    settle()
                    for h in range(PH):
                        step(V.tensor_tensor(cand[:, h * 256:(h + 1) * 256].rearrange("p (a b) -> p a b", a=16),
                                             tv[:, h, 0, :].rearrange("p (k o) -> p k o", o=1).to_broadcast([P, 16, 16]),
                                             tv[:, h, 1, :].rearrange("p (o k) -> p o k", o=1).to_broadcast([P, 16, 16]), ALU.add))
                    settle()
                    top16(cand_v, cand_i, cand, PH, 256)
                    settle()
                    step(V.tensor_scalar(rank_u[:, 0:P], cand_i, 4, None, ALU.logical_shift_right))
                    step(V.tensor_scalar(rank_u[:, P:2 * P], cand_i, 15, None, ALU.bitwise_and))
                    settle()
                    step(V.tensor_copy(rank_f, rank_u))
                    for c in range(2):
                        settle()
                        step(V.tensor_tensor(oh.rearrange("p (s k) -> p s k", k=16),
                                             rank_f[:, c * P:(c + 1) * P].rearrange("p (s o) -> p s o", o=1).to_broadcast([P, P, 16]),
                                             iota16[:, 0:16].rearrange("p (o k) -> p o k", o=1).to_broadcast([P, P, 16]), ALU.is_equal))
                        settle()
                        for h in range(PH):
                            v = oh[:, h * 256:(h + 1) * 256].rearrange("p (s k) -> p s k", k=16)
                            step(V.tensor_tensor(v, v, ti[:, h, c, :].rearrange("p (o k) -> p o k", o=1).to_broadcast([P, 16, 16]), ALU.mult))
                        settle()
                        step(V.tensor_reduce(slot3[:, (c * TB + tb) * P:(c * TB + tb + 1) * P],
                                             oh.rearrange("p (s k) -> p s k", k=16), AX.X, ALU.add))
                    cvv = cand_v.rearrange("p (h k) -> p h k", h=PH)
                    V.tensor_tensor(slot3[:, (2 * TB + tb) * P:(2 * TB + tb + 1) * P].rearrange("p (h k) -> p h k", h=PH),
                                    cvv, cvv[:, :, 0:1].to_broadcast([P, PH, 16]), ALU.subtract).then_inc(g["gate_shifted"], 1)
                for tb in range(TB):
                    gt = slot3[:, (2 * TB + tb) * P:(2 * TB + tb + 1) * P].rearrange("p (h k) -> p h k", h=PH)
                    gs = gate_s[:, tb * PH:(tb + 1) * PH]
                    dve.wait_ge(g["gate_exped"], TB * layer + tb + 1)
                    step(V.tensor_reduce(gs, gt, AX.X, ALU.add))
                    settle()
                    step(V.reciprocal(gs, gs))
                    settle()
                    V.tensor_tensor(gt, gt, gs.rearrange("p (h o) -> p h o", o=1).to_broadcast([P, PH, 16]),
                                    ALU.mult).then_inc(g["slots_ready"], 1)
                settle()
                dve.wait_ge(g["slots_turned"], layer + 1)
                V.tensor_copy(e1T, bank[4][:, 0:T]).then_inc(g["turned"], 1)
                V.tensor_copy(e2T, bank[4][:, T:2 * T]).then_inc(g["turned"], 1)
                rest = sco[:, 0:T]
                step(V.tensor_copy(g_part[0], bank[5][:, 0:T]))
                settle()
                step(V.tensor_tensor(rest, bank[5][:, 0:T], g_part[0], ALU.subtract))
                settle()
                step(V.tensor_copy(g_part[1], rest))
                settle()
                V.tensor_tensor(g_part[2], rest, g_part[1], ALU.subtract).then_inc(g["turned"], 1)
                dve.wait_ge(g["turned"], 3 * layer + 3)
                acts = big[:, :].rearrange("p (e t) -> p e t", t=T)
                groups = T // GROUP_T
                base = 2 * groups * layer

                def build(m, i=0):
                    half, t0 = m // groups, i * (3 * GROUP_T) + (m % groups) * GROUP_T
                    if base + m >= 3:
                        dve.wait_ge(g["gates_spread"], i * 3 + (base + m - 2))

                    def match(dst, keys, row):
                        n = keys.shape[1]
                        return V.tensor_tensor(b3(dst, GROUP_T), keys.rearrange("p (o e) -> p o e", o=1).to_broadcast([P, GROUP_T, n]),
                                               row[:, bass.ds(t0, GROUP_T)].rearrange("p (t o) -> p t o", o=1)
                                               .to_broadcast([P, GROUP_T, n]), ALU.is_equal)

                    match(hot1[(base + m) % 3][2], iota16[:, half * HALF:(half + 1) * HALF], e1T).then_inc(g["matched"], 1)
                    match(hot2[(base + m) % 3], iota16[:, :], e2T).then_inc(g["second_hot"], 1)

                def gate(m, i=0):
                    half, t0 = m // groups, i * (3 * GROUP_T) + (m % groups) * GROUP_T
                    dve.wait_ge(g["gates_spread"], i * 3 + (base + m + 1))
                    v = acts[:, half * HALF:(half + 1) * HALF, bass.ds(t0, GROUP_T)]
                    b = m % 3 if half else 4 + m % 3
                    V.tensor_tensor(v, bank[b][:, :].rearrange("p (j e) -> p e j", j=GROUP_T), v, ALU.mult).then_inc(g["gated"], 1)

                u[0] += 8 + 64
                k0 = starts[f"u{layer}b"]
                build(0)
                build(1)
                dve.wait_ge(g["units_out"], u[0] - 32)
                with dve.Fori(0, groups // 3) as i:
                    for q in range(3):
                        low(k0 + 2 * q, i)
                        low(k0 + 2 * q + 1, i)
                        gate(q, i)
                        build(q + 2, i)
                for m in (groups - 2, groups - 1):
                    low(k0 + 2 * m)
                    low(k0 + 2 * m + 1)
                    gate(m)
                build(groups)
                build(groups + 1)
                dve.wait_ge(g["units_out"], u[0])
                k0 += HALF
                src = lambda k, i: big[:, bass.ds(i * BODY * T + k * T, T)]
                for k in range(RING):
                    low(k0 + k)
                    chunk(k0, k, src)
                with dve.Fori(0, groups // 3) as i:
                    for q in range(3):
                        gate(groups + q, i)
                        build(groups + q + 2, i)
                        for k in (2 * q + 3, 2 * q + 4):
                            low(k0 + k, i)
                            chunk(k0, k, src, i)
                gate(2 * groups - 2)
                gate(2 * groups - 1)
                low(k0 + HALF - 1)
                chunk(k0, HALF - 1, src)
                ax[0] += HALF
                accumulated(f"v{layer}b", HALF, lambda k, i: src(HALF + k, i))
                residual(NK, False)

            experts(0)

            def log_sigmoid_rows():
                dve.wait_ge(g["units_out"], u[0] + 9)
                dve.wait_ge(g["od_tables_loaded"], 16)
                V.tensor_scalar(o_z[0], o_z[0], o_fb[:, 0:1], None, ALU.add).then_inc(g["od_z_in"], 1)
                dve.wait_ge(g["od_z_in"], 1)
                step(V.tensor_scalar(o_z[3], o_z[0], 0.0, None, ALU.min))
                settle()
                dve.wait_ge(g["od_z_log"], 1)
                step(V.tensor_tensor(o_z[4], o_z[3], o_z[2], ALU.subtract))
                settle()
                step(V.memset(o_z[0], 1.0))
                settle()
                step(V.tensor_tensor_scan(o_z[5], o_z[0], o_z[4], 0.0, ALU.mult, ALU.add))
                settle()
                dve.wait_ge(g["od_sel"], 1)
                for rows in (0, 64):
                    step(V.tensor_scalar(o_right.rearrange("p (h t) -> p h t", h=FH)[rows:rows + 32],
                                         o_z[5][rows:rows + 32].rearrange("p (o t) -> p o t", o=1).to_broadcast([32, FH, T]),
                                         -1.0, None, ALU.mult))
                    step(V.tensor_copy(o_left.rearrange("p (h t) -> p h t", h=FH)[rows + 32:rows + 48],
                                       o_z[5][rows + 32:rows + 48].rearrange("p (o t) -> p o t", o=1).to_broadcast([16, FH, T])))
                settle()
                V.memset(neg_row[:, 0:1], 0.0).then_inc(g["od_bias_ready"], 1)

            def head_norm(count, raw, dst, gain, root, ready):
                for s in range(count):
                    v = dst[:, s * 512:(s + 1) * 512]
                    dve.wait_ge(g[root], s + 1)
                    V.scalar_tensor_tensor(v, raw[:, s * 512:(s + 1) * 512], gain(s), v, ALU.mult, ALU.mult).then_inc(g[ready], 1)

            def attention(p):
                for h in range(p["heads"] + 1):
                    if h < p["heads"]:
                        c = p["base"] + h
                        S, sm = p["s"][h % 2], p["small"][:, (h % 2) * 8:(h % 2) * 8 + 8]
                        dve.wait_ge(g["at_score"], c + 1)
                        if h >= 2:
                            dve.wait_ge(g["at_exped"], c - 1)
                        step(V.scalar_tensor_tensor(S, p["table"], p["factor"](h), bank[3 + h % 3][:, 0:3 * P],
                                                    ALU.mult, ALU.add))
                        settle()
                        first = V.tensor_reduce(sm[:, 0:1], S[:, 0:P], AX.X, ALU.max, negate=True)
                        step(first)
                        if p["tag"]:
                            step(V.tensor_reduce(sm[:, 1:2], S[:, P:3 * P], AX.X, ALU.max, negate=True))
                            settle()
                            V.tensor_scalar(sm[:, 0:2], sm[:, 0:2], nsink[:, h:h + 1], None, ALU.min).then_inc(g["at_masked"], 1)
                        else:
                            settle()
                            V.tensor_reduce(sm[:, 1:2], S[:, P:3 * P], AX.X, ALU.max, negate=True).then_inc(g["at_masked"], 1)
                    if h >= 1:
                        c = p["base"] + h - 1
                        PR, sm = p["p"][(h - 1) % 2], p["small"][:, ((h - 1) % 2) * 8:((h - 1) % 2) * 8 + 8]
                        dve.wait_ge(g["at_exped"], c + 1)
                        if p["tag"]:
                            step(V.tensor_tensor(sm[:, 2:4], sm[:, 2:4], sm[:, 4:6], ALU.add))
                            settle()
                        step(V.reciprocal(sm[:, 6:8], sm[:, 2:4]))
                        settle()
                        step(V.tensor_scalar(PR[:, 0:P], PR[:, 0:P], sm[:, 6:7], None, ALU.mult))
                        settle()
                        V.tensor_scalar(PR[:, P:3 * P], PR[:, P:3 * P], sm[:, 7:8], None, ALU.mult).then_inc(g["at_prob"], 1)

            norm(G_OD)
            step(V.tensor_scalar(qk_gain[:, 0:1], qk_gain[:, 0:1], HD ** -0.5, None, ALU.mult))
            step(V.tensor_scalar(qk_gain[:, 2:3], qk_gain[:, 2:3], HD ** -0.5, None, ALU.mult))
            for k in range(12):
                low(starts["od_in_b"] + k)
            log_sigmoid_rows()
            head_norm(8, o_qk, o_n, lambda s: qk_gain[:, 0:1] if s < 4 else qk_gain[:, 1:2],
                      "od_root", "od_qk_ready")
            attention(odd_att)
            u[0] += 13
            n[0] += 25
            lows_of(o_y)
            residual(8, True)

            experts(1)

            norm(G_MIX2)
            step(V.tensor_scalar(nsink[:, :], sinks[:, :], -1.0, None, ALU.mult))
            dve.wait_ge(g["sb_tables_loaded"], 80)
            head_norm(3, s_qk, s_n, lambda s: qk_gain[:, 2:3] if s < 2 else qk_gain[:, 3:4],
                      "sb_root", "sb_qk_ready")
            dve.wait_ge(g["units_out"], u[0] + 8)
            for tb in range(TB):
                v = s_gv[:, tb * 512:(tb + 1) * 512]
                step(V.tensor_tensor(s_gv2[:, tb * 512:(tb + 1) * 512], v, v, ALU.mult))
            settle()
            step(V.tensor_reduce(s_small[:, 0:2], b3(s_gv2, TB), AX.X, ALU.add))
            settle()
            V.tensor_scalar(s_small[:, 2:4], s_small[:, 0:2], 1.0 / 512, EPS, ALU.mult, ALU.add).then_inc(g["sgu_mean"], 1)
            dve.wait_ge(g["sgu_root"], 1)
            step(V.reciprocal(s_small[:, 6:8], s_small[:, 4:6]))
            settle()
            for tb in range(TB):
                V.scalar_tensor_tensor(s_vn[:, tb * 512:(tb + 1) * 512], s_gv[:, tb * 512:(tb + 1) * 512],
                                       s_small[:, 6 + tb:7 + tb], s_norm, ALU.mult, ALU.mult).then_inc(g["sgu_v_ready"], 1)
            dve.wait_ge(g["sgu_mixed"], 1)
            for j in range(2):
                step(V.tensor_tensor(s_mix[:, j * 512:(j + 1) * 512].rearrange("p (c b t) -> p c b t", c=2, b=TB),
                                     bank[6 + j][:, :].rearrange("p (c b t) -> p c b t", c=2, b=TB),
                                     s_bs[:, j * 256:(j + 1) * 256].rearrange("p (c o t) -> p c o t", c=2, o=1).to_broadcast([P, 2, TB, P]),
                                     ALU.add))
            settle()
            V.tensor_tensor(s_yb, s_mix, s_u, ALU.mult).then_inc(g["sgu_y"], 1)
            attention(swa_att)
            u[0] += 16
            lows_of(big[:, at_y:at_y + 8 * T])
            dve.wait_ge(g["units_out"], u[0])
            n[0] += 31
            gates = s_gate.rearrange("p (b c t) -> p b c t", b=2, c=KC)
            for c in range(KC):
                dve.wait_ge(g["pieces_used"], n[0] + c + 1)
                pr = s_prod[:, (c % 2) * 512:(c % 2 + 1) * 512]
                V.tensor_tensor(b3(pr, 2), b3(bank[c % 4][:, :], 2), gates[:, :, c, :], ALU.mult).then_inc(g["merged_out"], 1)
                dve.wait_ge(g["merged_out"], c + 1)
                V.tensor_tensor(s_m[:, c * T:(c + 1) * T], pr[:, 0:T], pr[:, T:2 * T], ALU.add).then_inc(g["merged"], 1)
            n[0] += 8
            lows_of(s_m)
            residual(8, True)

            norm(G_FFN2)
            for q in range(UNITS):
                V.memset(b3(f_z[q], 2)[:, :, 0:2], 0.0).then_inc(g["ff_gated"], 1)

            def convolve(m, i=0):
                dve.wait_ge(g["units_out"], i * UNITS + (u[0] + m + 1))
                z, zc = b3(f_z[m % 3], 2), b3(f_zc[m % 3], 2)
                for half in range(2):
                    col = m * 2 + half
                    V.tensor_scalar(zc[:, half, :], z[:, half, 0:T], f_cw[:, bass.ds(i * 18 + 3 * col, 1)],
                                    f_cb[:, bass.ds(i * 6 + col, 1)], ALU.mult, ALU.add).then_inc(g["ff_tap"], 1)
                for tap in (1, 2):
                    dve.wait_ge(g["ff_tap"], i * 12 + (m * 4 + 2 * tap))
                    for half in range(2):
                        col = m * 2 + half
                        ins = V.scalar_tensor_tensor(zc[:, half, :], z[:, half, tap:tap + T],
                                                     f_cw[:, bass.ds(i * 18 + (3 * col + tap), 1)], zc[:, half, :],
                                                     ALU.mult, ALU.add)
                        if tap == 1:
                            ins.then_inc(g["ff_tap"], 1)
                ins.then_inc(g["ff_z"], 1)

            def gate_value(m, i=0):
                dve.wait_ge(g["ff_silu"], i * UNITS + (m + 1))
                V.tensor_tensor(f_act[:, bass.ds(i * UNITS * T + m * T, T)], f_sil[m % 3], f_zc[m % 3][:, T:2 * T],
                                ALU.mult).then_inc(g["ff_gated"], 1)

            convolve(0)
            loops = (FC - 1) // UNITS
            with dve.Fori(0, loops) as i:
                for m in range(UNITS):
                    convolve(m + 1, i)
                    gate_value(m, i)
            for m in range(UNITS * loops, FC - 1):
                convolve(m + 1)
                gate_value(m)
            n[0] += 2 * FC
            accumulated("down", FC, lambda k, i: f_act[:, bass.ds(i * BODY * T + k * T, T)],
                        lambda: gate_value(FC - 1))
            residual(FC, False)

        @block.tensor
        def _(pe):
            n, u = [0], [0]
            mm = nc.tensor.matmul

            def keep_warm(count, unused=3):
                for _ in range(count):
                    mm(bank[unused][:, 0:T], zeros[:, :], ident[:, :].bitcast(BF16), start=True, stop=True)

            def norm(k):
                if k:
                    pe.wait_ge(g["norm_squared"], 4 * k)
                    keep_warm(10)
                for j in range(4):
                    pe.wait_ge(g["norm_squared"], 4 * k + j + 1)
                    for c in (2 * j, 2 * j + 1):
                        last = mm(bank[4][:, 0:T], ones[:, :], sqv[:, c, :], start=(c == 0), stop=(c == KC - 1))
                    if j < 3:
                        keep_warm(3)
                last.then_inc(g["norm_summed"], 1)
                keep_warm(24)

            xs, ax = [0], [0]
            xh, xl = b3(x_hi[:, :], KC), b3(x_lo[:, :], KC)

            def weights(at, i):
                k = n[0] + at
                pe.wait_ge(*low_bits(k, i))
                return w_hi[:, k % RING, :], w_lo[:, k % RING, :]

            def next_split():
                base = 4 * xs[0]
                xs[0] += 1

                def wait(half):
                    return lambda c: None if c % 2 else pe.wait_ge(g[half], base + c // 2 + 1)
                return wait("x_hi_done"), wait("x_lo_done")

            def features(dst, w, ready=None):
                hi, lo = w
                rows = [slice(c * P, (c + 1) * P) for c in range(KC)]
                for c in range(KC):
                    if ready:
                        ready[0](c)
                    mm(dst, hi[:, rows[c]], xh[:, c, :], start=(c == 0), stop=False)
                    mm(dst, lo[:, rows[c]], xh[:, c, :], start=False, stop=False)
                    if not ready:
                        last = mm(dst, hi[:, rows[c]], xl[:, c, :], start=False, stop=(c == KC - 1))
                for c in range(KC if ready else 0):
                    ready[1](c)
                    last = mm(dst, hi[:, rows[c]], xl[:, c, :], start=False, stop=(c == KC - 1))
                return last

            def tokens(dst, w, ready=None):
                hi, lo = w
                for b in range(TB):
                    for c in range(KC):
                        rows, t = slice(c * P, (c + 1) * P), slice(b * P, (b + 1) * P)
                        mm(dst[:, t], xh[:, c, t], hi[:, rows], start=(c == 0), stop=False)
                        mm(dst[:, t], xl[:, c, t], hi[:, rows], start=False, stop=False)
                        last = mm(dst[:, t], xh[:, c, t], lo[:, rows], start=False, stop=(c == KC - 1))
                return last

            def token_unit():
                if u[0] >= UNITS:
                    pe.wait_ge(g["units_out"], u[0] - UNITS + 1)
                for j in range(2):
                    hi, lo = weights(j, 0)
                    for b in range(TB):
                        dst, t = unit_bank(u[0])[:, b * T:(b + 1) * T], slice(b * P, (b + 1) * P)
                        for c in range(4):
                            cols = slice(c * T, (c + 1) * T)
                            first = j == 0 and b == 0 and c == 0
                            mm(dst, xh[:, 4 * j + c, t], hi[:, cols], start=first, stop=False, skip_group_check=True)
                            mm(dst, xl[:, 4 * j + c, t], hi[:, cols], start=False, stop=False, skip_group_check=True)
                            last = mm(dst, xh[:, 4 * j + c, t], lo[:, cols], start=False, stop=False, skip_group_check=True)
                    last.then_inc(g["pieces_used"], 1)
                n[0] += 2
                u[0] += 1

            def unit(make, pieces=2, at=0, q=0, i=0, ready=None):
                if u[0] + q >= UNITS:
                    pe.wait_ge(g["units_out"], i * UNITS + (u[0] + q - UNITS + 1))
                for j in range(pieces):
                    w = weights(at + j, i)
                    make(unit_bank(u[0] + q)[:, j * T:(j + 1) * T], w, ready if j == 0 else None).then_inc(g["pieces_used"], 1)

            def one_unit(make, pieces=2, ready=None):
                unit(make, pieces, ready=ready)
                n[0] += pieces
                u[0] += 1

            def unit_loop(units):
                loops = units // UNITS
                if loops:
                    with pe.Fori(0, loops) as i:
                        for q in range(UNITS):
                            unit(features, 2, 2 * q, q, i)
                n[0] += BODY * loops
                u[0] += UNITS * loops
                for q in range(units % UNITS):
                    one_unit(features)

            def add_to_stream():
                ready = next_split()
                for j in range(8):
                    w = weights(0, 0)
                    features(bank[4 + j // 2][:, (j % 2) * T:(j % 2 + 1) * T], w, ready if j == 0 else None).then_inc(g["pieces_used"], 1)
                    n[0] += 1

            def clear_banks():
                any_finite = ident[:, :].bitcast(BF16)
                for j in range(4):
                    for half in range(2):
                        mm(bank[4 + j][:, half * T:(half + 1) * T], zeros[:, :], any_finite, start=(half == 0), stop=False,
                           skip_group_check=True)

            def accumulate(count, spread=None, final=True, peeled=0):
                def piece(at, i=0, final=False):
                    hi, lo = weights(at, i)
                    pe.wait_ge(g["ax_lo"], i * BODY + (ax[0] + at + 1))
                    s = (n[0] + at) % RING
                    for c in range(KC):
                        dst, cols = bank[4 + c // 2][:, (c % 2) * T:(c % 2 + 1) * T], slice(c * P, (c + 1) * P)
                        mm(dst, hi[:, cols], xh[:, s, :], start=False, stop=False, skip_group_check=True)
                        mm(dst, hi[:, cols], xl[:, s, :], start=False, stop=False, skip_group_check=True)
                        last = mm(dst, lo[:, cols], xh[:, s, :], start=False, stop=False, skip_group_check=True)
                        if final and c in (1, 3, 5):
                            last.then_inc(g["bank_done"], 1)
                    last.then_inc(g["pieces_used"], 1)

                for j in range(peeled):
                    piece(j)
                loops = (count - 1 - peeled) // BODY
                with pe.Fori(0, loops) as i:
                    for j in range(BODY):
                        piece(peeled + j, i)
                        if spread and j % 2:
                            spread(j // 2 + 1, i)
                if spread:
                    spread(count // 2 - 1)
                for j in range(peeled + BODY * loops, count):
                    piece(j, 0, final and j == count - 1)
                n[0] += count
                ax[0] += count

            pe.wait_ge(g["consts"], 1)
            norm(G_EV)
            one_unit(features, 1, ready=next_split())
            for _ in range(2):
                one_unit(features)
            pe.wait_ge(g["ev_tables_loaded"], 32)
            pe.wait_ge(g["units_out"], 1)
            for f in range(2):
                last = mm(bank[5][:, f * T:(f + 1) * T], w_gate2[0:RANK, f * P:(f + 1) * P], e_glr[0:RANK, :], start=True, stop=True)
            last.then_inc(g["ev_z_ready"], 1)

            def level(lv):
                if lv < 6:
                    pe.wait_ge(g["ev_qk_level"], 2 * (lv + 1))
                    qe, ke = e_qe[lv % 2], e_ke[lv % 2]
                else:
                    qe, ke = e_q, e_k
                if lv >= 2:
                    pe.wait_ge(g["ev_level_in"], 2 * (lv - 1))
                for f in range(2):
                    for b in range(TB):
                        for r in range(2):
                            rows = slice(64 * r, 64 * r + 64)
                            cols = slice(f * T + b * P, f * T + b * P + P)
                            last = mm(bank[4 + 2 * (lv % 2) + r][:, (f * TB + b) * P:(f * TB + b + 1) * P],
                                      ke[rows, cols], qe[rows, cols], start=True, stop=True)
                last.then_inc(g["ev_level"], 1)

            def last_chunk_taps(first, end):
                pe.wait_ge(g["conv_input"], 1)
                pe.wait_ge(g["taps_laid"], end)
                for w in range(first, end):
                    at = (CC - 1) * UW + w
                    last = mm(bank[3][:, T:2 * T], tap_diag[w], e_u[:, at:at + T], start=(w == 0), stop=(w == CONV_W - 1))
                if end == CONV_W:
                    last.then_inc(g["conv_mixed"], 1)

            for _ in range(2):
                one_unit(features)
            for lv in range(4):
                level(lv)
                one_unit(features)
            level(4)
            token_unit()
            last_chunk_taps(0, 8)
            level(5)
            token_unit()
            level(6)
            pe.wait_ge(g["ev_kdec"], 2)
            pe.wait_ge(g["units_out"], 11)
            for b in range(TB):
                for f in range(2):
                    last = nc.tensor.transpose(bank[0][:, (b * 2 + f) * P:(b * 2 + f + 1) * P],
                                               e_kd[:, f * T + b * P:f * T + b * P + P], ident[:, :])
            last.then_inc(g["ev_kdec_turned"], 1)
            pe.wait_ge(g["ev_kdt"], 1)
            for c, dst in ((0, bank[1][:, 0:256]), (2, bank[1][:, 256:512]), (1, bank[2][:, 0:256])):
                for h in range(GH):
                    rows = slice(64 * (c % 2), 64 * (c % 2) + 64)
                    last = mm(dst[64 * (h % 2):64 * (h % 2) + 64, (h // 2) * DV:(h // 2 + 1) * DV],
                              e_kdt[rows, (c // 2) * 256 + h * DK:(c // 2) * 256 + (h + 1) * DK],
                              e_v[rows, (c // 2) * 512 + h * DV:(c // 2) * 512 + (h + 1) * DV], start=True, stop=True)
            last.then_inc(g["ev_chunk_sums"], 1)
            last_chunk_taps(8, 22)
            pe.wait_ge(g["ev_level_in"], 14)
            pe.wait_ge(g["ev_states"], 1)
            st = e_state.rearrange("p (c f n) -> p c f n", c=3, f=2)
            atv = e_at.rearrange("p (r f b t) -> p r f b t", r=2, f=2, b=TB)
            for h in range(GH):
                f, r = h // 2, h % 2
                rows = slice(64 * r, 64 * r + 64)
                for b in range(TB):
                    dst = bank[6 + r][:, (f * TB + b) * P:(f * TB + b + 1) * P]
                    last = mm(dst, e_v[:, b * 512 + h * DV:b * 512 + (h + 1) * DV], atv[:, r, f, b, :], start=True, stop=False)
                    for c in (2 * b, 2 * b + 1):
                        if c:
                            last = mm(dst[:, (c % 2) * CHUNK:(c % 2 + 1) * CHUNK], st[rows, c - 1, f, :],
                                      e_qb[rows, f * T + c * CHUNK:f * T + (c + 1) * CHUNK], start=False, stop=(c % 2 == 1))
            last.then_inc(g["ev_o"], 1)
            last_chunk_taps(22, CONV_W)
            pe.wait_ge(g["ev_o_sq"], 1)
            for r in range(2):
                last = mm(bank[4 + r][:, :], ones[:, :], e_osq[:, r * 512:(r + 1) * 512], start=True, stop=True)
            last.then_inc(g["ev_o_sum"], 1)
            pe.wait_ge(g["conv_step"], (CC - 1) * CONV_W + 1)
            for c in range(CC):
                last = mm(bank[3][:, 0:T], ones[:, :], b3(e_conv, CC)[:, c, :], start=(c == 0), stop=(c == CC - 1))
            last.then_inc(g["ln_sum"], 1)
            pe.wait_ge(g["ln_sq"], 1)
            for c in range(CC):
                last = mm(bank[3][:, 0:T], ones[:, :], b3(e_sq2, CC)[:, c, :], start=(c == 0), stop=(c == CC - 1))
            last.then_inc(g["ln_var"], 1)
            pe.wait_ge(g["ev_o_log"], 2)
            keep_warm(40, 1)
            add_to_stream()

            def experts(layer):
                norm(1 + 2 * layer)
                one_unit(features, ready=next_split())
                unit_loop(7)
                pe.wait_ge(g["units_out"], u[0])
                pe.wait_ge(g["keys_loaded"], 16 * (layer + 1))
                for s in range(8):
                    if s >= 4:
                        pe.wait_ge(g["scores_out"], 8 * layer + s - 3)
                    for j in range(4):
                        k = (s % 4) * 4 + j
                        last = mm(bank[4 + s % 4][:, j * P:(j + 1) * P], qT[:, k * T + (s // 4) * P:k * T + (s // 4) * P + P],
                                  keysb[:, k * NK:(k + 1) * NK], start=True, stop=True)
                    last.then_inc(g["key_scored"], 1)
                unit_loop(28)
                pe.wait_ge(g["slots_ready"], TB * (layer + 1))
                pe.wait_ge(g["scores_out"], 8 * (layer + 1))
                for c in range(3):
                    for b in range(TB):
                        dst = (bank[4][:, 0:T], bank[4][:, T:2 * T], bank[5][:, 0:T])[c]
                        last = nc.tensor.transpose(dst[:, b * P:(b + 1) * P], slot3[:, (c * TB + b) * P:(c * TB + b + 1) * P],
                                                   ident[:, :])
                last.then_inc(g["slots_turned"], 1)
                unit_loop(4)
                groups = T // GROUP_T
                base = 2 * groups * layer

                def spread(m, banks, i=0):
                    count = base + m
                    pe.wait_ge(g["first_hot"], i * 3 + (count + 1))
                    pe.wait_ge(g["second_hot"], i * 3 + (count + 1))
                    if count >= 3:
                        pe.wait_ge(g["gated"], i * 3 + (count - 2))
                    second, parts = b3(hot2[count % 3], GROUP_T), [b3(x, GROUP_T) for x in hot1[count % 3]]
                    for j in range(GROUP_T):
                        for p in range(3):
                            last = mm(bank[banks + m % 3][:, j * HALF:(j + 1) * HALF], second[:, j, :], parts[p][:, j, :],
                                      start=(p == 0), stop=(p == 2))
                    last.then_inc(g["gates_spread"], 1)

                spread(0, 4)
                with pe.Fori(0, groups // 3) as i:
                    for q in range(3):
                        unit(features, 2, 2 * q, q, i)
                        spread(q + 1, 4, i)
                n[0] += 2 * (groups - 2)
                u[0] += groups - 2
                spread(groups - 1, 4)
                for _ in range(2):
                    one_unit(features)
                pe.wait_ge(g["units_out"], u[0])
                spread(groups, 0)
                pe.wait_ge(g["gated"], base + groups)
                clear_banks()
                accumulate(HALF, lambda m, i=0: spread(groups + m, 0, i), False)
                accumulate(HALF)

            def attention(p, filler):
                def score(h):
                    c = p["base"] + h
                    rows = slice(64 * (h % 2), 64 * (h % 2) + 64)
                    (q, qc), (k, kc) = p["q"](h), p["k"](h)
                    if h >= 3:
                        pe.wait_ge(g["at_masked"], c - 2)
                    dst = bank[3 + h % 3]
                    last = None
                    for lo, b, keys in ((0, 0, P), (P, 1, 2 * P)):
                        last = mm(dst[:, lo:lo + keys], q[rows, qc, b * P:(b + 1) * P], k[rows, kc, 0:keys],
                                  start=True, stop=bool(p["tag"]))
                        if not p["tag"]:
                            rb = slice(64 * (h % 2), 64 * (h % 2) + 48)
                            last = mm(dst[:, lo:lo + keys], o_left[rb, h * T + b * P:h * T + (b + 1) * P],
                                      o_right[rb, h * T:h * T + keys], start=False, stop=True)
                    last.then_inc(g["at_score"], 1)

                for h in range(3):
                    score(h)
                for h in range(p["heads"]):
                    c = p["base"] + h
                    PR, PT = p["p"][h % 2], p["pt"][h % 2]
                    filler(h)
                    pe.wait_ge(g["at_prob"], c + 1)
                    if h:
                        pe.wait_ge(g["at_pt"], c)
                    for j in range(3):
                        last = nc.tensor.transpose(bank[6][:, j * P:(j + 1) * P], PR[:, j * P:(j + 1) * P], ident[:, :])
                    last.then_inc(g["at_turned"], 1)
                    if h + 3 < p["heads"]:
                        score(h + 3)
                    pe.wait_ge(g["at_pt"], c + 1)
                    if h % 2 == 0 and h:
                        pe.wait_ge(g["at_y"], (p["base"] + h) // 2)
                    dst = bank[7][64 * (h % 2):64 * (h % 2) + 64, 0:T]
                    mm(dst, p["v"](0, h), PT[:, 0:T], start=True, stop=False)
                    mm(dst[:, P:T], p["v"](1, h), PT[:, T:3 * P], start=False, stop=True).then_inc(g["at_mixed"], 1)

            def head_sums(s, src, done, mean):
                if s >= 4:
                    pe.wait_ge(g[mean], s - 3)
                mm(bank[4 + s % 4][:, :], halves[:, :], src[:, s * 512:(s + 1) * 512], start=True, stop=True).then_inc(g[done], 1)

            experts(0)

            norm(G_OD)
            one_unit(features, ready=next_split())
            unit_loop(7)
            one_unit(features, 1)
            for j in range(4):
                token_unit()
                for s in (2 * j, 2 * j + 1):
                    pe.wait_ge(g["od_sq"], s + 1)
                    head_sums(s, o_sq, "od_sum", "od_log")
            pe.wait_ge(g["od_qk_ready"], 8)
            pe.wait_ge(g["od_bias_ready"], 1)
            pe.wait_ge(g["units_out"], u[0])
            attention(odd_att, lambda h: None)
            add_to_stream()

            experts(1)

            norm(G_MIX2)
            one_unit(features, ready=next_split())
            for s in range(2):
                one_unit(features)
            one_unit(tokens, 1)
            for s in range(2):
                token_unit()
            for s in range(2):
                one_unit(features)
            for s in range(3):
                pe.wait_ge(g["sb_sq"], s + 1)
                head_sums(s, s_sq, "sb_sum", "sb_log")
            for _ in range(3):
                one_unit(features)
            pe.wait_ge(g["sgu_v_ready"], 2)
            pe.wait_ge(g["sgu_w_ready"], 1)
            pe.wait_ge(g["sb_qk_ready"], 3)
            for gr in range(SG):
                for b in range(TB):
                    c = gr // 2
                    last = mm(bank[6 + c // 2][64 * (gr % 2):64 * (gr % 2) + 64, ((c % 2) * TB + b) * P:((c % 2) * TB + b + 1) * P],
                              s_vn[:, b * 512 + gr * SGD:b * 512 + (gr + 1) * SGD], s_ws[:, gr * P:(gr + 1) * P],
                              start=True, stop=True)
            last.then_inc(g["sgu_mixed"], 1)
            pe.wait_ge(g["sgu_y"], 1)
            attention(swa_att, lambda h: one_unit(features) if h < 5 else None)
            pe.wait_ge(g["units_out"], u[0])
            ready = next_split()
            for c in range(KC):
                if c >= 4:
                    pe.wait_ge(g["merged_out"], c - 3)
                hi, lo = weights(0, 0)
                for half in range(2):
                    for k in range(4 * half, 4 * half + 4):
                        if c == 0:
                            ready[0](k)
                            ready[1](k)
                        dst, rows = bank[c % 4][:, half * T:(half + 1) * T], slice(k * P, (k + 1) * P)
                        mm(dst, hi[:, rows], xh[:, k, :], start=(k % 4 == 0), stop=False)
                        mm(dst, hi[:, rows], xl[:, k, :], start=False, stop=False)
                        last = mm(dst, lo[:, rows], xh[:, k, :], start=False, stop=(k % 4 == 3))
                last.then_inc(g["pieces_used"], 1)
                n[0] += 1
            add_to_stream()

            norm(G_FFN2)
            one_unit(features, ready=next_split())
            unit_loop(FC - 1)
            pe.wait_ge(g["x_ready"], 20)
            pe.wait_ge(g["norm_log"], 6)
            clear_banks()
            keep_warm(16)
            accumulate(FC, peeled=RING)


def columns(w, order=None):
    w = np.asarray(w)
    n = w.shape[1] // P
    p = w.reshape(w.shape[0] // P, P, n, P).transpose(2, 1, 0, 3).reshape(n, P, -1)
    return p if order is None else p[order]


def half_columns(w):
    w = np.asarray(w)
    n = w.shape[1] // 256
    return w.reshape(2, 4, P, n, 256).transpose(3, 0, 2, 1, 4).reshape(2 * n, P, -1)


def chunked(v):
    return np.asarray(v).reshape(-1, P).T


def layout(i):
    o = {}
    o["x"] = np.asarray(i["x"])[0].T.reshape(KC, P, T).transpose(1, 0, 2).reshape(P, KC * T)
    o["gains"] = np.concatenate([chunked(v) for v in (i["ev_norm_mix"][0], i["ffn_norm"][0], i["od_norm_mix"][0],
                                                      i["ffn_norm"][1], i["mix_norm_2"][0], i["ffn_norm_2"][0])], 1)
    w = np.asarray(i["ev_w_in"])[0]
    val, gate, q, k, v, r = 0, 512, 1024, 1280, 1536, 2048
    rank = np.zeros((D, P), w.dtype)
    rank[:, :RANK] = w[:, 2560:]
    o["ev_in"] = np.concatenate([columns(rank), columns(w[:, q:v]), columns(w[:, val:q]), columns(w[:, r:r + 512]),
                                 half_columns(w[:, v:r])])
    o["w_gate2"] = np.asarray(i["ev_gate_w2"])[0]
    o["ev_small"] = np.concatenate(
        [np.asarray(i["ev_conv_w"])[0].reshape(CONV_W, CC, P).transpose(2, 0, 1).reshape(P, -1),
         chunked(i["ev_conv_b"][0]), chunked(i["ev_conv_ln_g"][0]), chunked(i["ev_conv_ln_b"][0]),
         chunked(i["ev_gate_b"][0]), chunked(i["ev_gla_norm_g"][0])], 1)
    o["ev_out"] = columns(i["ev_w_out"][0])
    for l in range(2):
        o[f"wq{l}"] = columns(i["peer_wq"][l])
        o[f"keys{l}"] = np.asarray(i["peer_keys"])[l].transpose(3, 0, 1, 2).reshape(P, 16 * NK)
        o[f"u{l}"] = np.asarray(i["peer_u"])[l].reshape(NK, NK, KC, P).transpose(0, 3, 2, 1).reshape(NK, P, D)
        o[f"v{l}"] = np.asarray(i["peer_v"])[l].reshape(NK, P, D)
    w = np.asarray(i["od_w_in"])[0]
    fz = np.zeros((D, P), w.dtype)
    fb = np.zeros((P, 1), w.dtype)
    for at in (0, 32, 64, 96):
        fz[:, at:at + FH] = w[:, 3 * D:]
        fb[at:at + FH, 0] = np.asarray(i["od_fgate_b"])[0]
    o["od_in"] = np.concatenate([columns(w[:, :2 * D]), columns(fz), half_columns(w[:, 2 * D:3 * D])])
    o["od_fb"] = fb
    o["od_out"] = columns(i["od_w_out"][0])
    o["qk_gain"] = np.stack([np.tile(np.asarray(v)[0], 2) for v in
                             (i["od_q_norm_g"], i["od_k_norm_g"], i["q_norm_2"], i["k_norm_2"])], 1)
    o["sinks"] = np.broadcast_to(np.asarray(i["sinks_2"])[0], (P, QH))
    w = np.asarray(i["w_in_2"])[0]
    kk = w[:, 512:640].reshape(D, 2, 1, HD)
    kk = np.broadcast_to(kk, (D, 2, 2, HD)).reshape(D, 256)
    o["sb_in"] = np.concatenate([columns(w[:, 0:512]), columns(kk), columns(w[:, 640:768]), half_columns(w[:, 1280:1792]),
                                 columns(w[:, 768:1280]), columns(w[:, 1792:])])
    o["sb_ab"] = columns(np.concatenate([np.asarray(i["w_oa_2"])[0], np.asarray(i["w_ob_2"])[0]]))
    o["sb_out"] = columns(i["w_out_2"][0])
    o["sb_ws"] = np.asarray(i["w_s_2"])[0].transpose(2, 0, 1).reshape(P, SG * P)
    o["sb_bs"] = np.repeat(np.asarray(i["b_s_2"])[0], SGD, 0).reshape(4, P, P).transpose(1, 0, 2).reshape(P, 4 * P)
    o["sb_norm"] = np.broadcast_to(np.asarray(i["sgu_norm_2"])[0], (P, 512))
    both = np.arange(2 * FC).reshape(2, FC).T.reshape(-1)
    o["up"] = columns(i["w_up_2"][0], both)
    o["ff_cw"] = np.asarray(i["conv_w_2"])[0].reshape(3, 2 * FC, P)[:, both].transpose(2, 1, 0).reshape(P, -1)
    o["ff_cb"] = np.asarray(i["conv_b_2"])[0].reshape(2 * FC, P)[both].T
    o["down"] = np.asarray(i["w_down_2"])[0].reshape(FC, P, D)
    return {k: np.ascontiguousarray(v) for k, v in o.items()}


def kernel(**inputs):
    import concourse.bacc as _bacc
    from concourse.bass_utils import run_bass_kernel_spmd as _run

    arrays = layout(inputs)
    nc = _bacc.Bacc("TRN2", target_bir_lowering=False, num_devices=1)
    dram = {name: nc.dram_tensor(name + "_dram", v.shape, mybir.dt.from_np(v.dtype), kind="ExternalInput").ap()
            for name, v in arrays.items()}
    out = nc.dram_tensor("out_dram", (P, KC * T), F32, kind="ExternalOutput").ap()
    build(nc, dram, out)
    r = _run(nc, [{name + "_dram": v for name, v in arrays.items()}], core_ids=[0])
    got = r.results[0]["out_dram"]
    return got.reshape(P, KC, T).transpose(2, 1, 0).reshape(1, T, D)
```
